# Optimizing a Trainium2 kernel written in Bass

```python
import math
import jax, jax.numpy as jnp
from jax import lax
import numpy as np

D_MODEL = 2048
BATCH = 1
SEQ = 128
DEPTH = 1
DEC_BATCH = 1
DEC_SEQ = 256
PAST_LEN = 128

GRID_W = 64
D_MIX = D_MODEL
SSD_WIDTH = D_MIX // 2
SSD_HEAD_DIM = 64
SSD_HEADS = SSD_WIDTH // SSD_HEAD_DIM
SSD_GROUPS = 2
SSD_STATE = 128
SSD_CONV_W = 5
SSD_CHUNK = 128
SSD_CONV_CH = SSD_WIDTH + 2 * SSD_GROUPS * SSD_STATE
RWKV_WIDTH = D_MIX - SSD_WIDTH
RWKV_HEAD_DIM = 64
RWKV_HEADS = RWKV_WIDTH // RWKV_HEAD_DIM
DECAY_LORA = 64
ICLR_LORA = 64
GATE_LORA = 160
N_SSD_IN = 2 * SSD_WIDTH + 2 * SSD_GROUPS * SSD_STATE + 2 * SSD_HEADS
N_RWKV_IN = 3 * RWKV_WIDTH + 2 * DECAY_LORA + ICLR_LORA + GATE_LORA
N_IN = N_SSD_IN + N_RWKV_IN
RWKV_SPLITS = [RWKV_WIDTH, 2 * RWKV_WIDTH, 3 * RWKV_WIDTH, 3 * RWKV_WIDTH + DECAY_LORA,
               3 * RWKV_WIDTH + 2 * DECAY_LORA, 3 * RWKV_WIDTH + 2 * DECAY_LORA + ICLR_LORA]
N_EXPERTS = 16
EC_CAPACITY = 2
EXPERT_FF = 1024
N_MOD = 6
NORM_EPS = 1e-6
GN_EPS = 64e-5
DECAY_SCALE = 0.606531
POS_BASE = 10000.0

kernel_name = "hybrid_ssd_rwkv7_ec_diffusion_step"

def rms_norm(x, g):
    x32 = x.astype(jnp.float32)
    y = x32 * lax.rsqrt(jnp.mean(x32 * x32, axis=-1, keepdims=True) + NORM_EPS)
    return (y * g.astype(jnp.float32)).astype(x.dtype)

def adaln_modulation(cond, w, b):
    return (jax.nn.silu(cond) @ w + b).reshape(cond.shape[0], N_MOD, D_MODEL)

def grid_pos_embed(n_tokens, dim):
    rows = n_tokens // GRID_W
    row = jnp.repeat(jnp.arange(rows, dtype=jnp.float32), GRID_W)
    col = jnp.tile(jnp.arange(GRID_W, dtype=jnp.float32), rows)
    quarter = dim // 4
    freqs = jnp.exp(jnp.arange(quarter, dtype=jnp.float32) * (-math.log(POS_BASE) / quarter))

    def axis_embed(pos):
        ang = pos[:, None] * freqs[None, :]
        return jnp.concatenate([jnp.sin(ang), jnp.cos(ang)], axis=-1)

    return jnp.concatenate([axis_embed(row), axis_embed(col)], axis=-1)

def centred_depthwise_conv(u, w, b):
    pad = w.shape[0] // 2
    out = lax.conv_general_dilated(u, w[:, None, :].astype(u.dtype), window_strides=(1,),
                                   padding=[(pad, pad)], dimension_numbers=("NWC", "WIO", "NWC"),
                                   feature_group_count=u.shape[-1])
    return out + b

def centred_shift(u):
    up = jnp.pad(u, ((0, 0), (1, 1), (0, 0)))
    return 0.5 * (up[:, :-2] + up[:, 2:])

def ssd_chunked_scan(x, dt, A, Bm, Cm, h0):
    bsz, seq, nh, hp = x.shape
    nc = seq // SSD_CHUNK
    chunk = lambda t: t.reshape((bsz, nc, SSD_CHUNK) + t.shape[2:])
    x, dt, Bm, Cm = chunk(x), chunk(dt), chunk(Bm), chunk(Cm)
    a_cum = jnp.cumsum(dt * A, axis=2)
    pos = jnp.arange(SSD_CHUNK)
    lower = (pos[:, None] >= pos[None, :])[None, None, :, :, None]
    seg = a_cum[:, :, :, None, :] - a_cum[:, :, None, :, :]
    decay_in = jnp.exp(jnp.where(lower, seg, -jnp.inf))
    xdt = x * dt[..., None]
    scores = jnp.einsum("bcihn,bcjhn->bcijh", Cm, Bm) * decay_in
    y_diag = jnp.einsum("bcijh,bcjhp->bcihp", scores, xdt)
    decay_to_end = jnp.exp(a_cum[:, :, -1:, :] - a_cum)
    chunk_states = jnp.einsum("bcjhn,bcjhp->bchpn", Bm * decay_to_end[..., None], xdt)
    chunk_decay = jnp.exp(a_cum[:, :, -1, :])

    def step(h, inp):
        s_c, d_c = inp
        return h * d_c[:, :, None, None] + s_c, h

    h_final, h_in = lax.scan(step, h0, (jnp.moveaxis(chunk_states, 1, 0), jnp.moveaxis(chunk_decay, 1, 0)))
    h_in = jnp.moveaxis(h_in, 0, 1)
    y_off = jnp.einsum("bcihn,bchpn->bcihp", Cm * jnp.exp(a_cum)[..., None], h_in)
    return (y_diag + y_off).reshape(bsz, seq, nh, hp), h_final

def ssd_mixer(u, p, h0_f, h0_b):
    bsz, seq, _ = u.shape
    f32 = jnp.float32
    z, xbc, dt_raw = jnp.split(u, [SSD_WIDTH, SSD_WIDTH + SSD_CONV_CH], axis=-1)
    xbc = jax.nn.silu(centred_depthwise_conv(xbc, p["ssd_conv_w"], p["ssd_conv_b"])).astype(f32)
    xh, Bm, Cm = jnp.split(xbc, [SSD_WIDTH, SSD_WIDTH + SSD_GROUPS * SSD_STATE], axis=-1)
    xh = xh.reshape(bsz, seq, SSD_HEADS, SSD_HEAD_DIM)
    rep = SSD_HEADS // SSD_GROUPS
    Bm = jnp.repeat(Bm.reshape(bsz, seq, SSD_GROUPS, SSD_STATE), rep, axis=2)
    Cm = jnp.repeat(Cm.reshape(bsz, seq, SSD_GROUPS, SSD_STATE), rep, axis=2)
    dt = jax.nn.softplus(dt_raw.astype(f32).reshape(bsz, seq, 2, SSD_HEADS) + p["ssd_dt_bias"].astype(f32))
    A = -jnp.exp(p["ssd_A_log"].astype(f32))
    rev = lambda t: t[:, ::-1]
    y_f, h_f = ssd_chunked_scan(xh, dt[:, :, 0], A[0], Bm, Cm, h0_f.astype(f32))
    y_b, h_b = ssd_chunked_scan(rev(xh), rev(dt[:, :, 1]), A[1], rev(Bm), rev(Cm), h0_b.astype(f32))
    y = y_f + rev(y_b) + p["ssd_D"].astype(f32)[:, None] * xh
    y = y.reshape(bsz, seq, SSD_WIDTH) * jax.nn.silu(z.astype(f32))
    y = y.reshape(bsz, seq, SSD_GROUPS, SSD_WIDTH // SSD_GROUPS)
    y = y * lax.rsqrt(jnp.mean(y * y, axis=-1, keepdims=True) + NORM_EPS)
    y = y.reshape(bsz, seq, SSD_WIDTH) * p["ssd_norm_g"].astype(f32)
    return y, h_f, h_b

def rwkv7_scan(r, w, k, v, kk, a, s0):
    def step(S, inp):
        r_t, w_t, k_t, v_t, kk_t, a_t = inp
        sa = jnp.einsum("bhvk,bhk->bhv", S, -kk_t)
        S = S * w_t[:, :, None, :] + sa[..., None] * (kk_t * a_t)[:, :, None, :] + v_t[..., None] * k_t[:, :, None, :]
        return S, jnp.einsum("bhvk,bhk->bhv", S, r_t)

    xs = tuple(jnp.moveaxis(t, 1, 0) for t in (r, w, k, v, kk, a))
    s_final, ys = lax.scan(step, s0, xs)
    return jnp.moveaxis(ys, 0, 1), s_final

def rwkv7_mixer(u, p, s0_f, s0_b):
    bsz, seq, _ = u.shape
    f32 = jnp.float32
    u = u.astype(f32)
    u = u + p["rwkv_mu"] * (centred_shift(u) - u)
    r, k, v, wd_f, wd_b, ad, gd = jnp.split(u, RWKV_SPLITS, axis=-1)
    w0 = p["rwkv_w0"].astype(f32)
    w_up = p["rwkv_w_up"].astype(f32)
    decay_f = jnp.exp(-DECAY_SCALE * jax.nn.sigmoid(w0[0] + jnp.tanh(wd_f) @ w_up[0]))
    decay_b = jnp.exp(-DECAY_SCALE * jax.nn.sigmoid(w0[1] + jnp.tanh(wd_b) @ w_up[1]))
    a = jax.nn.sigmoid(p["rwkv_a0"] + ad @ p["rwkv_a_up"])
    g = jax.nn.sigmoid(gd) @ p["rwkv_g_up"]
    heads = lambda t: t.reshape(bsz, seq, RWKV_HEADS, RWKV_HEAD_DIM)
    kk = heads(k * p["rwkv_k_k"])
    kk = kk / jnp.maximum(jnp.sqrt(jnp.sum(kk * kk, axis=-1, keepdims=True)), 1e-12)
    k = heads(k * (1.0 + (a - 1.0) * p["rwkv_k_a"]))
    r, v, a = heads(r), heads(v), heads(a)
    rev = lambda t: t[:, ::-1]
    y_f, s_f = rwkv7_scan(r, heads(decay_f), k, v, kk, a, s0_f.astype(f32))
    y_b, s_b = rwkv7_scan(rev(r), rev(heads(decay_b)), rev(k), rev(v), rev(kk), rev(a), s0_b.astype(f32))
    y = y_f + rev(y_b)
    mean = jnp.mean(y, axis=-1, keepdims=True)
    var = jnp.mean(jnp.square(y - mean), axis=-1, keepdims=True)
    y = ((y - mean) * lax.rsqrt(var + GN_EPS)).reshape(bsz, seq, RWKV_WIDTH) * p["rwkv_ln_g"] + p["rwkv_ln_b"]
    bonus = jnp.sum(r * k * p["rwkv_r_k"].astype(f32), axis=-1, keepdims=True) * v
    y = (y + bonus.reshape(bsz, seq, RWKV_WIDTH)) * g
    return y, s_f, s_b

def expert_choice_ffn(h, p):
    bsz, seq, dm = h.shape
    t = h.reshape(bsz * seq, dm)
    n_tok = t.shape[0]
    cap = EC_CAPACITY * n_tok // N_EXPERTS
    aff = jax.nn.softmax((t @ p["router_w"]).astype(jnp.float32), axis=-1)
    gate, idx = lax.top_k(aff.T, cap)
    xs = t[idx]
    hid = jax.nn.silu(jnp.einsum("ecd,edf->ecf", xs, p["exp_w_gate"])) * jnp.einsum("ecd,edf->ecf", xs, p["exp_w_up"])
    out = jnp.einsum("ecf,efd->ecd", hid, p["exp_w_down"]) * gate[..., None].astype(t.dtype)
    y = jnp.zeros_like(t).at[idx.reshape(-1)].add(out.reshape(-1, dm).astype(t.dtype))
    return y.reshape(bsz, seq, dm)

def trunk_layer(x, mod, p, states):
    shift_m, scale_m, gate_m, shift_f, scale_f, gate_f = [mod[:, i, None, :] for i in range(N_MOD)]
    h = rms_norm(x, p["norm_mix_g"]) * (1 + scale_m) + shift_m
    proj = h @ p["w_in"]
    y_ssd, h_f, h_b = ssd_mixer(proj[..., :N_SSD_IN], p, states[0], states[1])
    y_rwkv, s_f, s_b = rwkv7_mixer(proj[..., N_SSD_IN:], p, states[2], states[3])
    mixed = jnp.concatenate([y_ssd, y_rwkv], axis=-1).astype(x.dtype) @ p["w_out"]
    x = x + gate_m * mixed
    h = rms_norm(x, p["norm_ffn_g"]) * (1 + scale_f) + shift_f
    x = x + gate_f * expert_choice_ffn(h, p)
    return x, (h_f, h_b, s_f, s_b)

def setup_inputs(seed: int = 0) -> dict:
    key = jax.random.key(seed)
    ks = iter(jax.random.split(key, 64))

    def nrm(shape, scale):
        return scale * jax.random.normal(next(ks), shape, jnp.float32)

    def near(shape, centre):
        return centre + nrm(shape, 0.05)

    L = DEPTH
    dt0 = jnp.exp(jax.random.uniform(next(ks), (L, 2, SSD_HEADS), jnp.float32, math.log(1e-3), math.log(1e-1)))
    return {
        "x_prompt": nrm((BATCH, SEQ, D_MODEL), 1.0),
        "x_sample": nrm((DEC_BATCH, DEC_SEQ, D_MODEL), 1.0),
        "state_ssd_fwd": nrm((DEC_BATCH, L, SSD_HEADS, SSD_HEAD_DIM, SSD_STATE), 0.5),
        "state_ssd_bwd": nrm((DEC_BATCH, L, SSD_HEADS, SSD_HEAD_DIM, SSD_STATE), 0.5),
        "state_rwkv_fwd": nrm((DEC_BATCH, L, RWKV_HEADS, RWKV_HEAD_DIM, RWKV_HEAD_DIM), 0.5),
        "state_rwkv_bwd": nrm((DEC_BATCH, L, RWKV_HEADS, RWKV_HEAD_DIM, RWKV_HEAD_DIM), 0.5),
        "c": nrm((DEC_BATCH, D_MODEL), 1.0),
        "c_ctx": nrm((D_MODEL,), 1.0),
        "w_ada": nrm((L, D_MODEL, N_MOD * D_MODEL), 0.5 * D_MODEL ** -0.5),
        "b_ada": nrm((L, N_MOD * D_MODEL), 0.02),
        "norm_mix_g": near((L, D_MODEL), 1.0),
        "norm_ffn_g": near((L, D_MODEL), 1.0),
        "w_in": nrm((L, D_MODEL, N_IN), D_MODEL ** -0.5),
        "w_out": nrm((L, D_MIX, D_MODEL), D_MIX ** -0.5),
        "ssd_conv_w": nrm((L, SSD_CONV_W, SSD_CONV_CH), SSD_CONV_W ** -0.5),
        "ssd_conv_b": nrm((L, SSD_CONV_CH), 0.02),
        "ssd_A_log": jnp.log(jax.random.uniform(next(ks), (L, 2, SSD_HEADS), jnp.float32, 1.0, 16.0)),
        "ssd_dt_bias": dt0 + jnp.log(-jnp.expm1(-dt0)),
        "ssd_D": near((L, SSD_HEADS), 1.0),
        "ssd_norm_g": near((L, SSD_WIDTH), 1.0),
        "rwkv_mu": jax.random.uniform(next(ks), (L, N_RWKV_IN), jnp.float32, 0.0, 1.0),
        "rwkv_w0": nrm((L, 2, RWKV_WIDTH), 1.0),
        "rwkv_w_up": nrm((L, 2, DECAY_LORA, RWKV_WIDTH), 0.5 * DECAY_LORA ** -0.5),
        "rwkv_a0": nrm((L, RWKV_WIDTH), 0.5),
        "rwkv_a_up": nrm((L, ICLR_LORA, RWKV_WIDTH), 0.5 * ICLR_LORA ** -0.5),
        "rwkv_g_up": nrm((L, GATE_LORA, RWKV_WIDTH), GATE_LORA ** -0.5),
        "rwkv_k_k": near((L, RWKV_WIDTH), 0.85),
        "rwkv_k_a": near((L, RWKV_WIDTH), 1.0),
        "rwkv_r_k": nrm((L, RWKV_HEADS, RWKV_HEAD_DIM), 0.1),
        "rwkv_ln_g": near((L, RWKV_WIDTH), 1.0),
        "rwkv_ln_b": nrm((L, RWKV_WIDTH), 0.02),
        "router_w": nrm((L, D_MODEL, N_EXPERTS), D_MODEL ** -0.5),
        "exp_w_gate": nrm((L, N_EXPERTS, D_MODEL, EXPERT_FF), D_MODEL ** -0.5),
        "exp_w_up": nrm((L, N_EXPERTS, D_MODEL, EXPERT_FF), D_MODEL ** -0.5),
        "exp_w_down": nrm((L, N_EXPERTS, EXPERT_FF, D_MODEL), EXPERT_FF ** -0.5),
        "final_norm_g": near((D_MODEL,), 1.0),
    }

def reference(x_prompt, x_sample, state_ssd_fwd, state_ssd_bwd, state_rwkv_fwd, state_rwkv_bwd, c, c_ctx,
              w_ada, b_ada, norm_mix_g, norm_ffn_g, w_in, w_out, ssd_conv_w, ssd_conv_b, ssd_A_log,
              ssd_dt_bias, ssd_D, ssd_norm_g, rwkv_mu, rwkv_w0, rwkv_w_up, rwkv_a0, rwkv_a_up, rwkv_g_up,
              rwkv_k_k, rwkv_k_a, rwkv_r_k, rwkv_ln_g, rwkv_ln_b, router_w, exp_w_gate, exp_w_up,
              exp_w_down, final_norm_g):
    layers = [dict(norm_mix_g=norm_mix_g[l], norm_ffn_g=norm_ffn_g[l], w_in=w_in[l], w_out=w_out[l],
                   ssd_conv_w=ssd_conv_w[l], ssd_conv_b=ssd_conv_b[l], ssd_A_log=ssd_A_log[l],
                   ssd_dt_bias=ssd_dt_bias[l], ssd_D=ssd_D[l], ssd_norm_g=ssd_norm_g[l],
                   rwkv_mu=rwkv_mu[l], rwkv_w0=rwkv_w0[l], rwkv_w_up=rwkv_w_up[l], rwkv_a0=rwkv_a0[l],
                   rwkv_a_up=rwkv_a_up[l], rwkv_g_up=rwkv_g_up[l], rwkv_k_k=rwkv_k_k[l], rwkv_k_a=rwkv_k_a[l],
                   rwkv_r_k=rwkv_r_k[l], rwkv_ln_g=rwkv_ln_g[l], rwkv_ln_b=rwkv_ln_b[l], router_w=router_w[l],
                   exp_w_gate=exp_w_gate[l], exp_w_up=exp_w_up[l], exp_w_down=exp_w_down[l])
              for l in range(DEPTH)]

    bp = x_prompt.shape[0]
    zero_states = (jnp.zeros((bp, SSD_HEADS, SSD_HEAD_DIM, SSD_STATE), jnp.float32),
                   jnp.zeros((bp, SSD_HEADS, SSD_HEAD_DIM, SSD_STATE), jnp.float32),
                   jnp.zeros((bp, RWKV_HEADS, RWKV_HEAD_DIM, RWKV_HEAD_DIM), jnp.float32),
                   jnp.zeros((bp, RWKV_HEADS, RWKV_HEAD_DIM, RWKV_HEAD_DIM), jnp.float32))
    xp = x_prompt
    ctx_states = []
    for l in range(DEPTH):
        mod_ctx = adaln_modulation(c_ctx[None, :], w_ada[l], b_ada[l])
        xp, st = trunk_layer(xp, mod_ctx, layers[l], zero_states)
        ctx_states.append(st)
    y_prompt = rms_norm(xp, final_norm_g)
    new_ssd_fwd = jnp.stack([s[0] for s in ctx_states], axis=1).astype(x_prompt.dtype)
    new_ssd_bwd = jnp.stack([s[1] for s in ctx_states], axis=1).astype(x_prompt.dtype)
    new_rwkv_fwd = jnp.stack([s[2] for s in ctx_states], axis=1).astype(x_prompt.dtype)
    new_rwkv_bwd = jnp.stack([s[3] for s in ctx_states], axis=1).astype(x_prompt.dtype)

    xs = x_sample + grid_pos_embed(x_sample.shape[1], D_MODEL).astype(x_sample.dtype)[None]
    for l in range(DEPTH):
        mod_lat = adaln_modulation(c, w_ada[l], b_ada[l])
        cached = (state_ssd_fwd[:, l], state_ssd_bwd[:, l], state_rwkv_fwd[:, l], state_rwkv_bwd[:, l])
        xs, _ = trunk_layer(xs, mod_lat, layers[l], cached)
    y_sample = rms_norm(xs, final_norm_g)

    return (y_prompt, y_sample, new_ssd_fwd, new_ssd_bwd, new_rwkv_fwd, new_rwkv_bwd)


_drawn_inputs = setup_inputs


def setup_inputs(seed=0):
    import zlib

    import numpy as np

    out = dict(_drawn_inputs(seed))
    spreads = {}
    factors = {'state_rwkv_fwd': 8.0,
     'state_rwkv_bwd': 8.0,
     'norm_ffn_g': 5.55,
     'ssd_D': 8.0,
     'ssd_norm_g': 4.904,
     'rwkv_ln_g': 8.0,
     'rwkv_ln_b': 8.0}
    for name, (base, spread) in spreads.items():
        noise = np.random.default_rng([zlib.crc32(name.encode()), seed]).standard_normal(out[name].shape)
        drawn = base * np.exp(spread * noise) if base else spread * noise
        out[name] = __import__('jax').numpy.asarray(drawn.astype(out[name].dtype))
    for name, factor in factors.items():
        out[name] = (out[name] * factor).astype(out[name].dtype)
    return out
```

```python
import math
from contextlib import ExitStack

import numpy as np

import concourse.bass as bass
from concourse import mybir

F32 = mybir.dt.float32
F32R = mybir.dt.float32r
ALU = mybir.AluOpType
ACT = mybir.ActivationFunctionType
AX = mybir.AxisListType

P = 128
D = 2048
KC = D // P
LC, LS = 128, 256
T = LC + LS
TILES = T // P
GRID_W = 64
HEADS = 16
HD = 64
PAIRS = HEADS // 2
N_SSD_IN = 2592
N_EXP = 16
FF = 1024
CAPC, CAPS = 2 * LC // N_EXP, 2 * LS // N_EXP
SLOTS = CAPC + CAPS
EPS, GN_EPS = 1e-6, 64e-5
DECAY = 0.606531
Q = 64
NCH = T // Q

COND, CCTX = 96, 112
G_MIX, G_FFN, G_FIN, CONV_W, CONV_B, G_SSD = 128, 144, 160, 176, 236, 248
W0, A0, K_K, K_A, R_K, LN_G, LN_B, MU = 256, 272, 280, 288, 296, 304, 312, 320
NPAR = 348
MU_WD, MU_GD0, MU_AD, MU_GD1 = 24, 25, 26, 27

CONST = {}


def constants():
    r = np.arange(P)
    pieces = {
        "ident": np.eye(P),
        "ones": np.ones((P, P)),
        "blk": (r[:, None] // HD == r[None, :] // HD),
        "i2": np.concatenate([np.eye(HD)] * 2),
        "neg0": np.where(r[None, :] >= r[:, None], 0.0, -1e30),
        "neg1": np.where(r[None, :] <= r[:, None], 0.0, -1e30),
        "iota": np.tile(np.arange(CAPS), (P, 1)),
    }
    u, s = (r % Q)[:, None], np.arange(Q)[None, :]
    one = np.ones((P, Q))
    for d in range(2):
        before = (s < u) if d == 0 else (s > u)
        after = (s > u) if d == 0 else (s < u)
        upto = after | (s == u)
        pieces[f"e1_{d}"] = np.concatenate([one, before, before], 1)
        pieces[f"e2_{d}"] = np.concatenate([upto, one, after], 1)
        top = (r < Q)[:, None]
        pieces[f"x_{d}"] = np.concatenate([top | upto, one], 1)
    for n in range(6):
        b = 1 << n
        low = (u // (2 * b) == s // (2 * b)) & ((u // b) % 2 == 1) & ((s // b) % 2 == 0)
        high = (u // (2 * b) == s // (2 * b)) & ((u // b) % 2 == 0) & ((s // b) % 2 == 1)
        pieces[f"low{n}"] = low
        pieces[f"high{n}"] = high
    pieces["fold"] = np.zeros((P, 2))
    pieces["fold"][0:4] = [[1, 0], [0, 1], [1, 0], [0, 1]]
    f = np.float32
    quarter = D // 4
    freqs = np.exp(np.arange(quarter, dtype=f) * f(-math.log(10000.0) / quarter)).astype(f)
    for name, n in (("row", LS // GRID_W), ("col", GRID_W)):
        ang = (np.arange(n, dtype=f)[:, None] * freqs[None, :]).astype(f)
        table = np.concatenate([np.sin(ang), np.cos(ang)], -1).astype(f)
        pieces[name] = table.T.reshape(KC // 2, P, n).transpose(1, 0, 2).reshape(P, -1)
    at = 0
    for name, a in pieces.items():
        CONST[name] = (at, at + a.shape[1])
        at += a.shape[1]
    return np.ascontiguousarray(np.concatenate([np.asarray(a, f) for a in pieces.values()], 1))


def ahead(eng, S, *names):
    for name in names:
        eng.sem_inc(S(name), 1)


class Link:

    def __init__(self, eng, sem, base=0):
        self.eng, self.sem, self.base, self.n = eng, sem, base, 0

    def __call__(self, ins):
        ins.then_inc(self.sem, 1)
        self.n += 1
        self.eng.wait_ge(self.sem, self.base + self.n)


def program(nc, I, O, table, stop="all"):
    ctx = ExitStack()
    sem = {}

    def S(name):
        if name not in sem:
            sem[name] = nc.alloc_semaphore(name)
        return sem[name]

    def reuse_semaphores():
        nc.clear_and_free_semaphores(list(sem.values()))
        sem.clear()
        nc.all_engine_barrier()

    def sb(stack, name, shape, dt=F32):
        return stack.enter_context(nc.sbuf_tensor(name, shape, dt))

    with ctx:
        ps = [ctx.enter_context(nc.psum_tensor(f"bank{n}", [P, 512], F32)) for n in range(8)]
        cst = sb(ctx, "cst", [P, CONST["row"][0]])
        par = sb(ctx, "par", [P, 352])
        modT = sb(ctx, "modT", [P, 96, 2])
        gain = sb(ctx, "gain", [P, 2, KC, 2])
        xT = sb(ctx, "xT", [P, KC, T])

        def C(name, p0=0, p1=P):
            a, b = CONST[name]
            return cst[p0:p1, a:b]

        env = dict(nc=nc, I=I, O=O, table=table, S=S, sb=sb, ps=ps, cst=cst, par=par, modT=modT, gain=gain, xT=xT, C=C)
        setup(**env)
        if stop == "ada":
            return
        with ExitStack() as mix:
            mixed = sb(mix, "mixed", [P, KC, T])
            with ExitStack() as proj:
                hT = sb(proj, "hT", [P, KC, T])
                lora = sb(proj, "lora", [P, 4, T])
                norm(**env, which=0, out=hT)
                ssd(**env, hT=hT, mixed=mixed, lora=lora)
                if stop == "ssd":
                    return
                reuse_semaphores()
                rwkv(**env, hT=hT, mixed=mixed, lora=lora)
            reuse_semaphores()
            if stop == "rwkv":
                return
            project_out(**env, mixed=mixed)
        if stop == "mix":
            return
        with ExitStack() as ffn:
            picked = sb(ffn, "picked", [P, KC, N_EXP * SLOTS])
            rank = sb(ffn, "rank", [P, TILES, N_EXP])
            aff = sb(ffn, "aff", [P, TILES, N_EXP])
            gates = sb(ffn, "gates", [2 * SLOTS, D])
            route(**env, picked=picked, rank=rank, aff=aff, gates=gates)
            reuse_semaphores()
            experts(**env, picked=picked, rank=rank, aff=aff, gates=gates)
        finish(**env)


def setup(nc, I, O, table, S, sb, ps, cst, par, modT, gain, xT, C):
    RING, HL = 8, 4
    with ExitStack() as st:
        grid = sb(st, "grid", [P, table.shape[1] - CONST["row"][0]])
        rows = sb(st, "rows", [P, 3, P])
        xtok = sb(st, "xtok", [P, TILES, D])
        cs = sb(st, "cs", [P, 2, 2, KC])
        cond = sb(st, "cond", [P, KC, 4], F32R)
        raw = sb(st, "raw", [P, RING, 4, 512])
        hi = sb(st, "hi", [P, HL, 4, 512], F32R)
        lo = sb(st, "lo", [P, HL, 4, 512], F32R)
        arow = sb(st, "arow", [4, 2, 512])
        loaded = [S(f"ada_loaded{n}") for n in range(RING)]
        w_ada = I["w_ada"].rearrange("l (q c p) n -> p (l q) c n", p=P, c=4)
        block = st.enter_context(nc.Block())

        @block.sync
        def _(sp):
            def rows_in(t, r0, src):
                n, m = src.shape
                sp.dma_start(rows[r0:r0 + n, t, 0:m], src).then_inc(S("rows_in"), 16)

            at = CONST["row"][0]
            sp.dma_start(cst[:], table[:, 0:at]).then_inc(S("cst_in"), 16)
            sp.dma_start(grid[:], table[:, at:]).then_inc(S("grid_in"), 16)
            rows_in(0, 0, I["b_ada"].rearrange("l (r c) -> (l r) c", c=P))
            rows_in(0, COND, I["c"].rearrange("l (r c) -> (l r) c", c=P))
            rows_in(0, CCTX, I["c_ctx"].rearrange("(r c) -> r c", c=P))
            for at, name in ((G_MIX, "norm_mix_g"), (G_FFN, "norm_ffn_g"), (CONV_B, "ssd_conv_b"), (G_SSD, "ssd_norm_g")):
                rows_in(1, at - 128, I[name].rearrange("l (r c) -> (l r) c", c=P))
            rows_in(1, G_FIN - 128, I["final_norm_g"].rearrange("(r c) -> r c", c=P))
            rows_in(1, CONV_W - 128, I["ssd_conv_w"].rearrange("l t (r c) -> (l t r) c", c=P))
            rows_in(2, W0 - 256, I["rwkv_w0"].rearrange("l d (r c) -> (l d r) c", c=P))
            for at, name in ((A0, "rwkv_a0"), (K_K, "rwkv_k_k"), (K_A, "rwkv_k_a"), (LN_G, "rwkv_ln_g"), (LN_B, "rwkv_ln_b")):
                rows_in(2, at - 256, I[name].rearrange("l (r c) -> (l r) c", c=P))
            rows_in(2, R_K - 256, I["rwkv_r_k"].rearrange("l (r h) c -> (l r) (h c)", h=2))
            mu = I["rwkv_mu"]
            sp.wait_ge(S("rows_zero"), 1)
            rows_in(2, MU - 256, mu[:, 0:25 * P].rearrange("l (r c) -> (l r) c", c=P))
            rows_in(2, MU - 256 + MU_GD0, mu[:, 3264:3392])
            rows_in(2, MU - 256 + MU_AD, mu[:, 3200:3264])
            rows_in(2, MU - 256 + MU_GD1, mu[:, 3392:3424])
            sp.dma_start(xtok[:, 0, :], I["x_prompt"][0]).then_inc(S("x_in"), 16)
            for t in range(2):
                sp.dma_start(xtok[:, 1 + t, :], I["x_sample"][0, t * P:(t + 1) * P, :]).then_inc(S("x_in"), 16)

            def load(i, n):
                sp.dma_start(raw[:, n], w_ada[:, n % 4, :, bass.ds(i * 1024 + (n // 4) * 512, 512)]).then_inc(loaded[n], 16)

            for n in range(RING):
                load(0, n)
            with sp.Fori(1, 12) as i:
                for n in range(RING):
                    sp.wait_ge(S("ada_lo"), i * RING + n - RING + 1)
                    load(i, n)

        NROWS = 20

        @block.gpsimd
        def _(pool):
            pool.sem_inc(S("ada_used"), HL)
            nc.gpsimd.memset(rows[64:96, 2, :], 0.0).then_inc(S("rows_zero"), 1)

        @block.tensor
        def _(pe):
            pe.wait_ge(S("cst_in"), 16)
            pe.wait_ge(S("rows_in"), 16 * NROWS)
            for t, n in ((0, 128), (1, 128), (2, 92)):
                mm = pe.transpose(ps[0][:, t * P:t * P + n], rows[0:n, t, :], C("ident", 0, n)[:, 0:n])
            mm.then_inc(S("par_T"), 1)
            pe.wait_ge(S("x_in"), 16 * TILES)
            for t in range(TILES):
                for q in range(4):
                    g = 4 * t + q
                    if g >= 2:
                        pe.wait_ge(S("xT_out"), g - 1)
                    for k in range(4):
                        mm = pe.transpose(ps[1 + g % 2][:, k * P:(k + 1) * P], xtok[:, t, (4 * q + k) * P:(4 * q + k + 1) * P], C("ident"))
                    mm.then_inc(S("xT_in"), 1)
            pe.wait_ge(S("cond"), 1)
            def columns(i, g):
                pe.wait_ge(S("ada_row"), 2 * i + g + 1)
                for j in range(4):
                    mm = pe.matmul(ps[5][:, bass.ds(i * 16 + (4 * g + j) * 2, 2)], arow[:, g, j * P:(j + 1) * P], C("fold", 0, 4), start=True, stop=True)
                mm.then_inc(S("ada_col"), 1)

            def body(i, prev):
                for n in range(RING):
                    g, q = n // 4, n % 4
                    pe.wait_ge(S("ada_lo"), i * RING + n + 1)
                    for c in range(4):
                        for half in (hi, lo):
                            mm = pe.matmul(ps[3 + g][0:4, :], cond[:, 4 * q + c, :], half[:, n % HL, c, :],
                                           start=(q == 0 and c == 0 and half is hi), stop=(q == 3 and c == 3 and half is lo))
                    mm.then_inc(S("ada_used"), 1)
                    if n == 2 and prev:
                        columns(i - 1, 1)
                    if n == 6:
                        columns(i, 0)

            body(0, False)
            with pe.Fori(1, 12) as i:
                body(i, True)
            columns(11, 1)

        @block.scalar
        def _(act):
            act.wait_ge(S("par_done"), 1)
            nc.scalar.activation(cs[:, 1], par[:, COND:COND + 32].rearrange("p (a k) -> p a k", a=2), ACT.Sigmoid).then_inc(S("cond_sig"), 1)
            def row_out(i, g):
                act.wait_ge(S("ada_used"), i * RING + 4 * g + 4 + HL)
                nc.scalar.copy(arow[:, g], ps[3 + g][0:4, :]).then_inc(S("ada_row"), 1)

            def body(i, prev):
                for n in range(RING):
                    act.wait_ge(loaded[n], (i + 1) * 16)
                    act.wait_ge(S("ada_used"), i * RING + n + 1)
                    nc.scalar.copy(hi[:, n % HL], raw[:, n]).then_inc(S("ada_hi"), 1)
                    if n == 1 and prev:
                        row_out(i - 1, 1)
                    if n == 5:
                        row_out(i, 0)

            body(0, False)
            with act.Fori(1, 12) as i:
                body(i, True)
            row_out(11, 1)

        @block.vector
        def _(dve):
            link = Link(dve, S("setup_dve"))
            dve.wait_ge(S("par_T"), 1)
            nc.vector.tensor_copy(par[:, 0:NPAR], ps[0][:, 0:NPAR]).then_inc(S("par_done"), 1)
            dve.wait_ge(S("cond_sig"), 1)
            link(nc.vector.tensor_tensor(cs[:, 0], cs[:, 1], par[:, COND:COND + 32].rearrange("p (a k) -> p a k", a=2), ALU.mult))
            csk = cs[:, 0].rearrange("p a k -> p k a")
            link(nc.vector.tensor_copy(cond[:, :, 0:2], csk))
            nc.vector.tensor_tensor(cond[:, :, 2:4], csk, cond[:, :, 0:2].bitcast(F32), ALU.subtract).then_inc(S("cond"), 1)
            dve.wait_ge(S("grid_in"), 16)
            nrow = CONST["row"][1] - CONST["row"][0]
            for t in range(TILES):
                for q in range(4):
                    g = 4 * t + q
                    dve.wait_ge(S("xT_in"), g + 1)
                    src = ps[1 + g % 2][:].rearrange("p (k r c) -> p k r c", k=4, r=2)
                    dst = xT[:, 4 * q:4 * q + 4, t * P:(t + 1) * P].rearrange("p k (r c) -> p k r c", r=2)
                    if t == 0:
                        ins = nc.vector.tensor_copy(dst, src)
                    elif q < 2:
                        pos = grid[:, 0:nrow].rearrange("p (k r) -> p k r", r=4)[:, 4 * q:4 * q + 4, 2 * (t - 1):2 * t]
                        ins = nc.vector.tensor_tensor(dst, src, pos.unsqueeze(3).to_broadcast([P, 4, 2, 64]), ALU.add)
                    else:
                        pos = grid[:, nrow:].rearrange("p (k c) -> p k c", c=64)[:, 4 * q - 8:4 * q - 4, :]
                        ins = nc.vector.tensor_tensor(dst, src, pos.unsqueeze(2).to_broadcast([P, 4, 2, 64]), ALU.add)
                    ins.then_inc(S("xT_out"), 1)
            with dve.Fori(0, 12) as i:
                for n in range(RING):
                    dve.wait_ge(S("ada_hi"), i * RING + n + 1)
                    nc.vector.tensor_tensor(lo[:, n % HL], raw[:, n], hi[:, n % HL].bitcast(F32), ALU.subtract).then_inc(S("ada_lo"), 1)
            dve.wait_ge(S("ada_col"), 24)
            link(nc.vector.tensor_tensor(modT[:], ps[5][:, 0:192].rearrange("p (k a) -> p k a", a=2),
                                         par[:, 0:96].unsqueeze(2).to_broadcast([P, 96, 2]), ALU.add))
            for which, g in ((0, G_MIX), (1, G_FFN)):
                scale = modT[:, (3 * which + 1) * KC:(3 * which + 2) * KC, :]
                link(nc.vector.scalar_tensor_tensor(gain[:, which], scale, 1.0, par[:, g:g + KC].unsqueeze(2).to_broadcast([P, KC, 2]), ALU.add, ALU.mult))


def norm(nc, I, O, table, S, sb, ps, cst, par, modT, gain, xT, C, which, out):
    tag = f"norm{which}_"
    with ExitStack() as st:
        sq = sb(st, tag + "sq", [P, 2, T])
        rstd = sb(st, tag + "rstd", [P, T])
        xs = sb(st, tag + "xs", [P, 2, T])
        block = st.enter_context(nc.Block())

        @block.scalar
        def _(act):
            for k in range(KC):
                if k >= 2:
                    act.wait_ge(S(tag + "sum"), k - 1)
                nc.scalar.activation(sq[:, k % 2], xT[:, k], ACT.Square).then_inc(S(tag + "sq"), 1)
            act.wait_ge(S(tag + "mean"), 1)
            nc.scalar.sqrt(rstd[:], rstd[:]).then_inc(S(tag + "root"), 1)
            for k in range(KC):
                act.wait_ge(S(tag + "xs"), k + 1)
                for a, c0, c1 in ((1, 0, LC), (0, LC, T)):
                    ins = nc.scalar.activation(out[:, k, c0:c1], xs[:, k % 2, c0:c1], ACT.Identity,
                                               bias=modT[:, 3 * which * KC + k, a:a + 1], scale=gain[:, which, k, a:a + 1])
                ins.then_inc(S(tag + "out"), 1)

        @block.tensor
        def _(pe):
            for k in range(KC):
                pe.wait_ge(S(tag + "sq"), k + 1)
                pe.matmul(ps[0][:, 0:T], C("ones"), sq[:, k % 2], start=(k == 0), stop=(k == KC - 1)).then_inc(S(tag + "sum"), 1)

        @block.vector
        def _(dve):
            dve.wait_ge(S(tag + "sum"), KC)
            nc.vector.tensor_scalar(rstd[:], ps[0][:, 0:T], 1.0 / D, EPS, ALU.mult, ALU.add).then_inc(S(tag + "mean"), 1)
            dve.wait_ge(S(tag + "root"), 1)
            nc.vector.reciprocal(rstd[:], rstd[:]).then_inc(S(tag + "rstd"), 1)
            dve.wait_ge(S(tag + "rstd"), 1)
            for k in range(KC):
                if k >= 2:
                    dve.wait_ge(S(tag + "out"), k - 1)
                nc.vector.tensor_tensor(xs[:, k % 2], xT[:, k], rstd[:], ALU.mult).then_inc(S(tag + "xs"), 1)


def conv_silu(nc, S, tag, eng, link, cin, acc, sig, out, taps, bias):
    link(nc.vector.tensor_scalar(acc[:], cin[:, 0:388], taps(0), None, ALU.mult))
    for t in range(1, 4):
        link(nc.vector.scalar_tensor_tensor(acc[:], cin[:, t:t + 388], taps(t), acc[:], ALU.mult, ALU.add))
    nc.vector.scalar_tensor_tensor(acc[:], cin[:, 4:392], taps(4), acc[:], ALU.mult, ALU.add).then_inc(S(tag + "conv"), 1)


def ssd(nc, I, O, table, S, sb, ps, cst, par, modT, gain, xT, C, hT, mixed, lora):
    w_in = I["w_in"].rearrange("l (k p) n -> p (l k) n", p=P)
    with ExitStack() as st:
        B = sb(st, "B", [P, 2, T])
        Cm = sb(st, "Cm", [P, 2, T])
        Btok = sb(st, "Btok", [P, 2, TILES, P])
        BC = sb(st, "BC", [P, 2, TILES, P])
        cum = sb(st, "cum", [HEADS, 2, T])
        ea = sb(st, "ea", [HEADS, 2, T])
        r7 = sb(st, "r7", [HEADS, 7])
        tokq = sb(st, "tokq", [P, 3, 2, TILES, HEADS])
        cin = sb(st, "cin", [P, 2, 392])
        acc = sb(st, "acc", [P, 388])
        sig = sb(st, "sig", [P, 388])
        ssd_shared(nc, I, S, sb, ps, par, C, hT, lora, w_in, B, Cm, Btok, BC, cum, ea, r7, tokq, cin, acc, sig)
        ssd_heads(nc, I, O, S, sb, ps, par, C, hT, mixed, w_in, Cm, Btok, BC, cum, ea, r7, tokq, cin, acc, sig)


def ssd_shared(nc, I, S, sb, ps, par, C, hT, lora, w_in, B, Cm, Btok, BC, cum, ea, r7, tokq, cin, acc, sig):
    COLS = [(2560, 32)] + [(2048 + n * P, P) for n in range(4)] + \
           [(N_SSD_IN + 3072, P), (N_SSD_IN + 3200, 64), (N_SSD_IN + 3264, P), (N_SSD_IN + 3392, 32)]
    with ExitStack() as st:
        w = sb(st, "w_shared", [P, 6, KC, P])
        dt = sb(st, "dt", [HEADS, 2, T])
        q = sb(st, "q", [HEADS, 4, 2, T])
        small = sb(st, "small", [HEADS, 6])
        reset = sb(st, "reset", [HEADS, 2, T])
        lp = sb(st, "lp", [P, 4, T + 3])
        lt = sb(st, "lt", [P, T + 1])
        mu = sb(st, "mu_l", [P, 2, 4])
        loaded = [S(f"shared_loaded{n}") for n in range(9)]
        block = st.enter_context(nc.Block())
        LW = [P, 64, P, 32]
        LMU = [MU_WD, MU_AD, MU_GD0, MU_GD1]

        @block.sync
        def _(sp):
            for n, (c0, width) in enumerate(COLS):
                if n == 6:
                    sp.wait_ge(S("dt_proj"), 2)
                if n > 6:
                    sp.wait_ge(S("bc_proj"), n - 6)
                sp.dma_start(w[:, n % 6, :, 0:width], w_in[:, :, c0:c0 + width]).then_inc(loaded[n], 16)
            with nc.allow_non_contiguous_dma(reason="per-head scalars"):
                sp.dma_start(small[:, 0:2], I["ssd_A_log"].rearrange("l d h -> h (l d)")).then_inc(S("small_in"), 16)
                sp.dma_start(small[:, 2:4], I["ssd_dt_bias"].rearrange("l d h -> h (l d)")).then_inc(S("small_in"), 16)
                sp.dma_start(r7[:, 6:7], I["ssd_D"].rearrange("l h -> h l")).then_inc(S("small_in"), 16)

        @block.gpsimd
        def _(pool):
            nc.gpsimd.memset(cin[:], 0.0)
            nc.gpsimd.memset(lp[:], 0.0).then_inc(S("pads_zero"), 1)

        @block.tensor
        def _(pe):
            def project(n, bank, m0, m, done):
                pe.wait_ge(loaded[n], 16)
                for k in range(KC):
                    mm = pe.matmul(bank, w[:, n % 6, k, m0:m0 + m], hT[:, k], start=(k == 0), stop=(k == KC - 1))
                mm.then_inc(done, 1)

            project(0, ps[0][0:HEADS, 0:T], 0, HEADS, S("dt_proj"))
            project(0, ps[1][0:HEADS, 0:T], HEADS, HEADS, S("dt_proj"))
            for n in range(4):
                if n >= 2:
                    pe.wait_ge(S("bc_in"), n - 1)
                project(1 + n, ps[2 + n % 2][:, 0:T], 0, P, S("bc_proj"))
            for n in range(4):
                if n >= 2:
                    pe.wait_ge(S("lora_in"), n - 1)
                project(5 + n, ps[4 + n % 2][0:LW[n], 0:T], 0, LW[n], S("lora_proj"))
            for g in range(2):
                pe.wait_ge(S("bc_ready"), 4)
                for t in range(TILES):
                    mm = pe.transpose(ps[6][:, t * P:(t + 1) * P], B[:, g, t * P:(t + 1) * P], C("ident"))
                mm.then_inc(S("btok_in"), 1)
                for t in range(TILES):
                    mm = pe.matmul(ps[7][:, t * P:(t + 1) * P], B[:, g, t * P:(t + 1) * P], Cm[:, g, t * P:(t + 1) * P], start=True, stop=True)
                mm.then_inc(S("bcm_in"), 1)
                pe.wait_ge(S("btok_out"), 2 * g + 2)
            pe.wait_ge(S("rows_ready"), 1)
            for j, src in enumerate((dt, cum, q[:, 3])):
                for d in range(2):
                    for t in range(TILES):
                        at = ((j * 2 + d) * TILES + t) * HEADS
                        mm = pe.transpose(ps[0][:, at:at + HEADS], src[:, d, t * P:(t + 1) * P], C("ident", 0, HEADS)[:, 0:HEADS])
            mm.then_inc(S("tokq_in"), 1)

        @block.scalar
        def _(act):
            act.wait_ge(S("small_in"), 48)
            nc.scalar.activation(small[:, 4:6], small[:, 0:2], ACT.Exp).then_inc(S("A_exp"), 1)
            act.wait_ge(S("dt_abs"), 1)
            nc.scalar.activation(q[:, 1], q[:, 1], ACT.Exp, scale=-1.0).then_inc(S("dt_exp"), 1)
            act.wait_ge(S("pads_zero"), 1)
            for n in range(4):
                act.wait_ge(S("bc_proj"), n + 1)
                if n >= 2:
                    act.wait_ge(S("bc_conv"), n - 1)
                nc.scalar.copy(cin[:, n % 2, 2:130], ps[2 + n % 2][:, 0:LC])
                nc.scalar.copy(cin[:, n % 2, 134:390], ps[2 + n % 2][:, LC:T]).then_inc(S("bc_in"), 1)
                act.wait_ge(S("bc_conv"), n + 1)
                nc.scalar.activation(sig[:], acc[:], ACT.Sigmoid, bias=par[:, CONV_B + 8 + n:CONV_B + 9 + n]).then_inc(S("bc_sig"), 1)
            for n in range(4):
                act.wait_ge(S("lora_proj"), n + 1)
                b = ps[4 + n % 2][0:LW[n]]
                nc.scalar.copy(lp[0:LW[n], n, 1:129], b[:, 0:LC])
                nc.scalar.copy(lp[0:LW[n], n, 130:386], b[:, LC:T]).then_inc(S("lora_in"), 1)
            for g in range(2):
                act.wait_ge(S("btok_in"), g + 1)
                nc.scalar.copy(Btok[:, g], ps[6][:, 0:T].rearrange("p (t n) -> p t n", t=TILES)).then_inc(S("btok_out"), 1)
                act.wait_ge(S("bcm_in"), g + 1)
                nc.scalar.copy(BC[:, g], ps[7][:, 0:T].rearrange("p (t n) -> p t n", t=TILES)).then_inc(S("btok_out"), 1)
            act.wait_ge(S("lora_mixed"), 4)
            nc.scalar.activation(lora[:, 0], lora[:, 0], ACT.Tanh)
            nc.scalar.activation(lora[:, 2:4], lora[:, 2:4], ACT.Sigmoid)
            act.wait_ge(S("cum_ready"), 2)
            nc.scalar.activation(ea[:], cum[:], ACT.Exp)
            nc.scalar.activation(r7[:, 0:6], q[:, 0, :, 0:3], ACT.Exp)
            nc.scalar.activation(q[:, 2], q[:, 2], ACT.Exp).then_inc(S("decay_exp"), 1)

        @block.vector
        def _(dve):
            link = Link(dve, S("shared_dve"))
            link(nc.vector.memset(reset[:], 1.0))
            link(nc.vector.memset(reset[:].rearrange("p d (t c) -> p (d t) c", c=P)[:, :, 0:1], 0.0))
            link(nc.vector.memset(lora[:, 3], 0.0))
            dve.wait_ge(S("A_exp"), 1)
            dve.wait_ge(S("dt_proj"), 2)
            for d in range(2):
                link(nc.vector.tensor_scalar(dt[:, d], ps[d][0:HEADS, 0:T], small[:, 2 + d:3 + d], None, ALU.add))
            nc.vector.scalar_tensor_tensor(q[:, 1], dt[:], -1.0, dt[:], ALU.mult, ALU.max).then_inc(S("dt_abs"), 1)
            dve.wait_ge(S("dt_exp"), 1)
            link(nc.vector.tensor_scalar(q[:, 2], q[:, 1], 2.0, None, ALU.add))
            link(nc.vector.reciprocal(q[:, 2], q[:, 2]))
            link(nc.vector.tensor_tensor(q[:, 1], q[:, 1], q[:, 2], ALU.mult))
            link(nc.vector.tensor_tensor(q[:, 2], q[:, 1], q[:, 1], ALU.mult))
            link(nc.vector.tensor_scalar(q[:, 3], q[:, 2], 1.0 / 17, None, ALU.mult))
            for odd in (15, 13, 11, 9, 7, 5, 3):
                link(nc.vector.scalar_tensor_tensor(q[:, 3], q[:, 3], 1.0 / odd, q[:, 2], ALU.add, ALU.mult))
            link(nc.vector.scalar_tensor_tensor(q[:, 3], q[:, 3], 1.0, q[:, 1], ALU.add, ALU.mult))
            link(nc.vector.tensor_scalar(q[:, 3], q[:, 3], 2.0, None, ALU.mult))
            link(nc.vector.scalar_tensor_tensor(dt[:], dt[:], 0.0, q[:, 3], ALU.max, ALU.add))
            for d in range(2):
                link(nc.vector.tensor_scalar(q[:, 1, d], dt[:, d], small[:, 4 + d:5 + d], -1.0, ALU.mult, ALU.mult))
            for d in range(2):
                link(nc.vector.tensor_tensor_scan(cum[:, d], reset[:, d], q[:, 1, d], 0.0, ALU.mult, ALU.add))
            tot = q[:, 0, :, 0:3]
            link(nc.vector.tensor_copy(tot, cum[:].rearrange("p d (t c) -> p d t c", c=P)[:, :, :, P - 1]))
            link(nc.vector.tensor_tensor(cum[:, 1], q[:, 1, 1], cum[:, 1], ALU.subtract))
            for d in range(2):
                c3 = cum[:, d].rearrange("p (t c) -> p t c", c=P)
                tb = tot[:, d].unsqueeze(2).to_broadcast([HEADS, TILES, P])
                if d == 1:
                    link(nc.vector.tensor_tensor(c3, c3, tb, ALU.add))
                nc.vector.tensor_tensor(q[:, 2, d].rearrange("p (t c) -> p t c", c=P), tb, c3, ALU.subtract).then_inc(S("cum_ready"), 1)
            for n in range(4):
                dve.wait_ge(S("bc_in"), n + 1)
                conv_silu(nc, S, "bc_", dve, link, cin[:, n % 2], acc, sig, None, lambda t: par[:, CONV_W + 12 * t + 8 + n:CONV_W + 12 * t + 9 + n], None)
                dve.wait_ge(S("bc_sig"), n + 1)
                out = (B, Cm)[n // 2][:, n % 2]
                b = par[:, CONV_B + 8 + n:CONV_B + 9 + n]
                nc.vector.scalar_tensor_tensor(out[:, 0:LC], acc[:, 0:LC], b, sig[:, 0:LC], ALU.add, ALU.mult)
                nc.vector.scalar_tensor_tensor(out[:, LC:T], acc[:, 132:388], b, sig[:, 132:388], ALU.add, ALU.mult).then_inc(S("bc_ready"), 1)
                dve.wait_ge(S("bc_ready"), n + 1)
            for n in range(4):
                m = par[:, MU + LMU[n]:MU + LMU[n] + 1]
                link(nc.vector.tensor_scalar(mu[:, 0, n:n + 1], m, -1.0, 1.0, ALU.mult, ALU.add))
                link(nc.vector.tensor_scalar(mu[:, 1, n:n + 1], m, 0.5, None, ALU.mult))
            for n in range(4):
                r = LW[n]
                dve.wait_ge(S("lora_in"), n + 1)
                link(nc.vector.tensor_tensor(lt[0:r], lp[0:r, n, 0:T + 1], lp[0:r, n, 2:T + 3], ALU.add))
                link(nc.vector.tensor_scalar(lt[0:r], lt[0:r], mu[0:r, 1, n:n + 1], None, ALU.mult))
                for c0, c1, skip in ((0, LC, 0), (LC, T, 1)):
                    ins = nc.vector.scalar_tensor_tensor(lora[0:r, n, c0:c1], lp[0:r, n, c0 + 1 + skip:c1 + 1 + skip], mu[0:r, 0, n:n + 1],
                                                         lt[0:r, c0 + skip:c1 + skip], ALU.mult, ALU.add)
                ins.then_inc(S("lora_mixed"), 1)
                dve.wait_ge(S("lora_mixed"), n + 1)
            dve.wait_ge(S("decay_exp"), 1)
            nc.vector.tensor_tensor(q[:, 3], q[:, 2], dt[:], ALU.mult).then_inc(S("rows_ready"), 1)
            dve.wait_ge(S("tokq_in"), 1)
            src = ps[0][:, 0:288].rearrange("p (q r) -> p q r", q=3)
            dst = tokq[:].rearrange("p q d t h -> p q (d t h)")
            link(nc.vector.tensor_copy(dst, src))
            link(nc.vector.tensor_scalar(dst[:, 1], dst[:, 1], -1.0, None, ALU.mult))


def ssd_heads(nc, I, O, S, sb, ps, par, C, hT, mixed, w_in, Cm, Btok, BC, cum, ea, r7, tokq, cin, acc, sig):
    HG = KC // 4
    with ExitStack() as st:
        w = sb(st, "w_xz", [P, 2, KC, P])
        h0 = sb(st, "h0", [P, 2, P])
        xc = sb(st, "xc", [P, T])
        z = sb(st, "z", [P, 2, T])
        sel = sb(st, "sel", [HEADS, 2, P])
        selc = sb(st, "selc", [HEADS, P])
        xq = sb(st, "xq", [P, 4, TILES, P])
        M = sb(st, "M", [P, 4, TILES, P])
        eac = sb(st, "eac", [P, 2, LS])
        r7c = sb(st, "r7c", [P, 7])
        fin = sb(st, "fin", [P, 2, P])
        s1 = sb(st, "s1", [P, 2, P])
        sT = sb(st, "sT", [P, 4, P])
        yo = sb(st, "yo", [P, 2, LS])
        y = sb(st, "y", [P, T])
        block = st.enter_context(nc.Block())
        states = [I["state_ssd_fwd"].rearrange("b l h p n -> (b l h p) n"), I["state_ssd_bwd"].rearrange("b l h p n -> (b l h p) n")]
        finals = [O["ssd_fwd"].rearrange("b l h p n -> (b l h p) n"), O["ssd_bwd"].rearrange("b l h p n -> (b l h p) n")]
        ident16 = C("ident", 0, HEADS)

        @block.gpsimd
        def _(pool):
            ahead(pool, S, "z_proj", "hT_in", "eac_out", "r7_out", "seg_done", "sT_out", "s1_ready", "y_done", "xtok_in", "x_conv", "fin_out", "y_in")

        def turns(eng, body):
            with eng.Fori(0, 2) as g:
                with eng.Fori(0, HG) as c4:
                    body(g, g * HG + c4)

        @block.sync
        def _(sp):
            def body(g, c):
                x_cols, z_cols, turn, stored = c * P + 1024, c * P, sp.snap(c), sp.snap(c + 1)
                sp.wait_ge(S("z_proj"), turn + 1)
                sp.dma_start(w[:, 0], w_in[:, :, bass.ds(x_cols, P)]).then_inc(S("wx_loaded"), 16)
                sp.dma_start(w[:, 1], w_in[:, :, bass.ds(z_cols, P)]).then_inc(S("wz_loaded"), 16)
                sp.wait_ge(S("hT_in"), turn + 1)
                for d in range(2):
                    sp.dma_start(h0[:, d], states[d][bass.ds(z_cols, P), :]).then_inc(S("h0_in"), 16)
                sp.wait_ge(S("fin_ready"), stored)
                for d in range(2):
                    sp.dma_start(finals[d][bass.ds(z_cols, P), :], fin[:, d]).then_inc(S("fin_out"), 16)
            turns(sp, body)
            sp.wait_ge(S("fin_out"), 16 * 2 * PAIRS + 1)

        @block.tensor
        def _(pe):
            def body(g, c):
                pe.wait_ge(S("wx_loaded"), (c + 1) * 16)
                pe.wait_ge(S("eac_out"), c + 1)
                for k in range(KC):
                    mm = pe.matmul(ps[0][:, 0:T], w[:, 0, k], hT[:, k], start=(k == 0), stop=(k == KC - 1))
                mm.then_inc(S("x_proj"), 1)
                pe.wait_ge(S("wz_loaded"), (c + 1) * 16)
                pe.wait_ge(S("r7_out"), c + 1)
                for k in range(KC):
                    mm = pe.matmul(ps[1][:, 0:T], w[:, 1, k], hT[:, k], start=(k == 0), stop=(k == KC - 1))
                mm.then_inc(S("z_proj"), 1)
                pe.wait_ge(S("sel_ready"), c + 1)
                for u in range(4):
                    if u < 2:
                        pe.wait_ge(S("seg_done"), c * 4 + 1)
                    else:
                        pe.wait_ge(S("seg_done"), c * 4 + u - 1 + 1)
                    pe.matmul(ps[3 + u % 2][:, 0:T], sel[:, u // 2], cum[:, u % 2], start=True, stop=True).then_inc(S("seg_in"), 1)
                pe.wait_ge(S("x_in_conv"), c + 1)
                for d in range(2):
                    mm = pe.matmul(ps[0][:, d * LS:(d + 1) * LS], selc[:], ea[:, d, LC:T], start=True, stop=True)
                mm.then_inc(S("eac_in"), 1)
                pe.wait_ge(S("z_out"), c + 1)
                pe.matmul(ps[1][:, 0:7], selc[:], r7[:], start=True, stop=True).then_inc(S("r7_in"), 1)
                pe.wait_ge(S("xc_ready"), c + 1)
                pe.wait_ge(S("sT_out"), c + 1)
                for t in range(TILES):
                    mm = pe.transpose(ps[2][:, t * P:(t + 1) * P], xc[:, t * P:(t + 1) * P], C("ident"))
                mm.then_inc(S("xtok_in"), 1)
                pe.wait_ge(S("xq_ready"), c + 1)
                pe.wait_ge(S("s1_ready"), c + 1)
                for k, (d, t) in enumerate(((0, 0), (1, 0), (0, 1), (1, 2))):
                    mm = pe.matmul(ps[5][:, k * P:(k + 1) * P], xq[:, 2 + d, t], Btok[:, bass.ds(g, 1), t], start=True, stop=True)
                mm.then_inc(S("states_in"), 1)
                pe.wait_ge(S("s1_ready"), c + 2)
                for k in range(4):
                    mm = pe.transpose(ps[2][:, k * P:(k + 1) * P], (h0, s1)[k // 2][:, k % 2], C("ident"))
                mm.then_inc(S("hT_in"), 1)
                pe.wait_ge(S("M_ready"), 4 * (c + 1))
                pe.wait_ge(S("y_done"), c + 1)
                for t in range(TILES):
                    for h in range(2):
                        for d in range(2):
                            mm = pe.matmul(ps[6][h * HD:(h + 1) * HD, t * P:(t + 1) * P], xq[:, d, t, h * HD:(h + 1) * HD], M[:, 2 * h + d, t],
                                           start=(d == 0), stop=(d == 1))
                mm.then_inc(S("y_in"), 1)
                pe.wait_ge(S("sT_out"), c + 2)
                for d, t, k in ((0, 1, 0), (0, 2, 2), (1, 2, 1), (1, 1, 3)):
                    at = d * LS + (t - 1) * P
                    mm = pe.matmul(ps[7][:, at:at + P], sT[:, k], Cm[:, bass.ds(g, 1), t * P:(t + 1) * P], start=True, stop=True)
                mm.then_inc(S("yo_in"), 1)
            turns(pe, body)

        @block.scalar
        def _(act):
            def body(g, c):
                act.wait_ge(S("xtok_in"), c + 1)
                nc.scalar.copy(sel[:], ident16[:, bass.ds(c * 2, 2)].unsqueeze(2).to_broadcast([HEADS, 2, P]))
                nc.scalar.copy(selc[:].rearrange("p (h c) -> p h c", h=2),
                               ident16[:, bass.ds(c * 2, 2)].unsqueeze(2).to_broadcast([HEADS, 2, HD])).then_inc(S("sel_ready"), 1)
                act.wait_ge(S("x_proj"), c + 1)
                act.wait_ge(S("x_conv"), c + 1)
                nc.scalar.copy(cin[:, 0, 2:130], ps[0][:, 0:LC])
                nc.scalar.copy(cin[:, 0, 134:390], ps[0][:, LC:T]).then_inc(S("x_in_conv"), 1)
                act.wait_ge(S("z_proj"), c + 2)
                act.wait_ge(S("y_done"), c + 1)
                nc.scalar.activation(z[:, 1], ps[1][:, 0:T], ACT.Sigmoid)
                nc.scalar.copy(z[:, 0], ps[1][:, 0:T]).then_inc(S("z_out"), 1)
                act.wait_ge(S("x_conv"), c + 2)
                nc.scalar.activation(sig[:], acc[:], ACT.Sigmoid, bias=par[:, bass.ds(c + CONV_B, 1)]).then_inc(S("x_sig"), 1)
                act.wait_ge(S("eac_in"), c + 1)
                nc.scalar.copy(eac[:], ps[0][:].rearrange("p (d t) -> p d t", d=2)).then_inc(S("eac_out"), 1)
                act.wait_ge(S("r7_in"), c + 1)
                nc.scalar.copy(r7c[:], ps[1][:, 0:7]).then_inc(S("r7_out"), 1)
                for u in range(4):
                    act.wait_ge(S("seg_done"), c * 4 + u + 2)
                    nc.scalar.activation(M[:, u], M[:, u], ACT.Exp).then_inc(S("M_exp"), 1)
                act.wait_ge(S("states_in"), c + 1)
                act.wait_ge(S("fin_out"), c * 32 + 1)
                nc.scalar.copy(fin[:], ps[5][:, 0:2 * P].rearrange("p (d n) -> p d n", d=2)).then_inc(S("fin_ready"), 1)
                act.wait_ge(S("hT_in"), c + 2)
                nc.scalar.copy(sT[:], ps[2][:].rearrange("p (k n) -> p k n", k=4)).then_inc(S("sT_out"), 1)
            turns(act, body)

        STEPS = 4 + 5

        @block.vector
        def _(dve):
            def body(g, c):
                link = Link(dve, S("ssd_dve"), c * STEPS)
                dve.wait_ge(S("x_in_conv"), c + 1)
                conv_silu(nc, S, "x_", dve, link, cin[:, 0], acc, sig, None, lambda t: par[:, bass.ds(c + (CONV_W + 12 * t), 1)], None)
                dve.wait_ge(S("x_sig"), c + 1)
                b = par[:, bass.ds(c + CONV_B, 1)]
                nc.vector.scalar_tensor_tensor(xc[:, 0:LC], acc[:, 0:LC], b, sig[:, 0:LC], ALU.add, ALU.mult)
                nc.vector.scalar_tensor_tensor(xc[:, LC:T], acc[:, 132:388], b, sig[:, 132:388], ALU.add, ALU.mult).then_inc(S("xc_ready"), 1)
                for u in range(4):
                    dve.wait_ge(S("seg_in"), c * 4 + u + 1)
                    dve.wait_ge(S("y_in"), c + 1)
                    for t in range(TILES):
                        ins = nc.vector.scalar_tensor_tensor(M[:, u, t], ps[3 + u % 2][:, t * P:(t + 1) * P], tokq[:, 1, u % 2, t, bass.ds(c * 2 + u // 2, 1)],
                                                             C(f"neg{u % 2}"), ALU.add, ALU.add)
                    ins.then_inc(S("seg_done"), 1)
                dve.wait_ge(S("xtok_in"), c + 2)
                src = ps[2][:, 0:T].rearrange("p (t h c) -> p t h c", t=TILES, h=2)
                for k in range(4):
                    f = tokq[:, (0, 2)[k // 2], k % 2, :, bass.ds(c * 2, 2)].unsqueeze(3).to_broadcast([P, TILES, 2, HD])
                    ins = nc.vector.tensor_tensor(xq[:, k].rearrange("p t (h c) -> p t h c", h=2), src, f, ALU.mult)
                ins.then_inc(S("xq_ready"), 1)
                dve.wait_ge(S("states_in"), c + 1)
                dve.wait_ge(S("r7_out"), c + 2)
                dve.wait_ge(S("h0_in"), (c + 1) * 32)
                dve.wait_ge(S("fin_ready"), c + 1)
                for d in range(2):
                    ins = nc.vector.scalar_tensor_tensor(s1[:, d], h0[:, d], r7c[:, 3 * d + (1, 2)[d]:3 * d + (1, 2)[d] + 1], ps[5][:, (2 + d) * P:(3 + d) * P], ALU.mult, ALU.add)
                ins.then_inc(S("s1_ready"), 1)
                for u in range(4):
                    dve.wait_ge(S("M_exp"), c * 4 + u + 1)
                    nc.vector.tensor_tensor(M[:, u], M[:, u], BC[:, bass.ds(g, 1)].rearrange("p a t n -> p (a t) n"), ALU.mult).then_inc(S("M_ready"), 1)
                dve.wait_ge(S("y_in"), c + 2)
                dve.wait_ge(S("y_done"), c + 1)
                link(nc.vector.scalar_tensor_tensor(y[:], xc[:], r7c[:, 6:7], ps[6][:, 0:T], ALU.mult, ALU.add))
                dve.wait_ge(S("yo_in"), c + 1)
                link(nc.vector.tensor_tensor(yo[:], ps[7][:].rearrange("p (d t) -> p d t", d=2), eac[:], ALU.mult))
                for d in range(2):
                    link(nc.vector.tensor_tensor(y[:, LC:T], y[:, LC:T], yo[:, d], ALU.add))
                link(nc.vector.tensor_tensor(y[:], y[:], z[:, 0], ALU.mult))
                nc.vector.tensor_tensor(mixed[:, bass.ds(c, 1)].rearrange("p a t -> p (a t)"), y[:], z[:, 1], ALU.mult).then_inc(S("y_done"), 1)
                assert link.n == STEPS
            turns(dve, body)

    with ExitStack() as st:
        sq = sb(st, "sq", [P, 2, T])
        rstd = sb(st, "rstd", [P, 2, T])
        block = st.enter_context(nc.Block())

        @block.scalar
        def _(act):
            for k in range(PAIRS):
                if k >= 2:
                    act.wait_ge(S("gn_sum"), k - 1)
                nc.scalar.activation(sq[:, k % 2], mixed[:, k], ACT.Square).then_inc(S("gn_sq"), 1)
            act.wait_ge(S("gn_mean"), 1)
            nc.scalar.sqrt(rstd[:], rstd[:]).then_inc(S("gn_root"), 1)

        @block.tensor
        def _(pe):
            for k in range(PAIRS):
                pe.wait_ge(S("gn_sq"), k + 1)
                pe.matmul(ps[k // HG][:, 0:T], C("ones"), sq[:, k % 2], start=(k % HG == 0), stop=(k % HG == HG - 1)).then_inc(S("gn_sum"), 1)

        @block.vector
        def _(dve):
            dve.wait_ge(S("gn_sum"), PAIRS)
            for g in range(2):
                ins = nc.vector.tensor_scalar(rstd[:, g], ps[g][:, 0:T], 1.0 / (HG * P), EPS, ALU.mult, ALU.add)
            ins.then_inc(S("gn_mean"), 1)
            dve.wait_ge(S("gn_root"), 1)
            nc.vector.reciprocal(rstd[:], rstd[:]).then_inc(S("gn_rstd"), 1)
            dve.wait_ge(S("gn_rstd"), 1)
            for k in range(PAIRS):
                ins = nc.vector.scalar_tensor_tensor(mixed[:, k], mixed[:, k], par[:, G_SSD + k:G_SSD + k + 1], rstd[:, k // HG], ALU.mult, ALU.mult)
            ins.then_inc(S("gn_done"), 1)


def rwkv(nc, I, O, table, S, sb, ps, cst, par, modT, gain, xT, C, hT, mixed, lora):
    w_in = I["w_in"].rearrange("l (k p) n -> p (l k) n", p=P)
    w_up = I["rwkv_w_up"].rearrange("l d r n -> (l d r) n")
    a_up, g_up = I["rwkv_a_up"][0], I["rwkv_g_up"][0]
    with ExitStack() as st:
        w = sb(st, "w_rkv", [P, 3, KC, P])
        lw = sb(st, "lw", [P, 4, P])
        raw = sb(st, "raw_rkv", [P, 3, T + 3])
        sh = sb(st, "sh", [P, T + 1])
        mu = sb(st, "mu_rkv", [P, 2, 24])
        omk = sb(st, "omk", [P, PAIRS])
        reset = sb(st, "reset64", [P, T])
        r, k, kk, ka, a, g, bonus, t0 = (sb(st, n, [P, T]) for n in ("r", "k", "kk", "ka", "a", "g", "bonus", "t0"))
        v = sb(st, "v", [P, Q + T])
        sg = sb(st, "sg", [P, 2, T])
        ex = sb(st, "ex", [P, 3, T])
        wl = sb(st, "wl", [P, 2 * NCH])
        wls = sb(st, "wls", [Q, 2, 2 * NCH])
        s0 = sb(st, "s0", [P, 2, HD])
        fin = sb(st, "fin_r", [Q, 2, P])
        fo = sb(st, "fo", [P, 2, HD])
        M1 = [sb(st, f"M1_{d}", [P, NCH, 3, Q]) for d in range(2)]
        M2 = [sb(st, f"M2_{d}", [P, NCH, 3, Q]) for d in range(2)]
        W1 = [sb(st, f"W1_{d}", [P, NCH, 3, Q]) for d in range(2)]
        WX = [sb(st, f"WX_{d}", [P, 4 * NCH * Q]) for d in range(2)]
        WI = [sb(st, f"WI_{d}", [P, 3, NCH * Q]) for d in range(2)]
        VS = [sb(st, f"VS_{d}", [P, NCH, 2, HD]) for d in range(2)]
        W2 = [x[:, 0:3 * NCH * Q].rearrange("p (c j q) -> p c j q", c=NCH, j=3) for x in WX]
        P1 = [x[:, 3 * NCH * Q:].rearrange("p (c q) -> p c q", c=NCH) for x in WX]
        XX = [x[:].rearrange("p (h c q) -> p h c q", h=2, c=NCH) for x in WX]
        X, XT, CT = ([x[:, j].rearrange("p (c q) -> p c q", c=NCH) for x in WI] for j in range(3))
        PU = [x[:, 1:3].rearrange("p j q -> p (j q)").rearrange("p (c q) -> p c q", c=NCH) for x in WI]
        block = st.enter_context(nc.Block())
        HP = (slice(0, Q), slice(Q, P))
        SEQ = (((0, 1), (2, 3, 4, 5)), ((1, 0), (5, 4, 3, 2)))
        states = [I["state_rwkv_fwd"].rearrange("b l h v k -> (b l h v) k"), I["state_rwkv_bwd"].rearrange("b l h v k -> (b l h v) k")]
        finals = [O["rwkv_fwd"].rearrange("b l h v k -> (b l h v) k"), O["rwkv_bwd"].rearrange("b l h v k -> (b l h v) k")]

        def c6(x):
            return x.rearrange("p (c q) -> p c q", c=NCH)

        def rounds():
            for rnd in range(3):
                for d in range(2):
                    for part in range(2):
                        seq = SEQ[d][part]
                        if rnd < 2 or part == 1:
                            yield rnd, 2 * d + part, d, seq[rnd], seq[rnd + 1] if rnd + 1 < len(seq) else None

        @block.sync
        def _(sp):
            def load_rkv(p):
                for j in range(3):
                    sp.dma_start(w[:, j], w_in[:, :, bass.ds(p * P + (N_SSD_IN + 1024 * j), P)]).then_inc(S("rkv_loaded"), 16)

            def load_small(p):
                sp.dma_start(lw[:, 0], w_up[:, bass.ds(p * P + 0, P)]).then_inc(S("lw_loaded"), 16)
                sp.dma_start(lw[0:64, 1], a_up[:, bass.ds(p * P + 0, P)]).then_inc(S("lw_loaded"), 16)
                sp.dma_start(lw[:, 2], g_up[0:P, bass.ds(p * P + 0, P)]).then_inc(S("lw_loaded"), 16)
                sp.dma_start(lw[0:32, 3], g_up[P:P + 32, bass.ds(p * P + 0, P)]).then_inc(S("lw_loaded"), 16)

            def load_states(p):
                for d in range(2):
                    sp.dma_start(s0[:, d], states[d][bass.ds(p * P + 0, P), :]).then_inc(S("s0_loaded"), 16)

            def body(p, more):
                if more >= 2:
                    sp.wait_ge(S("v_proj"), p + 2)
                    load_rkv(p + 2)
                if more >= 1:
                    sp.wait_ge(S("lora_up"), p + 1)
                    load_small(p + 1)
                    sp.wait_ge(S("s0_in"), p + 1)
                    load_states(p + 1)
                sp.wait_ge(S("fo_ready"), p + 1)
                for d in range(2):
                    sp.dma_start(finals[d][bass.ds(p * P + 0, P), :], fo[:, d]).then_inc(S("fo_out"), 16)

            load_rkv(0)
            load_small(0)
            load_states(0)
            sp.wait_ge(S("v_proj"), 1)
            load_rkv(1)
            with sp.Fori(0, PAIRS - 2) as p:
                body(p, 2)
            body(PAIRS - 2, 1)
            body(PAIRS - 1, 0)
            sp.wait_ge(S("fo_out"), 32 * PAIRS + 1)

        @block.gpsimd
        def _(pool):
            ahead(pool, S, "y_read", "var_read", "P1_in0", "P1_in1", "XX_ready0", "XX_ready1", "pair_done", "fo_out")
            nc.gpsimd.memset(raw[:], 0.0)
            nc.gpsimd.memset(v[:], 0.0)
            for d in range(2):
                nc.gpsimd.memset(VS[d][:], 0.0)
            nc.gpsimd.memset(reset[:], 1.0).then_inc(S("reset_ones"), 1)
            pool.wait_ge(S("reset_ones"), 1)
            nc.gpsimd.memset(c6(reset[:])[:, :, 0:1], 0.0)
            i2 = C("i2").unsqueeze(1).to_broadcast([P, NCH, Q])
            for d in range(2):
                nc.gpsimd.tensor_copy(M1[d][:, :, 0], i2)
                ins = nc.gpsimd.tensor_copy(M2[d][:, :, 1], i2)
            ins.then_inc(S("rwkv_fixed"), 1)
            with pool.Fori(0, PAIRS) as p:
                for n in range(1, 6):
                    for d in range(2):
                        pool.wait_ge(S(f"W2_ready{d}"), 3 * p + 3)
                        pool.wait_ge(S(f"P1_in{d}"), 5 * p + n - 1 + 1)
                        pool.wait_ge(S(f"XX_ready{d}"), 8 * p + 1)
                        m = C(("high", "low")[d] + str(n)).unsqueeze(1).to_broadcast([P, NCH, Q])
                        nc.gpsimd.tensor_tensor(CT[d], W2[d][:, :, 2], m, ALU.mult).then_inc(S(f"CT_ready{d}"), 1)

        @block.tensor
        def _(pe):
            def hold():
                pe.sem_inc(S("pe_held"), 1)

            def project(j, bank, done):
                for n in range(KC):
                    mm = pe.matmul(ps[bank][:, 0:T], w[:, j, n], hT[:, n], start=(n == 0), stop=(n == KC - 1))
                mm.then_inc(S(done), 1)

            def small(bank, m, lhsT, rhs, done, n=T, start=True, stop=True):
                mm = pe.matmul(ps[bank][0:m, 0:n], lhsT, rhs, start=start, stop=stop)
                if done:
                    mm.then_inc(S(done), 1)

            def body(p, more):
                pe.wait_ge(S("lw_loaded"), (p + 1) * 64)
                pe.wait_ge(S("y_read"), p + 1)
                pe.wait_ge(S("var_read"), p + 1)
                small(0, P, lw[0:64, 0], lora[0:64, 0], None)
                small(1, P, lw[64:128, 0], lora[64:128, 0], None)
                small(2, P, lw[0:64, 1], lora[0:64, 1], None)
                small(5, P, lw[:, 2], lora[:, 2], None, stop=False)
                small(5, P, lw[0:32, 3], lora[0:32, 3], "lora_up", start=False)
                pe.wait_ge(S("kk_sq"), p + 1)
                small(3, P, C("blk"), t0[:], "kk_sum")
                if more:
                    pe.wait_ge(S("rkv_loaded"), (p + 2) * 48)
                    pe.wait_ge(S("raw_in"), 3 * p + 3)
                    project(0, 6, "r_proj")
                pe.wait_ge(S("bonus_mul"), p + 1)
                small(4, P, C("blk"), t0[:], "bonus_sum")
                pe.wait_ge(S("v_ready"), p + 1)
                pe.wait_ge(S("g_out"), p + 1)
                pe.wait_ge(S("kk_root"), p + 1)
                pe.wait_ge(S("s0_loaded"), (p + 1) * 32)
                for c in range(NCH):
                    bank, at = (5, c * P) if c < 4 else (3, (c - 4) * P)
                    pe.transpose(ps[bank][:, at:at + P], v[:, c * Q:c * Q + P], C("ident"))
                for d in range(2):
                    mm = pe.transpose(ps[3][0:HD, (2 + d) * P:(3 + d) * P], s0[:, d], C("ident"))
                mm.then_inc(S("s0_in"), 1)
                pe.wait_ge(S("wl_ready"), 2 * p + 2)
                pe.wait_ge(S("bonus_ready"), p + 1)
                for h in range(2):
                    mm = pe.matmul(ps[4][0:Q, h * 2 * NCH:(h + 1) * 2 * NCH], C("ident")[:, h * Q:(h + 1) * Q], wl[:], start=True, stop=True)
                mm.then_inc(S("wls_in"), 1)
                if more:
                    project(1, 7, "k_proj")
                for d in range(2):
                    pe.wait_ge(S(f"hats{d}"), 4 * p + 4)
                    if d == 0:
                        pe.wait_ge(S("sig_out"), p + 1)
                    else:
                        pe.wait_ge(S("VS_ready"), p + 1)
                        pe.wait_ge(S("wls_out"), p + 1)
                    hold()
                    for c in range(NCH):
                        for h in range(2):
                            mm = pe.matmul(ps[3 * d + c // 2][HP[h], (c % 2) * 192:(c % 2 + 1) * 192], M2[d][HP[h], c, 2], M1[d][HP[h], c], start=True, stop=True)
                    mm.then_inc(S(f"E1_in{d}"), 1)
                for d in range(2):
                    pe.wait_ge(S(f"W1_ready{d}"), 3 * p + 3)
                    hold()
                    for c in range(NCH):
                        for h in range(2):
                            mm = pe.matmul(ps[3 * d + c // 2][HP[h], (c % 2) * 192:(c % 2 + 1) * 192], M1[d][HP[h], c, 2], M2[d][HP[h], c], start=True, stop=True)
                    mm.then_inc(S(f"E2_in{d}"), 1)
                if more:
                    pe.wait_ge(S("raw_in"), 3 * p + 4)
                    project(2, 6, "v_proj")
                for n in range(1, 6):
                    for d in range(2):
                        pe.wait_ge(S(f"CT_ready{d}"), 5 * p + n)
                        pe.wait_ge(S(f"X_ready{d}"), 5 * p + n)
                        hold()
                        for c in range(NCH):
                            for h in range(2):
                                mm = pe.matmul(ps[3 * d][HP[h], c * Q:(c + 1) * Q], CT[d][HP[h], c], X[d][HP[h], c], start=True, stop=True)
                        mm.then_inc(S(f"P1_in{d}"), 1)
                    for d in range(2):
                        pe.wait_ge(S(f"P1_out{d}"), 5 * p + n)
                        hold()
                        for c in range(NCH):
                            for h in range(2):
                                mm = pe.matmul(ps[3 * d + 1][HP[h], c * Q:(c + 1) * Q], XT[d][HP[h], c], P1[d][HP[h], c], start=True, stop=True)
                                if n < 5:
                                    mm = pe.matmul(ps[3 * d + 2][HP[h], c * Q:(c + 1) * Q], P1[d][HP[h], c], XT[d][HP[h], c], start=True, stop=True)
                        mm.then_inc(S(f"D_in{d}"), 1)
                for d in range(2):
                    pe.wait_ge(S(f"X_final{d}"), p + 1)
                    hold()
                    for c in range(NCH):
                        for h in range(2):
                            mm = pe.matmul(ps[3 * d + c // 4][HP[h], (c % 4) * P:(c % 4 + 1) * P], X[d][HP[h], c], W2[d][HP[h], c, 0:2], start=True, stop=True)
                    mm.then_inc(S(f"PU_in{d}"), 1)
                for u in range(8):
                    for d in range(2):
                        h, c0, c1 = u // 4, (0, 4)[u // 2 % 2], (4, NCH)[u // 2 % 2]
                        if u >= 3:
                            pe.wait_ge(S(f"XX_ready{d}"), 8 * p + u - 2 + 1)
                        elif u >= 1:
                            pe.wait_ge(S(f"PU_out{d}"), p + 1)
                        hold()
                        for c in range(c0, c1):
                            out = ps[3 * d + (2 + u) % 3][:, (c - c0) * P:(c - c0 + 1) * P]
                            if u % 2 == 0:
                                mm = pe.matmul(out, M1[d][HP[h], c, 0:2], M2[d][HP[h], c, 0:2], start=True, stop=True)
                            else:
                                mm = pe.matmul(out, W1[d][HP[h], c, 0:2], PU[d][HP[h], c], start=True, stop=True)
                        mm.then_inc(S(f"XX_in{d}"), 1)
                for rnd, item, d, c, nxt in rounds():
                    if (item, d) == (0 if rnd < 2 else 1, 0):
                        if rnd == 0:
                            pe.wait_ge(S("XX_ready0"), 8 * p + 8 + 1)
                            pe.wait_ge(S("XX_ready1"), 8 * p + 8 + 1)
                            pe.wait_ge(S("VS_ready"), p + 1)
                        else:
                            pe.wait_ge(S("state_out"), 10 * p + 4 * rnd)
                    hold()
                    for h in range(2):
                        at = item * P + h * HD
                        mm = pe.matmul(ps[rnd % 2][0:Q, at:at + HD], XX[d][:, h, c, Q:P], VS[d][:, c, h], start=True, stop=True)
                    mm.then_inc(S("state_in"), 1)
                pe.wait_ge(S("state_out"), 10 * p + 10)
                hold()
                for c in range(NCH):
                    for h in range(2):
                        for d in range(2):
                            mm = pe.matmul(ps[2][HP[h], c * Q:(c + 1) * Q], VS[d][:, c, h], XX[d][:, h, c, 0:Q], start=(d == 0), stop=(d == 1))
                mm.then_inc(S("y_in_r"), 1)
                for d in range(2):
                    mm = pe.transpose(ps[3][:, d * HD:(d + 1) * HD], fin[:, d], C("ident", 0, Q)[:, 0:Q])
                mm.then_inc(S("fin_T"), 1)
                pe.wait_ge(S("y_read"), p + 2)
                small(4, P, C("blk"), t0[:], "mean_in")
                pe.wait_ge(S("yc_sq"), p + 1)
                small(5, P, C("blk"), ex[:, 0], "var_in")

            pe.wait_ge(S("rkv_loaded"), 48)
            project(0, 6, "r_proj")
            project(1, 7, "k_proj")
            pe.wait_ge(S("raw_in"), 1)
            project(2, 6, "v_proj")
            with pe.Fori(0, PAIRS - 1) as p:
                body(p, True)
            body(PAIRS - 1, False)

        @block.scalar
        def _(act):
            def raw_in(p, j):
                act.wait_ge(S(("r_proj", "k_proj", "v_proj")[j]), p + 1)
                act.wait_ge(S("shifted"), 3 * p)
                b = ps[(6, 7, 6)[j]]
                nc.scalar.copy(raw[:, j, 1:129], b[:, 0:LC])
                nc.scalar.copy(raw[:, j, 130:386], b[:, LC:T]).then_inc(S("raw_in"), 1)

            def body(p, more):
                act.wait_ge(S("pair_done"), p + 1)
                act.wait_ge(S("lora_up"), p + 1)
                nc.scalar.copy(g[:], ps[5][:, 0:T]).then_inc(S("g_out"), 1)
                nc.scalar.activation(sg[:, 0], ps[0][:, 0:T], ACT.Sigmoid, bias=par[:, bass.ds(p + W0, 1)])
                nc.scalar.activation(sg[:, 1], ps[1][:, 0:T], ACT.Sigmoid, bias=par[:, bass.ds(p + (W0 + 8), 1)])
                nc.scalar.activation(a[:], ps[2][:, 0:T], ACT.Sigmoid, bias=par[:, bass.ds(p + A0, 1)]).then_inc(S("sig_out"), 1)
                act.wait_ge(S("kk_raw"), p + 1)
                nc.scalar.activation(t0[:], kk[:], ACT.Square).then_inc(S("kk_sq"), 1)
                act.wait_ge(S("kk_sum"), p + 1)
                nc.scalar.sqrt(t0[:], ps[3][:, 0:T]).then_inc(S("kk_root"), 1)
                for d in range(2):
                    act.wait_ge(S("cum_done"), 2 * p + d + 1)
                    nc.scalar.activation(ex[:, 0], ex[:, 1], ACT.Exp, scale=-DECAY)
                    nc.scalar.activation(ex[:, 2], ex[:, 2], ACT.Exp, scale=-DECAY).then_inc(S("ex_some"), 1)
                    act.wait_ge(S("ex_some"), 2 * p + d + 1)
                    nc.scalar.activation(ex[:, 1], ex[:, 1], ACT.Exp, scale=DECAY).then_inc(S("ex_ready"), 1)
                act.wait_ge(S("s0_in"), p + 1)
                for d in range(2):
                    nc.scalar.copy(VS[d][Q:P, 0:4].rearrange("p c h v -> p (c h v)"), ps[5][Q:P, :])
                    nc.scalar.copy(VS[d][Q:P, 4:6].rearrange("p c h v -> p (c h v)"), ps[3][Q:P, 0:2 * P])
                    ins = nc.scalar.copy(VS[d][0:Q, SEQ[d][1][0]].rearrange("p h v -> p (h v)"), ps[3][0:Q, (2 + d) * P:(3 + d) * P])
                ins.then_inc(S("VS_ready"), 1)
                act.wait_ge(S("wls_in"), p + 1)
                nc.scalar.copy(wls[:].rearrange("p h c -> p (h c)"), ps[4][0:Q, 0:4 * NCH]).then_inc(S("wls_out"), 1)
                if more:
                    raw_in(p + 1, 0)
                    raw_in(p + 1, 1)
                for n in range(1, 6):
                    for d in range(2):
                        act.wait_ge(S(f"P1_in{d}"), 5 * p + n + 1)
                        nc.scalar.copy(P1[d], c6(ps[3 * d][:, 0:T])).then_inc(S(f"P1_out{d}"), 1)
                    if n == 1 and more:
                        raw_in(p + 1, 2)
                for d in range(2):
                    act.wait_ge(S(f"PU_in{d}"), p + 1)
                    nc.scalar.mul(PU[d][:, 0:4].rearrange("p c q -> p (c q)"), ps[3 * d][:, :], -1.0)
                    nc.scalar.mul(PU[d][:, 4:6].rearrange("p c q -> p (c q)"), ps[3 * d + 1][:, 0:2 * P], -1.0).then_inc(S(f"PU_out{d}"), 1)
                act.wait_ge(S("fin_T"), p + 1)
                act.wait_ge(S("fo_out"), 32 * p + 1)
                nc.scalar.copy(fo[:].rearrange("p d k -> p (d k)"), ps[3][:, 0:2 * HD]).then_inc(S("fo_ready"), 1)
                act.wait_ge(S("yc"), p + 1)
                nc.scalar.activation(ex[:, 0], t0[:], ACT.Square).then_inc(S("yc_sq"), 1)
                act.wait_ge(S("var_read"), p + 2)
                nc.scalar.sqrt(ex[:, 1], ex[:, 1]).then_inc(S("var_root"), 1)

            act.wait_ge(S("rwkv_fixed"), 1)
            for j in range(3):
                raw_in(0, j)
            with act.Fori(0, PAIRS - 1) as p:
                body(p, True)
            body(PAIRS - 1, False)

        STEPS = 6 + 2 + 3 + 1 + 2 + 4 + 4

        @block.vector
        def _(dve):
            V = nc.vector

            def body(p):
                link = Link(dve, S("rwkv_dve"), p * STEPS + 3)

                def col(at):
                    return par[:, bass.ds(p + at, 1)]

                dve.wait_ge(S("raw_in"), 3 * p + 3)
                for j, out in enumerate((r[:], k[:], v[:, Q:Q + T])):
                    link(V.tensor_tensor(sh[:], raw[:, j, 0:T + 1], raw[:, j, 2:T + 3], ALU.add))
                    link(V.tensor_scalar(sh[:], sh[:], mu[:, 1, bass.ds(p + 8 * j, 1)], None, ALU.mult))
                    for c0, c1, skip in ((0, LC, 0), (LC, T, 1)):
                        ins = V.scalar_tensor_tensor(out[:, c0:c1], raw[:, j, c0 + 1 + skip:c1 + 1 + skip], mu[:, 0, bass.ds(p + 8 * j, 1)],
                                                     sh[:, c0 + skip:c1 + skip], ALU.mult, ALU.add)
                    ins.then_inc(S("shifted"), 1)
                    dve.wait_ge(S("shifted"), 3 * p + j + 1)
                V.tensor_scalar(kk[:], k[:], col(K_K), None, ALU.mult).then_inc(S("kk_raw"), 1)
                dve.wait_ge(S("sig_out"), p + 1)
                V.tensor_copy(bonus[:, 0:1], k[:, 0:1]).then_inc(S("v_ready"), 1)
                dve.wait_ge(S("v_ready"), p + 1)
                link(V.tensor_scalar(bonus[:], a[:], col(K_A), omk[:, bass.ds(p, 1)], ALU.mult, ALU.add))
                link(V.tensor_tensor(k[:], k[:], bonus[:], ALU.mult))
                dve.wait_ge(S("kk_root"), p + 1)
                link(V.tensor_scalar(t0[:], t0[:], 1e-12, None, ALU.max))
                link(V.reciprocal(t0[:], t0[:]))
                link(V.tensor_tensor(kk[:], kk[:], t0[:], ALU.mult))
                V.scalar_tensor_tensor(t0[:], r[:], col(R_K), k[:], ALU.mult, ALU.mult).then_inc(S("bonus_mul"), 1)
                link(V.tensor_tensor(ka[:], kk[:], a[:], ALU.mult))
                dve.wait_ge(S("bonus_sum"), p + 1)
                V.tensor_tensor(bonus[:], ps[4][:, 0:T], v[:, Q:Q + T], ALU.mult).then_inc(S("bonus_ready"), 1)
                for d in range(2):
                    back = slice(None, None, -1) if d else slice(None)
                    link(V.tensor_tensor_scan(ex[:, 1][:, back], reset[:], sg[:, d][:, back], 0.0, ALU.mult, ALU.add))
                    V.tensor_tensor(ex[:, 2], ex[:, 1], sg[:, d], ALU.subtract).then_inc(S("cum_done"), 1)
                    dve.wait_ge(S("ex_ready"), 2 * p + d + 1)
                    end = 0 if d else Q - 1
                    V.tensor_copy(wl[:, d * NCH:(d + 1) * NCH].unsqueeze(2), c6(ex[:, 0])[:, :, end:end + 1]).then_inc(S("wl_ready"), 1)
                    for out, x, y in ((M2[d][:, :, 0], r, 0), (M2[d][:, :, 2], kk, 2), (M1[d][:, :, 1], k, 1), (M1[d][:, :, 2], ka, 1)):
                        V.tensor_tensor(out, c6(x[:]), c6(ex[:, y]), ALU.mult).then_inc(S(f"hats{d}"), 1)
                    dve.wait_ge(S(f"hats{d}"), 4 * p + 4)
                for n, dst, mask in ((1, W1, "e1_"), (2, W2, "e2_")):
                    for d in range(2):
                        dve.wait_ge(S(f"E{n}_in{d}"), p + 1)
                        for b in range(3):
                            V.tensor_tensor(dst[d][:, 2 * b:2 * b + 2].rearrange("p c j q -> p c (j q)"), ps[3 * d + b][:, 0:384].rearrange("p (c q) -> p c q", c=2),
                                            C(mask + str(d)).unsqueeze(1).to_broadcast([P, 2, 3 * Q]), ALU.mult).then_inc(S(f"W{n}_ready{d}"), 1)
                for d in range(2):
                    dve.wait_ge(S(f"W2_ready{d}"), 3 * p + 3)
                    low, high = (("low0", "high0"), ("high0", "low0"))[d]
                    link(V.tensor_tensor(X[d], W1[d][:, :, 2], C(low).unsqueeze(1).to_broadcast([P, NCH, Q]), ALU.mult))
                    link(V.tensor_tensor(XT[d], W2[d][:, :, 2], C(high).unsqueeze(1).to_broadcast([P, NCH, Q]), ALU.mult))
                    i2 = C("i2").unsqueeze(1).to_broadcast([P, NCH, Q])
                    V.tensor_tensor(X[d], i2, X[d], ALU.subtract)
                    V.tensor_tensor(XT[d], i2, XT[d], ALU.subtract).then_inc(S(f"X_ready{d}"), 1)
                for n in range(1, 6):
                    for d in range(2):
                        dve.wait_ge(S(f"D_in{d}"), 5 * p + n)
                        dve.wait_ge(S(f"X_ready{d}"), 5 * p + n)
                        ins = V.tensor_tensor(X[d], X[d], c6(ps[3 * d + 1][:, 0:T]), ALU.subtract)
                        if n < 5:
                            V.tensor_tensor(XT[d], XT[d], c6(ps[3 * d + 2][:, 0:T]), ALU.subtract).then_inc(S(f"X_ready{d}"), 1)
                        else:
                            ins.then_inc(S(f"X_final{d}"), 1)
                for u in range(8):
                    for d in range(2):
                        h, c0, c1 = u // 4, (0, 4)[u // 2 % 2], (4, NCH)[u // 2 % 2]
                        dve.wait_ge(S(f"XX_in{d}"), 8 * p + u + 1)
                        src = ps[3 * d + (2 + u) % 3][:, 0:(c1 - c0) * P].rearrange("p (c q) -> p c q", q=P)
                        dst = XX[d][:, h, c0:c1]
                        if u % 2 == 0:
                            V.tensor_tensor(dst, src, C(f"x_{d}").unsqueeze(1).to_broadcast([P, c1 - c0, P]), ALU.mult).then_inc(S(f"XX_ready{d}"), 1)
                        else:
                            dve.wait_ge(S(f"XX_ready{d}"), 8 * p + u + 1)
                            V.tensor_tensor(dst, dst, src, ALU.add).then_inc(S(f"XX_ready{d}"), 1)
                dve.wait_ge(S("wls_out"), p + 1)
                for n, (rnd, item, d, c, nxt) in enumerate(rounds()):
                    dve.wait_ge(S("state_in"), 10 * p + (4, 8, 10)[rnd])
                    src = ps[rnd % 2][0:Q, item * P:(item + 1) * P].rearrange("p (h v) -> p h v", h=2)
                    dst = (fin[:, d] if nxt is None else VS[d][0:Q, nxt].rearrange("p h v -> p (h v)")).rearrange("p (h v) -> p h v", h=2)
                    V.tensor_tensor(dst, src, wls[:, :, d * NCH + c:d * NCH + c + 1].to_broadcast([Q, 2, HD]), ALU.mult).then_inc(S("state_out"), 1)
                dve.wait_ge(S("y_in_r"), p + 1)
                V.tensor_copy(t0[:], ps[2][:, 0:T]).then_inc(S("y_read"), 1)
                dve.wait_ge(S("y_read"), p + 2)
                dve.wait_ge(S("mean_in"), p + 1)
                V.scalar_tensor_tensor(t0[:], ps[4][:, 0:T], -1.0 / HD, t0[:], ALU.mult, ALU.add).then_inc(S("yc"), 1)
                dve.wait_ge(S("var_in"), p + 1)
                V.tensor_scalar(ex[:, 1], ps[5][:, 0:T], 1.0 / HD, GN_EPS, ALU.mult, ALU.add).then_inc(S("var_read"), 1)
                dve.wait_ge(S("var_root"), p + 1)
                link(V.reciprocal(ex[:, 1], ex[:, 1]))
                link(V.tensor_tensor(t0[:], t0[:], ex[:, 1], ALU.mult))
                link(V.tensor_scalar(t0[:], t0[:], col(LN_G), col(LN_B), ALU.mult, ALU.add))
                link(V.tensor_tensor(t0[:], t0[:], bonus[:], ALU.add))
                V.tensor_tensor(mixed[:, bass.ds(p + PAIRS, 1)].rearrange("p a t -> p (a t)"), t0[:], g[:], ALU.mult).then_inc(S("pair_done"), 1)
                assert link.n == STEPS, link.n

            link = Link(dve, S("rwkv_dve"))
            link(V.tensor_scalar(mu[:, 0], par[:, MU:MU + 24], -1.0, 1.0, ALU.mult, ALU.add))
            link(V.tensor_scalar(mu[:, 1], par[:, MU:MU + 24], 0.5, None, ALU.mult))
            link(V.tensor_scalar(omk[:], par[:, K_A:K_A + PAIRS], -1.0, 1.0, ALU.mult, ALU.add))
            with dve.Fori(0, PAIRS) as p:
                body(p)


def project_out(nc, I, O, table, S, sb, ps, cst, par, modT, gain, xT, C, mixed):
    RING = 4
    w_out = I["w_out"].rearrange("l (k p) n -> p (l k) n", p=P)
    with ExitStack() as st:
        w = sb(st, "w_out_ring", [P, RING, KC, P])
        loaded = [S(f"out_loaded{n}") for n in range(RING)]
        block = st.enter_context(nc.Block())

        @block.gpsimd
        def _(pool):
            ahead(pool, S, "out_added")

        @block.sync
        def _(sp):
            def load(i, n):
                sp.dma_start(w[:, n], w_out[:, :, bass.ds(i * (RING * P) + n * P, P)]).then_inc(loaded[n], 16)

            for n in range(RING):
                load(0, n)
            with sp.Fori(1, KC // RING) as i:
                for n in range(RING):
                    sp.wait_ge(S("out_in"), i * RING + (n - RING + 1))
                    load(i, n)

        @block.tensor
        def _(pe):
            with pe.Fori(0, KC // RING) as i:
                for n in range(RING):
                    pe.wait_ge(loaded[n], (i + 1) * 16)
                    pe.wait_ge(S("out_added"), i * RING + 1)
                    for k in range(KC):
                        mm = pe.matmul(ps[n][:, 0:T], w[:, n, k], mixed[:, k], start=(k == 0), stop=(k == KC - 1))
                    mm.then_inc(S("out_in"), 1)

        @block.vector
        def _(dve):
            with dve.Fori(0, KC // RING) as i:
                for n in range(RING):
                    dve.wait_ge(S("out_in"), i * RING + (n + 1))
                    for a, c0, c1 in ((1, 0, LC), (0, LC, T)):
                        x = xT[:, bass.ds(i * RING + n, 1), c0:c1].rearrange("p a t -> p (a t)")
                        gate = modT[:, bass.ds(i * RING + (2 * KC + n), 1), a]
                        ins = nc.vector.scalar_tensor_tensor(x, ps[n][:, c0:c1], gate, x, ALU.mult, ALU.add)
                    ins.then_inc(S("out_added"), 1)


HALVES = ((0, CAPC, 1, 0), (CAPC, SLOTS, 0, 1), (SLOTS, SLOTS + CAPC, 1, 0), (SLOTS + CAPC, 2 * SLOTS, 0, 1))


def route(nc, I, O, table, S, sb, ps, cst, par, modT, gain, xT, C, picked, rank, aff, gates):
    with ExitStack() as st:
        h2 = sb(st, "h2", [P, KC, T])
        norm(nc, I, O, table, S, sb, ps, cst, par, modT, gain, xT, C, which=1, out=h2)
        rw = sb(st, "rw", [P, KC, N_EXP])
        hhi = sb(st, "hhi", [P, TILES, D], F32R)
        hlo = sb(st, "hlo", [P, TILES, D], F32R)
        ohc = sb(st, "ohc", [P, N_EXP, CAPC], F32R)
        ohs = sb(st, "ohs", [P, 2, N_EXP, CAPS], F32R)
        lg = sb(st, "lg", [N_EXP, T])
        work = sb(st, "work", [N_EXP, 3, T])
        top8 = sb(st, "top8", [N_EXP, 8])
        mx = sb(st, "mx", [P, TILES])
        gcol = sb(st, "gcol", [P, KC, 2 * SLOTS])
        block = st.enter_context(nc.Block())

        @block.sync
        def _(sp):
            sp.dma_start(rw[:], I["router_w"].rearrange("l (k p) n -> p (l k) n", p=P)).then_inc(S("rw_loaded"), 16)

        @block.tensor
        def _(pe):
            pe.wait_ge(S("rw_loaded"), 16)
            for k in range(KC):
                mm = pe.matmul(ps[0][0:N_EXP, 0:T], rw[:, k], h2[:, k], start=(k == 0), stop=(k == KC - 1))
            mm.then_inc(S("logits_in"), 1)
            pe.wait_ge(S("logits"), 1)
            for t in range(TILES):
                mm = pe.transpose(ps[1][:, t * N_EXP:(t + 1) * N_EXP], lg[:, t * P:(t + 1) * P], C("ident", 0, N_EXP)[:, 0:N_EXP])
            mm.then_inc(S("logits_T"), 1)
            for g in range(12):
                t, q = g // 4, g % 4
                if g >= 2:
                    pe.wait_ge(S("h_lo"), g - 1)
                for k in range(4):
                    mm = pe.transpose(ps[4 + g % 2][:, k * P:(k + 1) * P], h2[:, 4 * q + k, t * P:(t + 1) * P], C("ident"))
                mm.then_inc(S("h_T"), 1)
            pe.wait_ge(S("aff"), 1)
            for t in range(TILES):
                mm = pe.transpose(ps[2][0:N_EXP, t * P:(t + 1) * P], aff[:, t], C("ident"))
            mm.then_inc(S("aff_T"), 1)
            pe.wait_ge(S("gcol"), 1)
            pe.wait_ge(S("h_lo"), 12)
            for q in range(4):
                if q >= 2:
                    pe.wait_ge(S("gates"), q - 1)
                for k in range(4):
                    mm = pe.matmul(ps[4 + q % 2][0:2 * SLOTS, k * P:(k + 1) * P], gcol[:, 4 * q + k], C("ident"), start=True, stop=True)
                mm.then_inc(S("gates_in"), 1)
            pe.wait_ge(S("rank_row"), 1)
            for t in range(TILES):
                mm = pe.transpose(ps[3][:, t * N_EXP:(t + 1) * N_EXP], work[:, 2, t * P:(t + 1) * P], C("ident", 0, N_EXP)[:, 0:N_EXP])
            mm.then_inc(S("rank_T"), 1)
            pe.wait_ge(S("onehot"), 1)
            for k in range(KC):
                if k >= 1:
                    pe.wait_ge(S("picked_c"), k)
                for half in (hhi, hlo):
                    mm = pe.matmul(ps[6][:, 0:N_EXP * CAPC], half[:, 0, k * P:(k + 1) * P], ohc[:].rearrange("p e c -> p (e c)"), start=(half is hhi), stop=(half is hlo))
                mm.then_inc(S("pick_c"), 1)
                if k >= 1:
                    pe.wait_ge(S("picked_s"), k)
                for t in range(2):
                    for half in (hhi, hlo):
                        mm = pe.matmul(ps[7][:], half[:, 1 + t, k * P:(k + 1) * P], ohs[:, t].rearrange("p e c -> p (e c)"),
                                       start=(t == 0 and half is hhi), stop=(t == 1 and half is hlo))
                mm.then_inc(S("pick_s"), 1)

        @block.scalar
        def _(act):
            act.wait_ge(S("logits_in"), 1)
            nc.scalar.copy(lg[:], ps[0][0:N_EXP, 0:T]).then_inc(S("logits"), 1)
            act.wait_ge(S("shift_max"), 1)
            nc.scalar.activation(aff[:], aff[:], ACT.Exp).then_inc(S("aff_exp"), 1)
            for g in range(12):
                t, q = g // 4, g % 4
                act.wait_ge(S("h_T"), g + 1)
                nc.scalar.copy(hhi[:, t, q * 512:(q + 1) * 512], ps[4 + g % 2][:]).then_inc(S("h_hi"), 1)
            for q in range(4):
                act.wait_ge(S("gates_in"), q + 1)
                nc.scalar.copy(gates[:, q * 512:(q + 1) * 512], ps[4 + q % 2][0:2 * SLOTS, :]).then_inc(S("gates"), 1)
            for k in range(KC):
                act.wait_ge(S("pick_c"), k + 1)
                nc.scalar.copy(picked[:, k].rearrange("p (e s) -> p e s", s=SLOTS)[:, :, 0:CAPC],
                               ps[6][:, 0:N_EXP * CAPC].rearrange("p (e c) -> p e c", e=N_EXP)).then_inc(S("picked_c"), 1)

        @block.vector
        def _(dve):
            V = nc.vector
            link = Link(dve, S("route_dve"))
            dve.wait_ge(S("logits_T"), 1)
            lt = ps[1][:, 0:TILES * N_EXP].rearrange("p (t e) -> p t e", t=TILES)
            link(V.tensor_reduce(mx[:], lt, AX.X, ALU.max))
            V.tensor_tensor(aff[:], lt, mx[:].unsqueeze(2).to_broadcast([P, TILES, N_EXP]), ALU.subtract).then_inc(S("shift_max"), 1)
            dve.wait_ge(S("aff_exp"), 1)
            link(V.tensor_reduce(mx[:], aff[:], AX.X, ALU.add))
            link(V.reciprocal(mx[:], mx[:]))
            V.tensor_tensor(aff[:], aff[:], mx[:].unsqueeze(2).to_broadcast([P, TILES, N_EXP]), ALU.mult).then_inc(S("aff"), 1)
            for c0, c1, a, _ in HALVES:
                ins = V.tensor_copy(gcol[:, :, c0:c1], modT[:, 5 * KC:6 * KC, a:a + 1].to_broadcast([P, KC, c1 - c0]))
            ins.then_inc(S("gcol"), 1)
            for g in range(12):
                t, q = g // 4, g % 4
                dve.wait_ge(S("h_hi"), g + 1)
                V.tensor_tensor(hlo[:, t, q * 512:(q + 1) * 512], ps[4 + g % 2][:], hhi[:, t, q * 512:(q + 1) * 512].bitcast(F32), ALU.subtract).then_inc(S("h_lo"), 1)
            dve.wait_ge(S("aff_T"), 1)
            link(V.tensor_copy(work[:, 0], ps[2][0:N_EXP, 0:T]))
            for c0, c1, cap in ((0, LC, CAPC), (LC, T, CAPS)):
                for _ in range(cap // 8):
                    link(V.max(top8[:], work[:, 0, c0:c1]))
                    link(V.match_replace(work[:, 0, c0:c1], top8[:], work[:, 0, c0:c1], -1.0))
            link(V.tensor_scalar(work[:, 1], work[:, 0], 0.0, None, ALU.is_lt))
            link(V.memset(work[:, 0], 1.0))
            for c0, c1 in ((0, LC), (LC, T)):
                link(V.tensor_tensor_scan(work[:, 2, c0:c1], work[:, 0, c0:c1], work[:, 1, c0:c1], 0.0, ALU.mult, ALU.add))
            link(V.tensor_tensor(work[:, 2], work[:, 2], work[:, 1], ALU.mult))
            V.tensor_scalar(work[:, 2], work[:, 2], -1.0, None, ALU.add).then_inc(S("rank_row"), 1)
            dve.wait_ge(S("rank_T"), 1)
            link(V.tensor_copy(rank[:].rearrange("p t e -> p (t e)"), ps[3][:, 0:TILES * N_EXP]))
            V.tensor_tensor(ohc[:], rank[:, 0].unsqueeze(2).to_broadcast([P, N_EXP, CAPC]), C("iota")[:, 0:CAPC].unsqueeze(1).to_broadcast([P, N_EXP, CAPC]), ALU.is_equal)
            for t in range(2):
                ins = V.tensor_tensor(ohs[:, t], rank[:, 1 + t].unsqueeze(2).to_broadcast([P, N_EXP, CAPS]), C("iota").unsqueeze(1).to_broadcast([P, N_EXP, CAPS]), ALU.is_equal)
            ins.then_inc(S("onehot"), 1)
            for k in range(KC):
                dve.wait_ge(S("pick_s"), k + 1)
                V.tensor_copy(picked[:, k].rearrange("p (e s) -> p e s", s=SLOTS)[:, :, CAPC:SLOTS],
                              ps[7][:].rearrange("p (e c) -> p e c", e=N_EXP)).then_inc(S("picked_s"), 1)


def experts(nc, I, O, table, S, sb, ps, cst, par, modT, gain, xT, C, picked, rank, aff, gates):
    RING, HL, NS, R2 = 4, 3, 24, 2 * SLOTS
    DOWN = 16
    w_src = [I[n].rearrange("l e (q c p) n -> p (l e q) c n", p=P, c=4) for n in ("exp_w_gate", "exp_w_up", "exp_w_down")]
    with ExitStack() as st:
        raw = sb(st, "w_raw", [P, RING, 4, 512])
        hi = sb(st, "w_hi", [P, HL, 4, 512], F32R)
        lo = sb(st, "w_lo", [P, HL, 4, 512], F32R)
        xs = sb(st, "xs", [P, KC, R2], F32R)
        gu = sb(st, "gu", [R2, 4, 512])
        gs = sb(st, "gs", [P, 4, 4, SLOTS])
        sg = sb(st, "sg_e", [P, 2, 4, SLOTS])
        hid = sb(st, "hid", [P, FF // P, R2], F32R)
        outs = sb(st, "outs", [R2, D])
        pg = sb(st, "pg", [P, TILES, R2])
        G = sb(st, "G", [R2, T])
        loaded = [S(f"exp_loaded{n}") for n in range(RING)]
        block = st.enter_context(nc.Block())

        def turns(eng, body):
            body(0)
            body(1)
            with eng.Fori(2, N_EXP - 1) as i:
                body(i)
            body(N_EXP - 1)
            body(N_EXP)

        def parts(i):
            if not isinstance(i, int):
                return True, True, True, range(NS)
            up, down = i < N_EXP, i >= 1
            return up, down, i >= 2, range(0 if up else DOWN, NS if down else DOWN)

        def before(i, n):
            if isinstance(i, int) and i == 0:
                return 0, n
            if isinstance(i, int) and i == N_EXP:
                return i - 1, n
            return i - 1, DOWN + n

        def count(i, n):
            t, r = before(i, n)
            return t * NS + r

        @block.sync
        def _(sp):
            def body(i):
                for n in parts(i)[3]:
                    t, r = before(i, n)
                    j, e, per, q, c0 = (n // 8, i, 4, n % 4, n % 8 // 4 * 512) if n < DOWN else (2, i - 1, 2, n % 2, (n - DOWN) // 2 * 512)
                    if not (isinstance(i, int) and i == 0 and n < RING):
                        sp.wait_ge(S("exp_lo"), t * NS + (r - RING + 1))
                        sp.sem_inc(S("sp_held"), 1)
                    src = w_src[j][:, bass.ds(e * per + q, 1), :, c0:c0 + 512].rearrange("p a c n -> p (a c) n")
                    sp.dma_start(raw[:, r % RING], src).then_inc(loaded[r % RING], 16)

            turns(sp, body)

        @block.tensor
        def _(pe):
            def slot(i, n):
                t, r = before(i, n)
                pe.wait_ge(S("exp_lo"), t * NS + (r + 1))
                bank, first, last = (n // 4, n % 4 == 0, n % 4 == 3) if n < DOWN else (4 + (n - DOWN) // 2 % 2, n % 2 == 0, n % 2 == 1)
                for c in range(4):
                    lhs = xs[:, 4 * (n % 4) + c] if n < DOWN else hid[:, 4 * (n % 2) + c]
                    for half in (hi, lo):
                        mm = pe.matmul(ps[bank][0:R2, :], lhs, half[:, r % HL, c], start=(first and c == 0 and half is hi), stop=(last and c == 3 and half is lo))
                mm.then_inc(S("exp_used"), 1)

            def turn_back(i, j):
                pe.wait_ge(S("gu_out"), i * 4 + (j + 1))
                for f in range(4):
                    mm = pe.transpose(ps[j][:, f * R2:(f + 1) * R2], gu[:, j, f * P:(f + 1) * P], C("ident", 0, R2)[:, 0:R2])
                mm.then_inc(S("gu_T"), 1)

            def add_out(i, k):
                pe.wait_ge(S("outs"), i * 4 + (k // 4 - 7))
                if k == 0:
                    pe.wait_ge(S("G"), i - 1)
                if k >= 2:
                    pe.wait_ge(S("added"), i * KC + (k - 1 - 2 * KC))
                pe.matmul(ps[6 + k % 2][:, 0:T], outs[:, k * P:(k + 1) * P], G[:], start=True, stop=True).then_inc(S("add_in"), 1)

            def body(i):
                up, down, add, _ = parts(i)
                if up:
                    pe.wait_ge(S("xs_lo"), i + 1)
                for n in range(DOWN):
                    if up:
                        if n % 4 == 0 and not (isinstance(i, int) and i == 0):
                            pe.wait_ge(S("gs"), i * 4 + (n // 4 - 3))
                        slot(i, n)
                        if n in (6, 10, 14):
                            turn_back(i, (n - 6) // 4)
                        if n == DOWN - 1 and not down:
                            turn_back(i, 3)
                    if add:
                        add_out(i, n)
                for n in range(DOWN, NS):
                    if down:
                        if n == DOWN:
                            pe.wait_ge(S("hid"), i)
                        if n % 2 == 0 and not (isinstance(i, int) and i == 1 and n < DOWN + 4):
                            pe.wait_ge(S("outs"), i * 4 + ((n - DOWN) // 2 - 5))
                        slot(i, n)
                    if n == 18 and up and down:
                        turn_back(i, 3)
                    if n == 20 and down:
                        pe.wait_ge(S("pg"), i)
                        if add:
                            pe.wait_ge(S("added"), i * KC - KC)
                        for t in range(TILES):
                            mm = pe.transpose(ps[6][0:R2, t * P:(t + 1) * P], pg[:, t], C("ident"))
                        mm.then_inc(S("pg_T"), 1)

            turns(pe, body)
            for k in range(KC):
                add_out(N_EXP + 1, k)

        @block.scalar
        def _(act):
            def xs_hi(e):
                nc.scalar.copy(xs[:, :, 0:SLOTS], picked[:, :, bass.ds(e * SLOTS, SLOTS)]).then_inc(S("xs_hi"), 1)

            def gu_out(i, j):
                act.wait_ge(S("exp_used"), count(i, 4 * j + 3) + 1)
                nc.scalar.copy(gu[:, j], ps[j][0:R2, :]).then_inc(S("gu_out"), 1)

            def gate(i):
                act.wait_ge(S("gs"), i * 4)
                nc.scalar.activation(sg[:], gs[:, 0:2], ACT.Sigmoid).then_inc(S("hid_sig"), 1)

            def body(i):
                up, down, add, slots = parts(i)
                more = up and not (isinstance(i, int) and i == N_EXP - 1)
                if not up:
                    gate(i)
                for n in slots:
                    t, r = before(i, n)
                    act.wait_ge(loaded[r % RING], (t * (NS // RING) + (r // RING + 1)) * 16)
                    if not (isinstance(i, int) and i == 0 and n < HL):
                        act.wait_ge(S("exp_used"), t * NS + (r - HL + 1))
                    nc.scalar.copy(hi[:, r % HL], raw[:, r % RING]).then_inc(S("exp_hi"), 1)
                    if n == 2 and down:
                        gate(i)
                    if n in (5, 9, 13) or (up and n == 17):
                        gu_out(i, (n - 5) // 4)
                    if n == 18 and more:
                        act.wait_ge(S("exp_used"), count(i, DOWN - 1) + 1)
                        xs_hi(i + 1)
                    if n == 22:
                        act.wait_ge(S("pg_T"), i)
                        nc.scalar.copy(G[:], ps[6][0:R2, 0:T]).then_inc(S("G"), 1)
                if not down:
                    gu_out(i, 3)
                    xs_hi(i + 1)

            xs_hi(0)
            turns(act, body)

        @block.vector
        def _(dve):
            V = nc.vector

            def added(i, k):
                dve.wait_ge(S("add_in"), i * KC + (k + 1 - 2 * KC))
                V.tensor_tensor(xT[:, k], xT[:, k], ps[6 + k % 2][:, 0:T], ALU.add).then_inc(S("added"), 1)

            def out(i, j):
                dve.wait_ge(S("exp_used"), count(i, DOWN + 2 * j + 1) + 1)
                V.tensor_tensor(outs[:, j * 512:(j + 1) * 512], ps[4 + j % 2][0:R2, :], gates[:, j * 512:(j + 1) * 512], ALU.mult).then_inc(S("outs"), 1)

            def halves(i, j):
                dve.wait_ge(S("gu_T"), i * 4 + (j + 1))
                src = ps[j][:, 0:4 * R2].rearrange("p (f r) -> p f r", f=4)
                V.tensor_copy(gs[:, j], src[:, :, 0:SLOTS]).then_inc(S("gs_half"), 1)
                dve.wait_ge(S("gs_half"), i * 4 + (j + 1))
                V.tensor_tensor(gs[:, j], gs[:, j], src[:, :, SLOTS:R2], ALU.add).then_inc(S("gs"), 1)

            def xs_lo(e):
                dve.wait_ge(S("xs_hi"), e + 1)
                V.tensor_tensor(xs[:, :, SLOTS:R2], picked[:, :, bass.ds(e * SLOTS, SLOTS)], xs[:, :, 0:SLOTS].bitcast(F32), ALU.subtract).then_inc(S("xs_lo"), 1)

            def hidden(i):
                link = Link(dve, S("exp_dve"), (i - 1) * 3)
                dve.wait_ge(S("hid_sig"), i)
                if not (isinstance(i, int) and i == 1):
                    dve.wait_ge(S("exp_used"), count(i - 1, NS - 1) + 1)
                link(V.tensor_tensor(sg[:], sg[:], gs[:, 0:2], ALU.mult))
                link(V.tensor_tensor(sg[:], sg[:], gs[:, 2:4], ALU.mult))
                s8 = sg[:].rearrange("p j f s -> p (j f) s")
                link(V.tensor_copy(hid[:, :, 0:SLOTS], s8))
                V.tensor_tensor(hid[:, :, SLOTS:R2], s8, hid[:, :, 0:SLOTS].bitcast(F32), ALU.subtract).then_inc(S("hid"), 1)

            def weights(i):
                if not (isinstance(i, int) and i == 1):
                    dve.wait_ge(S("pg_T"), i - 1)
                for c0, c1, a, late in HALVES:
                    for t in ((1, 2) if late else (0,)):
                        ins = V.tensor_scalar(pg[:, t, c0:c1], C("iota")[:, 0:c1 - c0], rank[:, t, bass.ds(i - 1, 1)], aff[:, t, bass.ds(i - 1, 1)], ALU.is_equal, ALU.mult)
                ins.then_inc(S("pg"), 1)

            def body(i):
                up, down, add, slots = parts(i)
                for n in range(NS):
                    if n in slots:
                        t, r = before(i, n)
                        dve.wait_ge(S("exp_hi"), t * NS + (r + 1))
                        V.tensor_tensor(lo[:, r % HL], raw[:, r % RING], hi[:, r % HL].bitcast(F32), ALU.subtract).then_inc(S("exp_lo"), 1)
                    if n == 1 and add:
                        out(i - 1, 3)
                    if n == 3 and down:
                        hidden(i)
                    if 2 <= n < KC + 2 and add:
                        added(i, n - 2)
                    if n == 5 and down:
                        weights(i)
                    if up and (n in (8, 12) or (down and n in (16, 20))):
                        halves(i, (n - 8) // 4)
                    if n == 19 and up and down and not (isinstance(i, int) and i == N_EXP - 1):
                        xs_lo(i + 1)
                    if down and n in (19, 21, 23):
                        out(i, (n - 19) // 2)
                if not down:
                    halves(i, 2)
                    halves(i, 3)
                    xs_lo(i + 1)

            V.memset(pg[:], 0.0).then_inc(S("pg_zero"), 1)
            dve.wait_ge(S("pg_zero"), 1)
            xs_lo(0)
            turns(dve, body)
            out(N_EXP, 3)
            for k in range(KC):
                added(N_EXP + 1, k)


def finish(nc, I, O, table, S, sb, ps, cst, par, modT, gain, xT, C):
    with ExitStack() as st:
        sq = sb(st, "f_sq", [P, 2, T])
        rstd = sb(st, "f_rstd", [P, T])
        ytok = sb(st, "ytok", [P, TILES, D])
        block = st.enter_context(nc.Block())

        @block.scalar
        def _(act):
            for k in range(KC):
                if k >= 2:
                    act.wait_ge(S("f_sum"), k - 1)
                nc.scalar.activation(sq[:, k % 2], xT[:, k], ACT.Square).then_inc(S("f_sq"), 1)
            act.wait_ge(S("f_mean"), 1)
            nc.scalar.sqrt(rstd[:], rstd[:]).then_inc(S("f_root"), 1)
            for g in range(1, 12, 2):
                act.wait_ge(S("f_T"), g + 1)
                nc.scalar.copy(ytok[:, g % 3, (g // 3) * 512:(g // 3 + 1) * 512], ps[1 + g % 4][:]).then_inc(S("f_out1"), 1)

        @block.tensor
        def _(pe):
            for k in range(KC):
                pe.wait_ge(S("f_sq"), k + 1)
                pe.matmul(ps[0][:, 0:T], C("ones"), sq[:, k % 2], start=(k == 0), stop=(k == KC - 1)).then_inc(S("f_sum"), 1)
            for g in range(12):
                t, q = g % 3, g // 3
                pe.wait_ge(S("f_y"), 4 * q + 4)
                if g >= 4:
                    pe.wait_ge(S(f"f_out{g % 2}"), (g - 4) // 2 + 1)
                for k in range(4):
                    mm = pe.transpose(ps[1 + g % 4][:, k * P:(k + 1) * P], xT[:, 4 * q + k, t * P:(t + 1) * P], C("ident"))
                mm.then_inc(S("f_T"), 1)

        @block.vector
        def _(dve):
            dve.wait_ge(S("f_sum"), KC)
            nc.vector.tensor_scalar(rstd[:], ps[0][:, 0:T], 1.0 / D, EPS, ALU.mult, ALU.add).then_inc(S("f_mean"), 1)
            dve.wait_ge(S("f_root"), 1)
            nc.vector.reciprocal(rstd[:], rstd[:]).then_inc(S("f_rstd"), 1)
            dve.wait_ge(S("f_rstd"), 1)
            for k in range(KC):
                nc.vector.scalar_tensor_tensor(xT[:, k], xT[:, k], par[:, G_FIN + k:G_FIN + k + 1], rstd[:], ALU.mult, ALU.mult).then_inc(S("f_y"), 1)
            for g in range(0, 12, 2):
                dve.wait_ge(S("f_T"), g + 1)
                nc.vector.tensor_copy(ytok[:, g % 3, (g // 3) * 512:(g // 3 + 1) * 512], ps[1 + g % 4][:]).then_inc(S("f_out0"), 1)

        @block.sync
        def _(sp):
            for q in range(4):
                n = 3 * q + 3
                sp.wait_ge(S("f_out0"), (n + 1) // 2)
                sp.wait_ge(S("f_out1"), n // 2)
                for t in range(TILES):
                    dst = O["y_prompt"][0] if t == 0 else O["y_sample"][0, (t - 1) * P:t * P, :]
                    sp.dma_start(dst[:, q * 512:(q + 1) * 512], ytok[:, t, q * 512:(q + 1) * 512]).then_inc(S("y_stored"), 16)
            sp.wait_ge(S("y_stored"), 16 * 12)


INS = ["x_prompt", "x_sample", "state_ssd_fwd", "state_ssd_bwd", "state_rwkv_fwd", "state_rwkv_bwd", "c", "c_ctx",
       "w_ada", "b_ada", "norm_mix_g", "norm_ffn_g", "w_in", "w_out", "ssd_conv_w", "ssd_conv_b", "ssd_A_log",
       "ssd_dt_bias", "ssd_D", "ssd_norm_g", "rwkv_mu", "rwkv_w0", "rwkv_w_up", "rwkv_a0", "rwkv_a_up", "rwkv_g_up",
       "rwkv_k_k", "rwkv_k_a", "rwkv_r_k", "rwkv_ln_g", "rwkv_ln_b", "router_w", "exp_w_gate", "exp_w_up",
       "exp_w_down", "final_norm_g"]
OUTS = [("y_prompt", (1, LC, D)), ("y_sample", (1, LS, D)),
        ("ssd_fwd", (1, 1, HEADS, HD, P)), ("ssd_bwd", (1, 1, HEADS, HD, P)),
        ("rwkv_fwd", (1, 1, HEADS, HD, HD)), ("rwkv_bwd", (1, 1, HEADS, HD, HD))]


def kernel(**inputs):
    import concourse.bacc as bacc
    from concourse.bass_utils import run_bass_kernel_spmd

    nc = bacc.Bacc("TRN2", target_bir_lowering=False, num_devices=1)
    table = constants()
    arrays = {"table": table}
    I, O = {}, {}
    for name in INS:
        arrays[name] = np.ascontiguousarray(inputs[name])
        I[name] = nc.dram_tensor(name, arrays[name].shape, F32, kind="ExternalInput").ap()
    for name, shape in OUTS:
        O[name] = nc.dram_tensor("out_" + name, shape, F32, kind="ExternalOutput").ap()
    table_ap = nc.dram_tensor("table", table.shape, F32, kind="ExternalInput").ap()
    program(nc, I, O, table_ap)
    got = run_bass_kernel_spmd(nc, [arrays], core_ids=[0]).results[0]
    return tuple(got["out_" + name] for name, _ in OUTS)
```

```python
import math
from contextlib import ExitStack

import numpy as np

import concourse.bass as bass
from concourse import mybir

F32 = mybir.dt.float32
F32R = mybir.dt.float32r
ALU = mybir.AluOpType
ACT = mybir.ActivationFunctionType
AX = mybir.AxisListType

P = 128
D = 2048
KC = D // P
LC, LS = 128, 256
T = LC + LS
TILES = T // P
GRID_W = 64
HEADS = 16
HD = 64
PAIRS = HEADS // 2
N_SSD_IN = 2592
N_EXP = 16
FF = 1024
CAPC, CAPS = 2 * LC // N_EXP, 2 * LS // N_EXP
SLOTS = CAPC + CAPS
EPS, GN_EPS = 1e-6, 64e-5
DECAY = 0.606531
Q = 64
NCH = T // Q

COND, CCTX = 96, 112
G_MIX, G_FFN, G_FIN, CONV_W, CONV_B, G_SSD = 128, 144, 160, 176, 236, 248
W0, A0, K_K, K_A, R_K, LN_G, LN_B, MU = 256, 272, 280, 288, 296, 304, 312, 320
NPAR = 348
MU_WD, MU_GD0, MU_AD, MU_GD1 = 24, 25, 26, 27

CONST = {}


def constants():
    r = np.arange(P)
    pieces = {
        "ident": np.eye(P),
        "ones": np.ones((P, P)),
        "blk": (r[:, None] // HD == r[None, :] // HD),
        "i2": np.concatenate([np.eye(HD)] * 2),
        "neg0": np.where(r[None, :] >= r[:, None], 0.0, -1e30),
        "neg1": np.where(r[None, :] <= r[:, None], 0.0, -1e30),
        "iota": np.tile(np.arange(CAPS), (P, 1)),
    }
    u, s = (r % Q)[:, None], np.arange(Q)[None, :]
    one = np.ones((P, Q))
    for d in range(2):
        before = (s < u) if d == 0 else (s > u)
        after = (s > u) if d == 0 else (s < u)
        upto = after | (s == u)
        pieces[f"e1_{d}"] = np.concatenate([one, before, before], 1)
        pieces[f"e2_{d}"] = np.concatenate([upto, one, after], 1)
        top = (r < Q)[:, None]
        pieces[f"x_{d}"] = np.concatenate([top | upto, one], 1)
    for n in range(6):
        b = 1 << n
        low = (u // (2 * b) == s // (2 * b)) & ((u // b) % 2 == 1) & ((s // b) % 2 == 0)
        high = (u // (2 * b) == s // (2 * b)) & ((u // b) % 2 == 0) & ((s // b) % 2 == 1)
        pieces[f"low{n}"] = low
        pieces[f"high{n}"] = high
    pieces["fold"] = np.zeros((P, 2))
    pieces["fold"][0:4] = [[1, 0], [0, 1], [1, 0], [0, 1]]
    f = np.float32
    quarter = D // 4
    freqs = np.exp(np.arange(quarter, dtype=f) * f(-math.log(10000.0) / quarter)).astype(f)
    for name, n in (("row", LS // GRID_W), ("col", GRID_W)):
        ang = (np.arange(n, dtype=f)[:, None] * freqs[None, :]).astype(f)
        table = np.concatenate([np.sin(ang), np.cos(ang)], -1).astype(f)
        pieces[name] = table.T.reshape(KC // 2, P, n).transpose(1, 0, 2).reshape(P, -1)
    at = 0
    for name, a in pieces.items():
        CONST[name] = (at, at + a.shape[1])
        at += a.shape[1]
    return np.ascontiguousarray(np.concatenate([np.asarray(a, f) for a in pieces.values()], 1))


def ahead(eng, S, *names):
    for name in names:
        eng.sem_inc(S(name), 1)


class Link:

    def __init__(self, eng, sem, base=0):
        self.eng, self.sem, self.base, self.n = eng, sem, base, 0

    def __call__(self, ins):
        ins.then_inc(self.sem, 1)
        self.n += 1
        self.eng.wait_ge(self.sem, self.base + self.n)


def program(nc, I, O, table, stop="all"):
    ctx = ExitStack()
    sem = {}

    def S(name):
        if name not in sem:
            sem[name] = nc.alloc_semaphore(name)
        return sem[name]

    def reuse_semaphores():
        nc.clear_and_free_semaphores(list(sem.values()))
        sem.clear()
        nc.all_engine_barrier()

    def sb(stack, name, shape, dt=F32):
        return stack.enter_context(nc.sbuf_tensor(name, shape, dt))

    with ctx:
        ps = [ctx.enter_context(nc.psum_tensor(f"bank{n}", [P, 512], F32)) for n in range(8)]
        cst = sb(ctx, "cst", [P, CONST["row"][0]])
        par = sb(ctx, "par", [P, 352])
        modT = sb(ctx, "modT", [P, 96, 2])
        gain = sb(ctx, "gain", [P, 2, KC, 2])
        xT = sb(ctx, "xT", [P, KC, T])

        def C(name, p0=0, p1=P):
            a, b = CONST[name]
            return cst[p0:p1, a:b]

        env = dict(nc=nc, I=I, O=O, table=table, S=S, sb=sb, ps=ps, cst=cst, par=par, modT=modT, gain=gain, xT=xT, C=C)
        setup(**env)
        if stop == "ada":
            return
        with ExitStack() as mix:
            mixed = sb(mix, "mixed", [P, KC, T])
            with ExitStack() as proj:
                hT = sb(proj, "hT", [P, KC, T])
                lora = sb(proj, "lora", [P, 4, T])
                ssd(**env, hT=hT, mixed=mixed, lora=lora)
                if stop == "ssd":
                    return
                reuse_semaphores()
                rwkv(**env, hT=hT, mixed=mixed, lora=lora)
            reuse_semaphores()
            if stop == "rwkv":
                return
            project_out(**env, mixed=mixed)
        if stop == "mix":
            return
        with ExitStack() as ffn:
            picked = sb(ffn, "picked", [P, KC, N_EXP * SLOTS])
            rank = sb(ffn, "rank", [P, TILES, N_EXP])
            aff = sb(ffn, "aff", [P, TILES, N_EXP])
            gates = sb(ffn, "gates", [2 * SLOTS, D])
            route(**env, picked=picked, rank=rank, aff=aff, gates=gates)
            reuse_semaphores()
            experts(**env, picked=picked, rank=rank, aff=aff, gates=gates)
        finish(**env)


def setup(nc, I, O, table, S, sb, ps, cst, par, modT, gain, xT, C):
    RING, HL = 8, 4
    with ExitStack() as st:
        grid = sb(st, "grid", [P, table.shape[1] - CONST["row"][0]])
        rows = sb(st, "rows", [P, 3, P])
        xtok = sb(st, "xtok", [P, TILES, D])
        cs = sb(st, "cs", [P, 2, 2, KC])
        cond = sb(st, "cond", [P, KC, 4], F32R)
        raw = sb(st, "raw", [P, RING, 4, 512])
        hi = sb(st, "hi", [P, HL, 4, 512], F32R)
        lo = sb(st, "lo", [P, HL, 4, 512], F32R)
        arow = sb(st, "arow", [4, 2, 512])
        loaded = [S(f"ada_loaded{n}") for n in range(RING)]
        w_ada = I["w_ada"].rearrange("l (q c p) n -> p (l q) c n", p=P, c=4)
        block = st.enter_context(nc.Block())

        @block.sync
        def _(sp):
            def rows_in(t, r0, src):
                n, m = src.shape
                sp.dma_start(rows[r0:r0 + n, t, 0:m], src).then_inc(S("rows_in"), 16)

            at = CONST["row"][0]
            sp.dma_start(cst[:], table[:, 0:at]).then_inc(S("cst_in"), 16)
            sp.dma_start(grid[:], table[:, at:]).then_inc(S("grid_in"), 16)
            rows_in(0, 0, I["b_ada"].rearrange("l (r c) -> (l r) c", c=P))
            rows_in(0, COND, I["c"].rearrange("l (r c) -> (l r) c", c=P))
            rows_in(0, CCTX, I["c_ctx"].rearrange("(r c) -> r c", c=P))
            for at, name in ((G_MIX, "norm_mix_g"), (G_FFN, "norm_ffn_g"), (CONV_B, "ssd_conv_b"), (G_SSD, "ssd_norm_g")):
                rows_in(1, at - 128, I[name].rearrange("l (r c) -> (l r) c", c=P))
            rows_in(1, G_FIN - 128, I["final_norm_g"].rearrange("(r c) -> r c", c=P))
            rows_in(1, CONV_W - 128, I["ssd_conv_w"].rearrange("l t (r c) -> (l t r) c", c=P))
            rows_in(2, W0 - 256, I["rwkv_w0"].rearrange("l d (r c) -> (l d r) c", c=P))
            for at, name in ((A0, "rwkv_a0"), (K_K, "rwkv_k_k"), (K_A, "rwkv_k_a"), (LN_G, "rwkv_ln_g"), (LN_B, "rwkv_ln_b")):
                rows_in(2, at - 256, I[name].rearrange("l (r c) -> (l r) c", c=P))
            rows_in(2, R_K - 256, I["rwkv_r_k"].rearrange("l (r h) c -> (l r) (h c)", h=2))
            mu = I["rwkv_mu"]
            sp.wait_ge(S("rows_zero"), 1)
            rows_in(2, MU - 256, mu[:, 0:25 * P].rearrange("l (r c) -> (l r) c", c=P))
            rows_in(2, MU - 256 + MU_GD0, mu[:, 3264:3392])
            rows_in(2, MU - 256 + MU_AD, mu[:, 3200:3264])
            rows_in(2, MU - 256 + MU_GD1, mu[:, 3392:3424])
            sp.dma_start(xtok[:, 0, :], I["x_prompt"][0]).then_inc(S("x_in"), 16)
            for t in range(2):
                sp.dma_start(xtok[:, 1 + t, :], I["x_sample"][0, t * P:(t + 1) * P, :]).then_inc(S("x_in"), 16)

            def load(i, n):
                sp.dma_start(raw[:, n], w_ada[:, n % 4, :, bass.ds(i * 1024 + (n // 4) * 512, 512)]).then_inc(loaded[n], 16)

            for n in range(RING):
                load(0, n)
            with sp.Fori(1, 12) as i:
                for n in range(RING):
                    sp.wait_ge(S("ada_lo"), i * RING + n - RING + 1)
                    load(i, n)

        NROWS = 20

        @block.gpsimd
        def _(pool):
            pool.sem_inc(S("ada_used"), HL)
            nc.gpsimd.memset(rows[64:96, 2, :], 0.0).then_inc(S("rows_zero"), 1)

        @block.tensor
        def _(pe):
            pe.wait_ge(S("cst_in"), 16)
            pe.wait_ge(S("rows_in"), 16 * NROWS)
            for t, n in ((0, 128), (1, 128), (2, 92)):
                mm = pe.transpose(ps[0][:, t * P:t * P + n], rows[0:n, t, :], C("ident", 0, n)[:, 0:n])
            mm.then_inc(S("par_T"), 1)
            pe.wait_ge(S("x_in"), 16 * TILES)
            for t in range(TILES):
                for q in range(4):
                    g = 4 * t + q
                    if g >= 2:
                        pe.wait_ge(S("xT_out"), g - 1)
                    for k in range(4):
                        mm = pe.transpose(ps[1 + g % 2][:, k * P:(k + 1) * P], xtok[:, t, (4 * q + k) * P:(4 * q + k + 1) * P], C("ident"))
                    mm.then_inc(S("xT_in"), 1)
            pe.wait_ge(S("cond"), 1)
            def columns(i, g):
                pe.wait_ge(S("ada_row"), 2 * i + g + 1)
                for j in range(4):
                    mm = pe.matmul(ps[5][:, bass.ds(i * 16 + (4 * g + j) * 2, 2)], arow[:, g, j * P:(j + 1) * P], C("fold", 0, 4), start=True, stop=True)
                mm.then_inc(S("ada_col"), 1)

            def body(i, prev):
                for n in range(RING):
                    g, q = n // 4, n % 4
                    pe.wait_ge(S("ada_lo"), i * RING + n + 1)
                    for c in range(4):
                        for half in (hi, lo):
                            mm = pe.matmul(ps[3 + g][0:4, :], cond[:, 4 * q + c, :], half[:, n % HL, c, :],
                                           start=(q == 0 and c == 0 and half is hi), stop=(q == 3 and c == 3 and half is lo))
                    mm.then_inc(S("ada_used"), 1)
                    if n == 2 and prev:
                        columns(i - 1, 1)
                    if n == 6:
                        columns(i, 0)

            body(0, False)
            with pe.Fori(1, 12) as i:
                body(i, True)
            columns(11, 1)

        @block.scalar
        def _(act):
            act.wait_ge(S("par_done"), 1)
            nc.scalar.activation(cs[:, 1], par[:, COND:COND + 32].rearrange("p (a k) -> p a k", a=2), ACT.Sigmoid).then_inc(S("cond_sig"), 1)
            def row_out(i, g):
                act.wait_ge(S("ada_used"), i * RING + 4 * g + 4 + HL)
                nc.scalar.copy(arow[:, g], ps[3 + g][0:4, :]).then_inc(S("ada_row"), 1)

            def body(i, prev):
                for n in range(RING):
                    act.wait_ge(loaded[n], (i + 1) * 16)
                    act.wait_ge(S("ada_used"), i * RING + n + 1)
                    nc.scalar.copy(hi[:, n % HL], raw[:, n]).then_inc(S("ada_hi"), 1)
                    if n == 1 and prev:
                        row_out(i - 1, 1)
                    if n == 5:
                        row_out(i, 0)

            body(0, False)
            with act.Fori(1, 12) as i:
                body(i, True)
            row_out(11, 1)

        @block.vector
        def _(dve):
            link = Link(dve, S("setup_dve"))
            dve.wait_ge(S("par_T"), 1)
            nc.vector.tensor_copy(par[:, 0:NPAR], ps[0][:, 0:NPAR]).then_inc(S("par_done"), 1)
            dve.wait_ge(S("cond_sig"), 1)
            link(nc.vector.tensor_tensor(cs[:, 0], cs[:, 1], par[:, COND:COND + 32].rearrange("p (a k) -> p a k", a=2), ALU.mult))
            csk = cs[:, 0].rearrange("p a k -> p k a")
            link(nc.vector.tensor_copy(cond[:, :, 0:2], csk))
            nc.vector.tensor_tensor(cond[:, :, 2:4], csk, cond[:, :, 0:2].bitcast(F32), ALU.subtract).then_inc(S("cond"), 1)
            dve.wait_ge(S("grid_in"), 16)
            nrow = CONST["row"][1] - CONST["row"][0]
            for t in range(TILES):
                for q in range(4):
                    g = 4 * t + q
                    dve.wait_ge(S("xT_in"), g + 1)
                    src = ps[1 + g % 2][:].rearrange("p (k r c) -> p k r c", k=4, r=2)
                    dst = xT[:, 4 * q:4 * q + 4, t * P:(t + 1) * P].rearrange("p k (r c) -> p k r c", r=2)
                    if t == 0:
                        ins = nc.vector.tensor_copy(dst, src)
                    elif q < 2:
                        pos = grid[:, 0:nrow].rearrange("p (k r) -> p k r", r=4)[:, 4 * q:4 * q + 4, 2 * (t - 1):2 * t]
                        ins = nc.vector.tensor_tensor(dst, src, pos.unsqueeze(3).to_broadcast([P, 4, 2, 64]), ALU.add)
                    else:
                        pos = grid[:, nrow:].rearrange("p (k c) -> p k c", c=64)[:, 4 * q - 8:4 * q - 4, :]
                        ins = nc.vector.tensor_tensor(dst, src, pos.unsqueeze(2).to_broadcast([P, 4, 2, 64]), ALU.add)
                    ins.then_inc(S("xT_out"), 1)
            with dve.Fori(0, 12) as i:
                for n in range(RING):
                    dve.wait_ge(S("ada_hi"), i * RING + n + 1)
                    nc.vector.tensor_tensor(lo[:, n % HL], raw[:, n], hi[:, n % HL].bitcast(F32), ALU.subtract).then_inc(S("ada_lo"), 1)
            dve.wait_ge(S("ada_col"), 24)
            link(nc.vector.tensor_tensor(modT[:], ps[5][:, 0:192].rearrange("p (k a) -> p k a", a=2),
                                         par[:, 0:96].unsqueeze(2).to_broadcast([P, 96, 2]), ALU.add))
            for which, g in ((0, G_MIX), (1, G_FFN)):
                scale = modT[:, (3 * which + 1) * KC:(3 * which + 2) * KC, :]
                link(nc.vector.scalar_tensor_tensor(gain[:, which], scale, 1.0, par[:, g:g + KC].unsqueeze(2).to_broadcast([P, KC, 2]), ALU.add, ALU.mult))


def norm(nc, st, S, sb, ps, modT, gain, xT, C, which, out):
    tag = f"norm{which}_"
    sq = sb(st, tag + "sq", [P, 2, T])
    rstd = sb(st, tag + "rstd", [P, T])
    xs = sb(st, tag + "xs", [P, 2, T])

    def scalar(act):
        for k in range(KC):
            if k >= 2:
                act.wait_ge(S(tag + "sum"), k - 1)
            nc.scalar.activation(sq[:, k % 2], xT[:, k], ACT.Square).then_inc(S(tag + "sq"), 1)
        act.wait_ge(S(tag + "mean"), 1)
        nc.scalar.sqrt(rstd[:], rstd[:]).then_inc(S(tag + "root"), 1)
        for k in range(KC):
            act.wait_ge(S(tag + "xs"), k + 1)
            for a, c0, c1 in ((1, 0, LC), (0, LC, T)):
                ins = nc.scalar.activation(out[:, k, c0:c1], xs[:, k % 2, c0:c1], ACT.Identity,
                                           bias=modT[:, 3 * which * KC + k, a:a + 1], scale=gain[:, which, k, a:a + 1])
            ins.then_inc(S(tag + "out"), 1)

    def tensor(pe):
        for k in range(KC):
            pe.wait_ge(S(tag + "sq"), k + 1)
            pe.matmul(ps[0][:, 0:T], C("ones"), sq[:, k % 2], start=(k == 0), stop=(k == KC - 1)).then_inc(S(tag + "sum"), 1)

    def vector(dve):
        dve.wait_ge(S(tag + "sum"), KC)
        nc.vector.tensor_scalar(rstd[:], ps[0][:, 0:T], 1.0 / D, EPS, ALU.mult, ALU.add).then_inc(S(tag + "mean"), 1)
        dve.wait_ge(S(tag + "root"), 1)
        nc.vector.reciprocal(rstd[:], rstd[:]).then_inc(S(tag + "rstd"), 1)
        dve.wait_ge(S(tag + "rstd"), 1)
        for k in range(KC):
            if k >= 2:
                dve.wait_ge(S(tag + "out"), k - 1)
            nc.vector.tensor_tensor(xs[:, k % 2], xT[:, k], rstd[:], ALU.mult).then_inc(S(tag + "xs"), 1)

    return scalar, tensor, vector


def conv_silu(nc, S, tag, eng, link, cin, acc, sig, out, taps, bias):
    link(nc.vector.tensor_scalar(acc[:], cin[:, 0:388], taps(0), None, ALU.mult))
    for t in range(1, 4):
        link(nc.vector.scalar_tensor_tensor(acc[:], cin[:, t:t + 388], taps(t), acc[:], ALU.mult, ALU.add))
    nc.vector.scalar_tensor_tensor(acc[:], cin[:, 4:392], taps(4), acc[:], ALU.mult, ALU.add).then_inc(S(tag + "conv"), 1)


def ssd(nc, I, O, table, S, sb, ps, cst, par, modT, gain, xT, C, hT, mixed, lora):
    w_in = I["w_in"].rearrange("l (k p) n -> p (l k) n", p=P)
    with ExitStack() as st:
        B = sb(st, "B", [P, 2, T])
        Cm = sb(st, "Cm", [P, 2, T])
        Btok = sb(st, "Btok", [P, 2, TILES, P])
        BC = sb(st, "BC", [P, 2, TILES, P])
        cum = sb(st, "cum", [HEADS, 2, T])
        ea = sb(st, "ea", [HEADS, 2, T])
        r7 = sb(st, "r7", [HEADS, 7])
        tokq = sb(st, "tokq", [P, 3, 2, TILES, HEADS])
        cin = sb(st, "cin", [P, 2, 392])
        acc = sb(st, "acc", [P, 388])
        sig = sb(st, "sig", [P, 388])
        w_xz = sb(st, "w_xz", [P, 2, KC, P])
        ssd_shared(nc, I, S, sb, ps, par, modT, gain, xT, C, hT, lora, w_xz, w_in, B, Cm, Btok, BC, cum, ea, r7, tokq, cin, acc, sig)
        ssd_heads(nc, I, O, S, sb, ps, par, C, hT, mixed, w_xz, w_in, Cm, Btok, BC, cum, ea, r7, tokq, cin, acc, sig)


def ssd_shared(nc, I, S, sb, ps, par, modT, gain, xT, C, hT, lora, w_xz, w_in, B, Cm, Btok, BC, cum, ea, r7, tokq, cin, acc, sig):
    COLS = [(2560, 32)] + [(2048 + n * P, P) for n in range(4)] + \
           [(N_SSD_IN + 3072, P), (N_SSD_IN + 3200, 64), (N_SSD_IN + 3264, P), (N_SSD_IN + 3392, 32)]
    with ExitStack() as st:
        RING = 5
        w = sb(st, "w_shared", [P, RING, KC, P])
        dt = sb(st, "dt", [HEADS, 2, T])
        q = sb(st, "q", [HEADS, 4, 2, T])
        small = sb(st, "small", [HEADS, 6])
        reset = sb(st, "reset", [HEADS, 2, T])
        lp = sb(st, "lp", [P, 4, T + 3])
        lt = sb(st, "lt", [P, T + 1])
        mu = sb(st, "mu_l", [P, 2, 4])
        norm_scalar, norm_tensor, norm_vector = norm(nc, st, S, sb, ps, modT, gain, xT, C, 0, hT)
        loaded = [S(f"shared_loaded{n}") for n in range(9)]
        block = st.enter_context(nc.Block())
        LW = [P, 64, P, 32]
        LMU = [MU_WD, MU_AD, MU_GD0, MU_GD1]

        @block.sync
        def _(sp):
            with nc.allow_non_contiguous_dma(reason="per-head scalars"):
                sp.dma_start(small[:, 0:2], I["ssd_A_log"].rearrange("l d h -> h (l d)")).then_inc(S("small_in"), 16)
                sp.dma_start(small[:, 2:4], I["ssd_dt_bias"].rearrange("l d h -> h (l d)")).then_inc(S("small_in"), 16)
                sp.dma_start(r7[:, 6:7], I["ssd_D"].rearrange("l h -> h l")).then_inc(S("small_in"), 16)
            for n, (c0, width) in enumerate(COLS):
                if n == RING:
                    sp.wait_ge(S("dt_proj"), 2)
                if n > RING:
                    sp.wait_ge(S("bc_proj"), n - RING)
                sp.dma_start(w[:, n % RING, :, 0:width], w_in[:, :, c0:c0 + width]).then_inc(loaded[n], 16)
            for j, name in enumerate("xz"):
                sp.dma_start(w_xz[:, j], w_in[:, :, 1024 * (1 - j):1024 * (1 - j) + P]).then_inc(S(f"w{name}_loaded"), 16)

        @block.gpsimd
        def _(pool):
            nc.gpsimd.memset(cin[:], 0.0)
            nc.gpsimd.memset(lp[:], 0.0).then_inc(S("pads_zero"), 1)

        @block.tensor
        def _(pe):
            def project(n, bank, m0, m, done):
                pe.wait_ge(loaded[n], 16)
                for k in range(KC):
                    if n == 0 and m0 == 0:
                        pe.wait_ge(S("norm0_out"), k + 1)
                    mm = pe.matmul(bank, w[:, n % RING, k, m0:m0 + m], hT[:, k], start=(k == 0), stop=(k == KC - 1))
                mm.then_inc(done, 1)

            norm_tensor(pe)
            project(0, ps[0][0:HEADS, 0:T], 0, HEADS, S("dt_proj"))
            project(0, ps[1][0:HEADS, 0:T], HEADS, HEADS, S("dt_proj"))
            for n in range(4):
                if n >= 2:
                    pe.wait_ge(S("bc_in"), n - 1)
                project(1 + n, ps[2 + n % 2][:, 0:T], 0, P, S("bc_proj"))
            for n in range(4):
                if n >= 2:
                    pe.wait_ge(S("lora_in"), n - 1)
                project(5 + n, ps[4 + n % 2][0:LW[n], 0:T], 0, LW[n], S("lora_proj"))
            for g in range(2):
                pe.wait_ge(S("bc_ready"), 4)
                for t in range(TILES):
                    mm = pe.transpose(ps[6][:, t * P:(t + 1) * P], B[:, g, t * P:(t + 1) * P], C("ident"))
                mm.then_inc(S("btok_in"), 1)
                for t in range(TILES):
                    mm = pe.matmul(ps[7][:, t * P:(t + 1) * P], B[:, g, t * P:(t + 1) * P], Cm[:, g, t * P:(t + 1) * P], start=True, stop=True)
                mm.then_inc(S("bcm_in"), 1)
                pe.wait_ge(S("btok_out"), 2 * g + 2)
            pe.wait_ge(S("dt_abs"), 1)
            for j, name in enumerate("xz"):
                pe.wait_ge(S(f"w{name}_loaded"), 16)
                for k in range(KC):
                    mm = pe.matmul(ps[j][:, 0:T], w_xz[:, j, k], hT[:, k], start=(k == 0), stop=(k == KC - 1))
                mm.then_inc(S(f"{name}_proj"), 1)
            pe.wait_ge(S("rows_ready"), 1)
            for j, src in enumerate((dt, cum, q[:, 3])):
                for d in range(2):
                    for t in range(TILES):
                        at = ((j * 2 + d) * TILES + t) * HEADS
                        mm = pe.transpose(ps[2][:, at:at + HEADS], src[:, d, t * P:(t + 1) * P], C("ident", 0, HEADS)[:, 0:HEADS])
            mm.then_inc(S("tokq_in"), 1)

        @block.scalar
        def _(act):
            norm_scalar(act)
            act.wait_ge(S("small_in"), 48)
            nc.scalar.activation(small[:, 4:6], small[:, 0:2], ACT.Exp).then_inc(S("A_exp"), 1)
            act.wait_ge(S("dt_abs"), 1)
            nc.scalar.activation(q[:, 1], q[:, 1], ACT.Exp, scale=-1.0).then_inc(S("dt_exp"), 1)
            act.wait_ge(S("pads_zero"), 1)
            for n in range(4):
                act.wait_ge(S("bc_proj"), n + 1)
                if n >= 2:
                    act.wait_ge(S("bc_conv"), n - 1)
                nc.scalar.copy(cin[:, n % 2, 2:130], ps[2 + n % 2][:, 0:LC])
                nc.scalar.copy(cin[:, n % 2, 134:390], ps[2 + n % 2][:, LC:T]).then_inc(S("bc_in"), 1)
                act.wait_ge(S("bc_conv"), n + 1)
                nc.scalar.activation(sig[:], acc[:], ACT.Sigmoid, bias=par[:, CONV_B + 8 + n:CONV_B + 9 + n]).then_inc(S("bc_sig"), 1)
            for n in range(4):
                act.wait_ge(S("lora_proj"), n + 1)
                b = ps[4 + n % 2][0:LW[n]]
                nc.scalar.copy(lp[0:LW[n], n, 1:129], b[:, 0:LC])
                nc.scalar.copy(lp[0:LW[n], n, 130:386], b[:, LC:T]).then_inc(S("lora_in"), 1)
            for g in range(2):
                act.wait_ge(S("btok_in"), g + 1)
                nc.scalar.copy(Btok[:, g], ps[6][:, 0:T].rearrange("p (t n) -> p t n", t=TILES)).then_inc(S("btok_out"), 1)
                act.wait_ge(S("bcm_in"), g + 1)
                nc.scalar.copy(BC[:, g], ps[7][:, 0:T].rearrange("p (t n) -> p t n", t=TILES)).then_inc(S("btok_out"), 1)
            act.wait_ge(S("lora_mixed"), 4)
            nc.scalar.activation(lora[:, 0], lora[:, 0], ACT.Tanh)
            nc.scalar.activation(lora[:, 2:4], lora[:, 2:4], ACT.Sigmoid)
            act.wait_ge(S("cum_ready"), 2)
            nc.scalar.activation(ea[:], cum[:], ACT.Exp)
            nc.scalar.activation(r7[:, 0:6], q[:, 0, :, 0:3], ACT.Exp)
            nc.scalar.activation(q[:, 2], q[:, 2], ACT.Exp).then_inc(S("decay_exp"), 1)

        @block.vector
        def _(dve):
            norm_vector(dve)
            link = Link(dve, S("shared_dve"))
            link(nc.vector.memset(reset[:], 1.0))
            link(nc.vector.memset(reset[:].rearrange("p d (t c) -> p (d t) c", c=P)[:, :, 0:1], 0.0))
            link(nc.vector.memset(lora[:, 3], 0.0))
            dve.wait_ge(S("A_exp"), 1)
            dve.wait_ge(S("dt_proj"), 2)
            for d in range(2):
                link(nc.vector.tensor_scalar(dt[:, d], ps[d][0:HEADS, 0:T], small[:, 2 + d:3 + d], None, ALU.add))
            nc.vector.scalar_tensor_tensor(q[:, 1], dt[:], -1.0, dt[:], ALU.mult, ALU.max).then_inc(S("dt_abs"), 1)
            dve.wait_ge(S("dt_exp"), 1)
            link(nc.vector.tensor_scalar(q[:, 2], q[:, 1], 2.0, None, ALU.add))
            link(nc.vector.reciprocal(q[:, 2], q[:, 2]))
            link(nc.vector.tensor_tensor(q[:, 1], q[:, 1], q[:, 2], ALU.mult))
            link(nc.vector.tensor_tensor(q[:, 2], q[:, 1], q[:, 1], ALU.mult))
            link(nc.vector.tensor_scalar(q[:, 3], q[:, 2], 1.0 / 17, None, ALU.mult))
            for odd in (15, 13, 11, 9, 7, 5, 3):
                link(nc.vector.scalar_tensor_tensor(q[:, 3], q[:, 3], 1.0 / odd, q[:, 2], ALU.add, ALU.mult))
            link(nc.vector.scalar_tensor_tensor(q[:, 3], q[:, 3], 1.0, q[:, 1], ALU.add, ALU.mult))
            link(nc.vector.tensor_scalar(q[:, 3], q[:, 3], 2.0, None, ALU.mult))
            link(nc.vector.scalar_tensor_tensor(dt[:], dt[:], 0.0, q[:, 3], ALU.max, ALU.add))
            for d in range(2):
                link(nc.vector.tensor_scalar(q[:, 1, d], dt[:, d], small[:, 4 + d:5 + d], -1.0, ALU.mult, ALU.mult))
            for d in range(2):
                link(nc.vector.tensor_tensor_scan(cum[:, d], reset[:, d], q[:, 1, d], 0.0, ALU.mult, ALU.add))
            tot = q[:, 0, :, 0:3]
            link(nc.vector.tensor_copy(tot, cum[:].rearrange("p d (t c) -> p d t c", c=P)[:, :, :, P - 1]))
            link(nc.vector.tensor_tensor(cum[:, 1], q[:, 1, 1], cum[:, 1], ALU.subtract))
            for d in range(2):
                c3 = cum[:, d].rearrange("p (t c) -> p t c", c=P)
                tb = tot[:, d].unsqueeze(2).to_broadcast([HEADS, TILES, P])
                if d == 1:
                    link(nc.vector.tensor_tensor(c3, c3, tb, ALU.add))
                nc.vector.tensor_tensor(q[:, 2, d].rearrange("p (t c) -> p t c", c=P), tb, c3, ALU.subtract).then_inc(S("cum_ready"), 1)
            for n in range(4):
                dve.wait_ge(S("bc_in"), n + 1)
                conv_silu(nc, S, "bc_", dve, link, cin[:, n % 2], acc, sig, None, lambda t: par[:, CONV_W + 12 * t + 8 + n:CONV_W + 12 * t + 9 + n], None)
                dve.wait_ge(S("bc_sig"), n + 1)
                out = (B, Cm)[n // 2][:, n % 2]
                b = par[:, CONV_B + 8 + n:CONV_B + 9 + n]
                nc.vector.scalar_tensor_tensor(out[:, 0:LC], acc[:, 0:LC], b, sig[:, 0:LC], ALU.add, ALU.mult)
                nc.vector.scalar_tensor_tensor(out[:, LC:T], acc[:, 132:388], b, sig[:, 132:388], ALU.add, ALU.mult).then_inc(S("bc_ready"), 1)
                dve.wait_ge(S("bc_ready"), n + 1)
            for n in range(4):
                m = par[:, MU + LMU[n]:MU + LMU[n] + 1]
                link(nc.vector.tensor_scalar(mu[:, 0, n:n + 1], m, -1.0, 1.0, ALU.mult, ALU.add))
                link(nc.vector.tensor_scalar(mu[:, 1, n:n + 1], m, 0.5, None, ALU.mult))
            for n in range(4):
                r = LW[n]
                dve.wait_ge(S("lora_in"), n + 1)
                link(nc.vector.tensor_tensor(lt[0:r], lp[0:r, n, 0:T + 1], lp[0:r, n, 2:T + 3], ALU.add))
                link(nc.vector.tensor_scalar(lt[0:r], lt[0:r], mu[0:r, 1, n:n + 1], None, ALU.mult))
                for c0, c1, skip in ((0, LC, 0), (LC, T, 1)):
                    ins = nc.vector.scalar_tensor_tensor(lora[0:r, n, c0:c1], lp[0:r, n, c0 + 1 + skip:c1 + 1 + skip], mu[0:r, 0, n:n + 1],
                                                         lt[0:r, c0 + skip:c1 + skip], ALU.mult, ALU.add)
                ins.then_inc(S("lora_mixed"), 1)
                dve.wait_ge(S("lora_mixed"), n + 1)
            dve.wait_ge(S("decay_exp"), 1)
            nc.vector.tensor_tensor(q[:, 3], q[:, 2], dt[:], ALU.mult).then_inc(S("rows_ready"), 1)
            dve.wait_ge(S("tokq_in"), 1)
            src = ps[2][:, 0:288].rearrange("p (q r) -> p q r", q=3)
            dst = tokq[:].rearrange("p q d t h -> p q (d t h)")
            link(nc.vector.tensor_copy(dst, src))
            link(nc.vector.tensor_scalar(dst[:, 1], dst[:, 1], -1.0, None, ALU.mult))


def ssd_heads(nc, I, O, S, sb, ps, par, C, hT, mixed, w, w_in, Cm, Btok, BC, cum, ea, r7, tokq, cin, acc, sig):
    HG = KC // 4
    with ExitStack() as st:
        h0 = sb(st, "h0", [P, 2, P])
        xc = sb(st, "xc", [P, T])
        z = sb(st, "z", [P, 2, T])
        sel = sb(st, "sel", [HEADS, 2, P])
        selc = sb(st, "selc", [HEADS, P])
        xq = sb(st, "xq", [P, 4, TILES, P])
        M = sb(st, "M", [P, 4, TILES, P])
        eac = sb(st, "eac", [P, 2, LS])
        r7c = sb(st, "r7c", [P, 7])
        fin = sb(st, "fin", [P, 2, P])
        s1 = sb(st, "s1", [P, 2, P])
        sT = sb(st, "sT", [P, 4, P])
        yo = sb(st, "yo", [P, 2, LS])
        y = sb(st, "y", [P, T])
        block = st.enter_context(nc.Block())
        states = [I["state_ssd_fwd"].rearrange("b l h p n -> (b l h p) n"), I["state_ssd_bwd"].rearrange("b l h p n -> (b l h p) n")]
        finals = [O["ssd_fwd"].rearrange("b l h p n -> (b l h p) n"), O["ssd_bwd"].rearrange("b l h p n -> (b l h p) n")]
        ident16 = C("ident", 0, HEADS)

        @block.gpsimd
        def _(pool):
            ahead(pool, S, "z_proj", "hT_in", "eac_out", "r7_out", "seg_done", "sT_out", "s1_ready", "y_done", "xtok_in", "x_conv", "fin_out", "y_in")

        def turns(eng, body):
            with eng.Fori(0, HG) as c:
                body(0, c, True)
            with eng.Fori(HG, PAIRS - 1) as c:
                body(1, c, True)
            body(1, PAIRS - 1, False)

        @block.sync
        def _(sp):
            def load_w(c):
                for j, name in enumerate("xz"):
                    sp.wait_ge(S(name + "_proj"), c + j)
                    sp.sem_inc(S("sp_held_s"), 1)
                    sp.dma_start(w[:, j], w_in[:, :, bass.ds(c * P + 1024 * (1 - j), P)]).then_inc(S(f"w{name}_loaded"), 16)

            def load_h0(c):
                for d in range(2):
                    sp.dma_start(h0[:, d], states[d][bass.ds(c * P + 0, P), :]).then_inc(S("h0_in"), 16)

            def body(g, c, more):
                if more:
                    load_w(c + 1)
                    sp.wait_ge(S("hT_in"), c + 2)
                    sp.sem_inc(S("sp_held_s"), 1)
                    load_h0(c + 1)
                sp.wait_ge(S("fin_ready"), c + 1)
                sp.sem_inc(S("sp_held_s"), 1)
                for d in range(2):
                    sp.dma_start(finals[d][bass.ds(c * P + 0, P), :], fin[:, d]).then_inc(S("fin_out"), 16)

            load_h0(0)
            turns(sp, body)
            sp.wait_ge(S("fin_out"), 16 * 2 * PAIRS + 1)

        @block.tensor
        def _(pe):
            def feed(c, n0, n1):
                for n in range(n0, n1):
                    j, k = n // KC, n % KC
                    if k == 0:
                        pe.wait_ge(S(("wx_loaded", "wz_loaded")[j]), (c + 1) * 16)
                        pe.wait_ge(S(("x_in_conv", "z_out")[j]), c)
                    mm = pe.matmul(ps[j][:, 0:T], w[:, j, k], hT[:, k], start=(k == 0), stop=(k == KC - 1))
                    if k == KC - 1:
                        mm.then_inc(S(("x_proj", "z_proj")[j]), 1)

            def body(g, c, more):
                def fed(n0, n1):
                    if more:
                        feed(c + 1, n0, n1)

                pe.wait_ge(S("sel_ready"), c + 1)
                for u in range(4):
                    if u == 2:
                        fed(0, FEED[0])
                    if u < 2:
                        pe.wait_ge(S("seg_done"), c * 4 + 1)
                    else:
                        pe.wait_ge(S("seg_done"), c * 4 + u - 1 + 1)
                    pe.matmul(ps[3 + u % 2][:, 0:T], sel[:, u // 2], cum[:, u % 2], start=True, stop=True).then_inc(S("seg_in"), 1)
                    if u == 2:
                        fed(FEED[0], FEED[1])
                pe.wait_ge(S("y_done"), c + 1)
                for d in range(2):
                    mm = pe.matmul(ps[7][:, d * LS:(d + 1) * LS], selc[:], ea[:, d, LC:T], start=True, stop=True)
                mm.then_inc(S("eac_in"), 1)
                pe.matmul(ps[6][:, 0:7], selc[:], r7[:], start=True, stop=True).then_inc(S("r7_in"), 1)
                fed(FEED[1], FEED[2])
                pe.wait_ge(S("xc_ready"), c + 1)
                pe.wait_ge(S("sT_out"), c + 1)
                for t in range(TILES):
                    mm = pe.transpose(ps[2][:, t * P:(t + 1) * P], xc[:, t * P:(t + 1) * P], C("ident"))
                mm.then_inc(S("xtok_in"), 1)
                fed(FEED[2], FEED[3])
                pe.wait_ge(S("xq_ready"), c + 1)
                pe.wait_ge(S("s1_ready"), c + 1)
                for k, (d, t) in enumerate(((0, 0), (1, 0), (0, 1), (1, 2))):
                    mm = pe.matmul(ps[5][:, k * P:(k + 1) * P], xq[:, 2 + d, t], Btok[:, bass.ds(g, 1), t], start=True, stop=True)
                mm.then_inc(S("states_in"), 1)
                fed(FEED[3], FEED[4])
                pe.wait_ge(S("s1_ready"), c + 2)
                for k in range(4):
                    mm = pe.transpose(ps[2][:, k * P:(k + 1) * P], (h0, s1)[k // 2][:, k % 2], C("ident"))
                mm.then_inc(S("hT_in"), 1)
                fed(FEED[4], FEED[5])
                pe.wait_ge(S("M_ready"), 4 * (c + 1))
                pe.wait_ge(S("r7_out"), c + 2)
                for t in range(TILES):
                    for h in range(2):
                        for d in range(2):
                            mm = pe.matmul(ps[6][h * HD:(h + 1) * HD, t * P:(t + 1) * P], xq[:, d, t, h * HD:(h + 1) * HD], M[:, 2 * h + d, t],
                                           start=(d == 0), stop=(d == 1))
                mm.then_inc(S("y_in"), 1)
                pe.wait_ge(S("sT_out"), c + 2)
                pe.wait_ge(S("eac_out"), c + 2)
                for d, t, k in ((0, 1, 0), (0, 2, 2), (1, 2, 1), (1, 1, 3)):
                    at = d * LS + (t - 1) * P
                    mm = pe.matmul(ps[7][:, at:at + P], sT[:, k], Cm[:, bass.ds(g, 1), t * P:(t + 1) * P], start=True, stop=True)
                mm.then_inc(S("yo_in"), 1)
                fed(FEED[5], 2 * KC)

            FEED = (12, 14, 18, 22, 26, 28)
            turns(pe, body)

        @block.scalar
        def _(act):
            def body(g, c, more):
                act.wait_ge(S("xtok_in"), c + 1)
                nc.scalar.copy(sel[:], ident16[:, bass.ds(c * 2, 2)].unsqueeze(2).to_broadcast([HEADS, 2, P]))
                nc.scalar.copy(selc[:].rearrange("p (h c) -> p h c", h=2),
                               ident16[:, bass.ds(c * 2, 2)].unsqueeze(2).to_broadcast([HEADS, 2, HD])).then_inc(S("sel_ready"), 1)
                act.wait_ge(S("x_proj"), c + 1)
                act.wait_ge(S("x_conv"), c + 1)
                nc.scalar.copy(cin[:, 0, 2:130], ps[0][:, 0:LC])
                nc.scalar.copy(cin[:, 0, 134:390], ps[0][:, LC:T]).then_inc(S("x_in_conv"), 1)
                act.wait_ge(S("x_conv"), c + 2)
                nc.scalar.activation(sig[:], acc[:], ACT.Sigmoid, bias=par[:, bass.ds(c + CONV_B, 1)]).then_inc(S("x_sig"), 1)
                act.wait_ge(S("z_proj"), c + 2)
                act.wait_ge(S("y_done"), c + 1)
                nc.scalar.activation(z[:, 1], ps[1][:, 0:T], ACT.Sigmoid)
                nc.scalar.copy(z[:, 0], ps[1][:, 0:T]).then_inc(S("z_out"), 1)
                act.wait_ge(S("eac_in"), c + 1)
                nc.scalar.copy(eac[:], ps[7][:].rearrange("p (d t) -> p d t", d=2)).then_inc(S("eac_out"), 1)
                act.wait_ge(S("r7_in"), c + 1)
                nc.scalar.copy(r7c[:], ps[6][:, 0:7]).then_inc(S("r7_out"), 1)
                for u in range(4):
                    act.wait_ge(S("seg_done"), c * 4 + u + 2)
                    nc.scalar.activation(M[:, u], M[:, u], ACT.Exp).then_inc(S("M_exp"), 1)
                act.wait_ge(S("states_in"), c + 1)
                act.wait_ge(S("fin_out"), c * 32 + 1)
                nc.scalar.copy(fin[:], ps[5][:, 0:2 * P].rearrange("p (d n) -> p d n", d=2)).then_inc(S("fin_ready"), 1)
                act.wait_ge(S("hT_in"), c + 2)
                nc.scalar.copy(sT[:], ps[2][:].rearrange("p (k n) -> p k n", k=4)).then_inc(S("sT_out"), 1)
            turns(act, body)

        STEPS = 4 + 5

        @block.vector
        def _(dve):
            def body(g, c, more):
                link = Link(dve, S("ssd_dve"), c * STEPS)
                dve.wait_ge(S("x_in_conv"), c + 1)
                conv_silu(nc, S, "x_", dve, link, cin[:, 0], acc, sig, None, lambda t: par[:, bass.ds(c + (CONV_W + 12 * t), 1)], None)
                dve.wait_ge(S("x_sig"), c + 1)
                b = par[:, bass.ds(c + CONV_B, 1)]
                nc.vector.scalar_tensor_tensor(xc[:, 0:LC], acc[:, 0:LC], b, sig[:, 0:LC], ALU.add, ALU.mult)
                nc.vector.scalar_tensor_tensor(xc[:, LC:T], acc[:, 132:388], b, sig[:, 132:388], ALU.add, ALU.mult).then_inc(S("xc_ready"), 1)
                for u in range(4):
                    dve.wait_ge(S("seg_in"), c * 4 + u + 1)
                    dve.wait_ge(S("y_in"), c + 1)
                    for t in range(TILES):
                        ins = nc.vector.scalar_tensor_tensor(M[:, u, t], ps[3 + u % 2][:, t * P:(t + 1) * P], tokq[:, 1, u % 2, t, bass.ds(c * 2 + u // 2, 1)],
                                                             C(f"neg{u % 2}"), ALU.add, ALU.add)
                    ins.then_inc(S("seg_done"), 1)
                dve.wait_ge(S("xtok_in"), c + 2)
                src = ps[2][:, 0:T].rearrange("p (t h c) -> p t h c", t=TILES, h=2)
                for k in range(4):
                    f = tokq[:, (0, 2)[k // 2], k % 2, :, bass.ds(c * 2, 2)].unsqueeze(3).to_broadcast([P, TILES, 2, HD])
                    ins = nc.vector.tensor_tensor(xq[:, k].rearrange("p t (h c) -> p t h c", h=2), src, f, ALU.mult)
                ins.then_inc(S("xq_ready"), 1)
                dve.wait_ge(S("states_in"), c + 1)
                dve.wait_ge(S("r7_out"), c + 2)
                dve.wait_ge(S("h0_in"), (c + 1) * 32)
                dve.wait_ge(S("fin_ready"), c + 1)
                for d in range(2):
                    ins = nc.vector.scalar_tensor_tensor(s1[:, d], h0[:, d], r7c[:, 3 * d + (1, 2)[d]:3 * d + (1, 2)[d] + 1], ps[5][:, (2 + d) * P:(3 + d) * P], ALU.mult, ALU.add)
                ins.then_inc(S("s1_ready"), 1)
                for u in range(4):
                    dve.wait_ge(S("M_exp"), c * 4 + u + 1)
                    nc.vector.tensor_tensor(M[:, u], M[:, u], BC[:, bass.ds(g, 1)].rearrange("p a t n -> p (a t) n"), ALU.mult).then_inc(S("M_ready"), 1)
                dve.wait_ge(S("y_in"), c + 2)
                dve.wait_ge(S("y_done"), c + 1)
                link(nc.vector.scalar_tensor_tensor(y[:], xc[:], r7c[:, 6:7], ps[6][:, 0:T], ALU.mult, ALU.add))
                dve.wait_ge(S("yo_in"), c + 1)
                link(nc.vector.tensor_tensor(yo[:], ps[7][:].rearrange("p (d t) -> p d t", d=2), eac[:], ALU.mult))
                for d in range(2):
                    link(nc.vector.tensor_tensor(y[:, LC:T], y[:, LC:T], yo[:, d], ALU.add))
                link(nc.vector.tensor_tensor(y[:], y[:], z[:, 0], ALU.mult))
                nc.vector.tensor_tensor(mixed[:, bass.ds(c, 1)].rearrange("p a t -> p (a t)"), y[:], z[:, 1], ALU.mult).then_inc(S("y_done"), 1)
                assert link.n == STEPS
            turns(dve, body)


def ssd_norm(nc, S, ps, par, C, mixed, sq, rstd):
    HG = KC // 4

    def scalar(act):
        for k in range(PAIRS):
            if k >= 2:
                act.wait_ge(S("gn_sum"), k - 1)
            nc.scalar.activation(sq[k % 2][:], mixed[:, k], ACT.Square).then_inc(S("gn_sq"), 1)
        act.wait_ge(S("gn_mean"), 1)
        for g in range(2):
            ins = nc.scalar.sqrt(rstd[g][:], rstd[g][:])
        ins.then_inc(S("gn_root"), 1)

    def tensor(pe):
        for k in range(PAIRS):
            pe.wait_ge(S("gn_sq"), k + 1)
            pe.matmul(ps[k // HG][:, 0:T], C("ones"), sq[k % 2][:], start=(k % HG == 0), stop=(k % HG == HG - 1)).then_inc(S("gn_sum"), 1)

    def vector(dve):
        dve.wait_ge(S("gn_sum"), PAIRS)
        for g in range(2):
            ins = nc.vector.tensor_scalar(rstd[g][:], ps[g][:, 0:T], 1.0 / (HG * P), EPS, ALU.mult, ALU.add)
        ins.then_inc(S("gn_mean"), 1)
        dve.wait_ge(S("gn_root"), 1)
        for g in range(2):
            ins = nc.vector.reciprocal(rstd[g][:], rstd[g][:])
        ins.then_inc(S("gn_rstd"), 1)
        dve.wait_ge(S("gn_rstd"), 1)
        for k in range(PAIRS):
            ins = nc.vector.scalar_tensor_tensor(mixed[:, k], mixed[:, k], par[:, G_SSD + k:G_SSD + k + 1], rstd[k // HG][:], ALU.mult, ALU.mult)
        ins.then_inc(S("gn_done"), 1)
        dve.wait_ge(S("gn_done"), 1)

    return scalar, tensor, vector


def rwkv(nc, I, O, table, S, sb, ps, cst, par, modT, gain, xT, C, hT, mixed, lora):
    w_in = I["w_in"].rearrange("l (k p) n -> p (l k) n", p=P)
    w_out = I["w_out"].rearrange("l (k p) n -> p (l k) n", p=P)
    w_up = I["rwkv_w_up"].rearrange("l d r n -> (l d r) n")
    a_up, g_up = I["rwkv_a_up"][0], I["rwkv_g_up"][0]
    with ExitStack() as st:
        w = sb(st, "w_rkv", [P, 3, KC // 2, P])
        lw = sb(st, "lw", [P, 4, P])
        raw = sb(st, "raw_rkv", [P, 3, T + 3])
        sh = sb(st, "sh", [P, T + 1])
        mu = sb(st, "mu_rkv", [P, 2, 24])
        omk = sb(st, "omk", [P, PAIRS])
        reset = sb(st, "reset64", [P, T])
        r, k, kk, ka, a, g, rk, bonus, t0, yc, rstd = (sb(st, n, [P, T]) for n in ("r", "k", "kk", "ka", "a", "g", "rk", "bonus", "t0", "yc", "gn_rstd"))
        v = sb(st, "v", [P, Q + T])
        sg = sb(st, "sg", [P, 2, T])
        ex = sb(st, "ex", [P, 3, T])
        wl = sb(st, "wl", [P, 2 * NCH])
        wls = sb(st, "wls", [Q, 2, 2 * NCH])
        s0 = sb(st, "s0", [P, 2, HD])
        fin = sb(st, "fin_r", [Q, 2, P])
        fo = sb(st, "fo", [P, 2, HD])
        M1 = [sb(st, f"M1_{d}", [P, NCH, 3, Q]) for d in range(2)]
        M2 = [sb(st, f"M2_{d}", [P, NCH, 3, Q]) for d in range(2)]
        W1 = [sb(st, f"W1_{d}", [P, NCH, 3, Q]) for d in range(2)]
        WX = [sb(st, f"WX_{d}", [P, 4 * NCH * Q]) for d in range(2)]
        WI = [sb(st, f"WI_{d}", [P, 3, NCH * Q]) for d in range(2)]
        VS = [sb(st, f"VS_{d}", [P, NCH, 2, HD]) for d in range(2)]
        W2 = [x[:, 0:3 * NCH * Q].rearrange("p (c j q) -> p c j q", c=NCH, j=3) for x in WX]
        P1 = [x[:, 3 * NCH * Q:].rearrange("p (c q) -> p c q", c=NCH) for x in WX]
        XX = [x[:].rearrange("p (h c q) -> p h c q", h=2, c=NCH) for x in WX]
        X, XT, CT = ([x[:, j].rearrange("p (c q) -> p c q", c=NCH) for x in WI] for j in range(3))
        PU = [x[:, 1:3].rearrange("p j q -> p (j q)").rearrange("p (c q) -> p c q", c=NCH) for x in WI]
        w_loaded = [S(f"w_loaded{n}") for n in range(3)]
        norm_scalar, norm_tensor, norm_vector = ssd_norm(nc, S, ps, par, C, mixed, (t0, rk), (yc, rstd))
        block = st.enter_context(nc.Block())
        HP = (slice(0, Q), slice(Q, P))
        SEQ = (((0, 1), (2, 3, 4, 5)), ((1, 0), (5, 4, 3, 2)))
        states = [I["state_rwkv_fwd"].rearrange("b l h v k -> (b l h v) k"), I["state_rwkv_bwd"].rearrange("b l h v k -> (b l h v) k")]
        finals = [O["rwkv_fwd"].rearrange("b l h v k -> (b l h v) k"), O["rwkv_bwd"].rearrange("b l h v k -> (b l h v) k")]

        def c6(x):
            return x.rearrange("p (c q) -> p c q", c=NCH)

        def rounds():
            for rnd in range(3):
                for d in range(2):
                    for part in range(2):
                        seq = SEQ[d][part]
                        if rnd < 2 or part == 1:
                            yield rnd, 2 * d + part, d, seq[rnd], seq[rnd + 1] if rnd + 1 < len(seq) else None

        def out_chunk(p, i):
            return 6 * (p - PAIRS + 2) + i if isinstance(p, int) and p >= PAIRS - 2 else None

        def turns(eng, body):
            body(0, False, 2)
            with eng.Fori(1, PAIRS - 2) as p:
                body(p, True, 2)
            body(PAIRS - 2, True, 1)
            body(PAIRS - 1, True, 0)

        @block.sync
        def _(sp):
            def load_half(p, m):
                if not (isinstance(p, int) and 6 * p + m < 3):
                    sp.wait_ge(S("w_used"), 6 * p + (m - 2))
                    sp.sem_inc(S("w_held"), 1)
                j, half = m % 6 // 2, m % 2
                n = out_chunk(p, m - 12) if m >= 12 else None
                if n is None:
                    src = w_in[:, half * (KC // 2):(half + 1) * (KC // 2), bass.ds((p + m // 6) * P + (N_SSD_IN + 1024 * j), P)]
                else:
                    src = w_out[:, 0:KC // 2, n * P:(n + 1) * P]
                sp.dma_start(w[:, m % 3], src).then_inc(w_loaded[m % 3], 16)

            def load_decay(p):
                sp.dma_start(lw[:, 0], w_up[:, bass.ds(p * P + 0, P)]).then_inc(S("lw_loaded"), 16)
                sp.dma_start(lw[0:64, 1], a_up[:, bass.ds(p * P + 0, P)]).then_inc(S("lw_loaded"), 16)

            def load_gate(p):
                sp.dma_start(lw[:, 2], g_up[0:P, bass.ds(p * P + 0, P)]).then_inc(S("lg_loaded"), 16)
                sp.dma_start(lw[0:32, 3], g_up[P:P + 32, bass.ds(p * P + 0, P)]).then_inc(S("lg_loaded"), 16)

            def load_states(p):
                for d in range(2):
                    sp.dma_start(s0[:, d], states[d][bass.ds(p * P + 0, P), :]).then_inc(S("s0_loaded"), 16)

            def store_states(p):
                sp.wait_ge(S("fo_ready"), p + 1)
                for d in range(2):
                    sp.dma_start(finals[d][bass.ds(p * P + 0, P), :], fo[:, d]).then_inc(S("fo_out"), 16)

            def body(p, prev, more):
                for m in range(12, 15):
                    load_half(p, m)
                if more:
                    sp.wait_ge(S("w1_in"), p + 1)
                    load_decay(p + 1)
                    sp.wait_ge(S("s0_in"), p + 1)
                    load_states(p + 1)
                if prev:
                    store_states(p - 1)
                load_half(p, 15)
                if more:
                    sp.wait_ge(S("g_in"), p + 1)
                    load_gate(p + 1)
                load_half(p, 16)
                load_half(p, 17)

            for m in range(3):
                load_half(0, m)
            load_decay(0)
            load_gate(0)
            load_states(0)
            for m in range(3, 12):
                load_half(0, m)
            turns(sp, body)
            store_states(PAIRS - 1)
            sp.wait_ge(S("fo_out"), 32 * PAIRS)

        @block.gpsimd
        def _(pool):
            ahead(pool, S, "P1_in0", "P1_in1", "XX_ready0", "XX_ready1")
            nc.gpsimd.memset(raw[:], 0.0)
            nc.gpsimd.memset(v[:], 0.0)
            for d in range(2):
                nc.gpsimd.memset(VS[d][:], 0.0)
            nc.gpsimd.memset(reset[:], 1.0).then_inc(S("reset_ones"), 1)
            pool.wait_ge(S("reset_ones"), 1)
            nc.gpsimd.memset(c6(reset[:])[:, :, 0:1], 0.0)
            i2 = C("i2").unsqueeze(1).to_broadcast([P, NCH, Q])
            for d in range(2):
                nc.gpsimd.tensor_copy(M1[d][:, :, 0], i2)
                ins = nc.gpsimd.tensor_copy(M2[d][:, :, 1], i2)
            ins.then_inc(S("rwkv_fixed"), 1)
            with pool.Fori(0, PAIRS) as p:
                for n in range(1, 6):
                    for d in range(2):
                        pool.wait_ge(S(f"W2_ready{d}"), 3 * p + 3)
                        pool.wait_ge(S(f"P1_in{d}"), 5 * p + n - 1 + 1)
                        pool.wait_ge(S(f"XX_ready{d}"), 8 * p + 1)
                        m = C(("high", "low")[d] + str(n)).unsqueeze(1).to_broadcast([P, NCH, Q])
                        nc.gpsimd.tensor_tensor(CT[d], W2[d][:, :, 2], m, ALU.mult).then_inc(S(f"CT_ready{d}"), 1)

        @block.tensor
        def _(pe):
            def hold():
                pe.sem_inc(S("pe_held"), 1)

            def feed(p, n0, n1):
                for n in range(n0, n1):
                    j, m = n // KC, n // 8
                    if n % 8 == 0:
                        pe.wait_ge(w_loaded[m % 3], (2 * p + (m // 3 + 5)) * 16)
                    chunk = out_chunk(p, m)
                    if chunk is not None:
                        if n % 8 == 0:
                            if chunk:
                                pe.wait_ge(S("out_part"), chunk)
                            else:
                                pe.wait_ge(S("raw_in"), 3 * PAIRS)
                        mm = pe.matmul(ps[6][:, 0:T], w[:, m % 3, n % 8], mixed[:, n % 8], start=(n % 8 == 0), stop=(n % 8 == 7))
                        if n % 8 == 7:
                            mm.then_inc(S("w_used"), 1)
                        continue
                    if n % KC == 0 and not (isinstance(p, int) and 3 * p + 6 + j == 0):
                        pe.wait_ge(S("raw_in"), 3 * p + (6 + j))
                    mm = pe.matmul(ps[6][:, 0:T], w[:, m % 3, n % 8], hT[:, n % KC], start=(n % KC == 0), stop=(n % KC == KC - 1))
                    if n % 8 == 7:
                        mm.then_inc(S("w_used"), 1)

            def small(bank, lhsT, rhs, done, start=True, stop=True):
                mm = pe.matmul(ps[bank][:, 0:T], lhsT, rhs, start=start, stop=stop)
                if done:
                    mm.then_inc(S(done), 1)

            def front(q, step):
                if step == 0:
                    pe.wait_ge(S("lw_loaded"), (q + 1) * 32)
                    if not (isinstance(q, int) and q == 0):
                        pe.wait_ge(S("g_out"), q)
                    small(7, lw[0:64, 1], lora[0:64, 1], "a_in")
                if step == 1:
                    pe.wait_ge(S("sig_out"), 3 * q + 1)
                    small(7, lw[0:64, 0], lora[0:64, 0], "w0_in")
                if step == 2:
                    pe.wait_ge(S("kk_sq"), q + 1)
                    pe.wait_ge(S("sig_out"), 3 * q + 2)
                    small(7, C("blk"), t0[:], "kk_sum")
                if step == 3:
                    pe.wait_ge(S("kk_root"), q + 1)
                    small(7, lw[64:128, 0], lora[64:128, 0], "w1_in")

            def gate(p):
                pe.wait_ge(S("bonus_ready"), p + 1)
                pe.wait_ge(S("lg_loaded"), (p + 1) * 32)
                pe.wait_ge(S("wl_ready"), 2 * p + 2)
                for h in range(2):
                    at = T + h * 2 * NCH
                    pe.matmul(ps[7][0:Q, at:at + 2 * NCH], C("ident")[:, h * Q:(h + 1) * Q], wl[:], start=True, stop=True)
                small(7, lw[:, 2], lora[:, 2], None, stop=False)
                small(7, lw[0:32, 3], lora[0:32, 3], "g_in", start=False)

            def mean(q):
                pe.wait_ge(S("y_read"), q + 1)
                small(4, C("blk"), yc[:], "mean_in")

            def variance(q):
                pe.wait_ge(S("yc_sq"), q + 1)
                small(5, C("blk"), rstd[:], "var_in")

            per_level = ((1, 1, 2, 2), (1, 1, 2, 2), (1, 1, 2, 2), (1, 1, 1, 1), (2, 2, 2, 2))
            FED = [10 + sum(sum(per_level, ())[:n]) for n in range(21)]

            def body(p, prev, more):
                pe.wait_ge(S("shifted"), 3 * p + 3)
                pe.wait_ge(S("s0_loaded"), (p + 1) * 32)
                for c in range(NCH):
                    pe.transpose(ps[c // 4][:, c % 4 * P:(c % 4 + 1) * P], v[:, c * Q:c * Q + P], C("ident"))
                for d in range(2):
                    mm = pe.transpose(ps[1][0:HD, (2 + d) * P:(3 + d) * P], s0[:, d], C("ident"))
                mm.then_inc(S("s0_in"), 1)
                feed(p, 0, 2)
                if prev:
                    mean(p - 1)
                for d in range(2):
                    pe.wait_ge(S(f"hats{d}"), 4 * p + 4)
                    if d == 0:
                        pe.wait_ge(S("VS_ready"), p + 1)
                    if prev:
                        pe.wait_ge(S("y_read" if d == 0 else "fo_ready"), p)
                    if prev and d == 1:
                        pe.wait_ge(S("var_read"), p)
                    hold()
                    for c in range(NCH):
                        for h in range(2):
                            mm = pe.matmul(ps[3 * d + c // 2][HP[h], (c % 2) * 192:(c % 2 + 1) * 192], M2[d][HP[h], c, 2], M1[d][HP[h], c], start=True, stop=True)
                    mm.then_inc(S(f"E1_in{d}"), 1)
                    feed(p, 2 + 2 * d, 4 + 2 * d)
                    if prev and d == 0:
                        variance(p - 1)
                pe.wait_ge(S("rk"), p + 1)
                pe.wait_ge(S("sig_out"), 3 * p + 3)
                small(7, C("blk"), rk[:], "bonus_sum")
                for d in range(2):
                    pe.wait_ge(S(f"W1_ready{d}"), 3 * p + 3)
                    hold()
                    for c in range(NCH):
                        for h in range(2):
                            mm = pe.matmul(ps[3 * d + c // 2][HP[h], (c % 2) * 192:(c % 2 + 1) * 192], M1[d][HP[h], c, 2], M2[d][HP[h], c], start=True, stop=True)
                    mm.then_inc(S(f"E2_in{d}"), 1)
                    feed(p, 6 + 2 * d, 8 + 2 * d)
                for n in range(1, 6):
                    for d in range(2):
                        pe.wait_ge(S(f"CT_ready{d}"), 5 * p + n)
                        pe.wait_ge(S(f"X_ready{d}"), 5 * p + n)
                        hold()
                        for c in range(NCH):
                            for h in range(2):
                                mm = pe.matmul(ps[3 * d][HP[h], c * Q:(c + 1) * Q], CT[d][HP[h], c], X[d][HP[h], c], start=True, stop=True)
                        mm.then_inc(S(f"P1_in{d}"), 1)
                        feed(p, FED[4 * (n - 1) + d], FED[4 * (n - 1) + d + 1])
                        if d == 1 and n in (3, 4) and more:
                            front(p + 1, 2 * n - 5)
                    for d in range(2):
                        pe.wait_ge(S(f"P1_out{d}"), 5 * p + n)
                        hold()
                        for c in range(NCH):
                            for h in range(2):
                                mm = pe.matmul(ps[3 * d + 1][HP[h], c * Q:(c + 1) * Q], XT[d][HP[h], c], P1[d][HP[h], c], start=True, stop=True)
                                if n < 5:
                                    mm = pe.matmul(ps[3 * d + 2][HP[h], c * Q:(c + 1) * Q], P1[d][HP[h], c], XT[d][HP[h], c], start=True, stop=True)
                        mm.then_inc(S(f"D_in{d}"), 1)
                        feed(p, FED[4 * (n - 1) + 2 + d], FED[4 * (n - 1) + 3 + d])
                        if (n, d) == (2, 0):
                            gate(p)
                    if n in (2, 3) and more:
                        front(p + 1, 2 * n - 4)
                for d in range(2):
                    pe.wait_ge(S(f"X_final{d}"), p + 1)
                    hold()
                    for c in range(NCH):
                        for h in range(2):
                            mm = pe.matmul(ps[3 * d + c // 4][HP[h], (c % 4) * P:(c % 4 + 1) * P], X[d][HP[h], c], W2[d][HP[h], c, 0:2], start=True, stop=True)
                    mm.then_inc(S(f"PU_in{d}"), 1)
                for u in range(8):
                    for d in range(2):
                        h, c0, c1 = u // 4, (0, 4)[u // 2 % 2], (4, NCH)[u // 2 % 2]
                        if u >= 3:
                            pe.wait_ge(S(f"XX_ready{d}"), 8 * p + u - 2 + 1)
                        elif u >= 1:
                            pe.wait_ge(S(f"PU_out{d}"), p + 1)
                        hold()
                        for c in range(c0, c1):
                            out = ps[3 * d + (2 + u) % 3][:, (c - c0) * P:(c - c0 + 1) * P]
                            if u % 2 == 0:
                                mm = pe.matmul(out, M1[d][HP[h], c, 0:2], M2[d][HP[h], c, 0:2], start=True, stop=True)
                            else:
                                mm = pe.matmul(out, W1[d][HP[h], c, 0:2], PU[d][HP[h], c], start=True, stop=True)
                        mm.then_inc(S(f"XX_in{d}"), 1)
                for rnd, item, d, c, nxt in rounds():
                    if (item, d) == (0 if rnd < 2 else 1, 0):
                        if rnd == 0:
                            pe.wait_ge(S("XX_ready0"), 8 * p + 8 + 1)
                            pe.wait_ge(S("XX_ready1"), 8 * p + 8 + 1)
                            pe.wait_ge(S("VS_ready"), p + 1)
                        else:
                            feed(p, 36 + 4 * rnd, 40 + 4 * rnd)
                            pe.wait_ge(S("state_out"), 10 * p + 4 * rnd)
                    hold()
                    for h in range(2):
                        at = item * P + h * HD
                        mm = pe.matmul(ps[rnd % 2][0:Q, at:at + HD], XX[d][:, h, c, Q:P], VS[d][:, c, h], start=True, stop=True)
                    mm.then_inc(S("state_in"), 1)
                pe.wait_ge(S("state_out"), 10 * p + 10)
                hold()
                for c in range(NCH):
                    for h in range(2):
                        for d in range(2):
                            mm = pe.matmul(ps[2][HP[h], c * Q:(c + 1) * Q], VS[d][:, c, h], XX[d][:, h, c, 0:Q], start=(d == 0), stop=(d == 1))
                mm.then_inc(S("y_in_r"), 1)
                for d in range(2):
                    mm = pe.transpose(ps[3][:, d * HD:(d + 1) * HD], fin[:, d], C("ident", 0, Q)[:, 0:Q])
                mm.then_inc(S("fin_T"), 1)

            norm_tensor(pe)
            feed(-2, 0, 3 * KC)
            for step in range(4):
                front(0, step)
                if step < 3:
                    feed(-1, step * KC, (step + 1) * KC)
            turns(pe, body)
            mean(PAIRS - 1)
            variance(PAIRS - 1)

        @block.scalar
        def _(act):
            def raw_in(q, j):
                act.wait_ge(S("w_used"), 6 * q + (2 * j + 2))
                if not (isinstance(q, int) and q == 0):
                    act.wait_ge(S("shifted"), 3 * q + (j - 2))
                nc.scalar.copy(raw[:, j, 1:129], ps[6][:, 0:LC])
                nc.scalar.copy(raw[:, j, 130:386], ps[6][:, LC:T]).then_inc(S("raw_in"), 1)

            def front(q, step):
                def sig(out, at, done):
                    act.wait_ge(S(done), q + 1)
                    nc.scalar.activation(out, ps[7][:, 0:T], ACT.Sigmoid, bias=par[:, bass.ds(q + at, 1)]).then_inc(S("sig_out"), 1)

                if step == 0:
                    act.wait_ge(S("kk_raw"), q + 1)
                    nc.scalar.activation(t0[:], kk[:], ACT.Square).then_inc(S("kk_sq"), 1)
                    sig(a[:], A0, "a_in")
                if step == 1:
                    sig(sg[:, 0], W0, "w0_in")
                if step == 2:
                    act.wait_ge(S("kk_sum"), q + 1)
                    nc.scalar.sqrt(t0[:], ps[7][:, 0:T]).then_inc(S("kk_root"), 1)
                if step == 3:
                    sig(sg[:, 1], W0 + 8, "w1_in")

            def decays(q, d):
                act.wait_ge(S("cum_done"), 2 * q + d + 1)
                nc.scalar.activation(ex[:, 0], ex[:, 1], ACT.Exp, scale=-DECAY)
                nc.scalar.activation(ex[:, 2], ex[:, 2], ACT.Exp, scale=-DECAY).then_inc(S("ex_some"), 1)
                act.wait_ge(S("ex_some"), 2 * q + d + 1)
                nc.scalar.activation(ex[:, 1], ex[:, 1], ACT.Exp, scale=DECAY).then_inc(S("ex_ready"), 1)

            def square(q):
                act.wait_ge(S("yc"), q + 1)
                nc.scalar.activation(rstd[:], yc[:], ACT.Square).then_inc(S("yc_sq"), 1)

            def root(q):
                act.wait_ge(S("var_read"), q + 1)
                nc.scalar.sqrt(rstd[:], rstd[:]).then_inc(S("var_root"), 1)

            def body(p, prev, more):
                act.wait_ge(S("s0_in"), p + 1)
                for d in range(2):
                    nc.scalar.copy(VS[d][Q:P, 0:4].rearrange("p c h v -> p (c h v)"), ps[0][Q:P, :])
                    nc.scalar.copy(VS[d][Q:P, 4:6].rearrange("p c h v -> p (c h v)"), ps[1][Q:P, 0:2 * P])
                    ins = nc.scalar.copy(VS[d][0:Q, SEQ[d][1][0]].rearrange("p h v -> p (h v)"), ps[1][0:Q, (2 + d) * P:(3 + d) * P])
                ins.then_inc(S("VS_ready"), 1)
                if prev:
                    square(p - 1)
                decays(p, 1)
                if prev:
                    root(p - 1)
                for n in range(1, 6):
                    if n in (3, 4) and more:
                        front(p + 1, 2 * n - 6)
                    for d in range(2):
                        act.wait_ge(S(f"P1_in{d}"), 5 * p + n + 1)
                        nc.scalar.copy(P1[d], c6(ps[3 * d][:, 0:T])).then_inc(S(f"P1_out{d}"), 1)
                    if n in (1, 4) and more == 2:
                        raw_in(p + 2, n // 4)
                    if n == 2:
                        if prev:
                            act.wait_ge(S("pair_done"), p)
                        act.wait_ge(S("g_in"), p + 1)
                        nc.scalar.copy(wls[:].rearrange("p h c -> p (h c)"), ps[7][0:Q, T:T + 4 * NCH])
                        nc.scalar.copy(g[:], ps[7][:, 0:T]).then_inc(S("g_out"), 1)
                    if n in (3, 4) and more:
                        front(p + 1, 2 * n - 5)
                    if n == 5 and more:
                        decays(p + 1, 0)
                for d in range(2):
                    act.wait_ge(S(f"PU_in{d}"), p + 1)
                    nc.scalar.mul(PU[d][:, 0:4].rearrange("p c q -> p (c q)"), ps[3 * d][:, :], -1.0)
                    nc.scalar.mul(PU[d][:, 4:6].rearrange("p c q -> p (c q)"), ps[3 * d + 1][:, 0:2 * P], -1.0).then_inc(S(f"PU_out{d}"), 1)
                if more == 2:
                    raw_in(p + 2, 2)
                act.wait_ge(S("fin_T"), p + 1)
                if prev:
                    act.wait_ge(S("fo_out"), 32 * p)
                nc.scalar.copy(fo[:].rearrange("p d k -> p (d k)"), ps[3][:, 0:2 * HD]).then_inc(S("fo_ready"), 1)

            norm_scalar(act)
            act.wait_ge(S("rwkv_fixed"), 1)
            for j in range(3):
                raw_in(0, j)
            for step in range(4):
                front(0, step)
                if step < 3:
                    raw_in(1, step)
            decays(0, 0)
            turns(act, body)
            square(PAIRS - 1)
            root(PAIRS - 1)

        @block.vector
        def _(dve):
            V = nc.vector

            def front(q, step):
                def col(at):
                    return par[:, bass.ds(q + at, 1)]

                if step < 3:
                    j, out = step, (r[:], k[:], v[:, Q:Q + T])[step]
                    link = Link(dve, S("shift_dve"), 6 * q + 2 * j)
                    dve.wait_ge(S("raw_in"), 3 * q + (j + 1))
                    link(V.tensor_tensor(sh[:], raw[:, j, 0:T + 1], raw[:, j, 2:T + 3], ALU.add))
                    link(V.tensor_scalar(sh[:], sh[:], mu[:, 1, bass.ds(q + 8 * j, 1)], None, ALU.mult))
                    for c0, c1, skip in ((0, LC, 0), (LC, T, 1)):
                        ins = V.scalar_tensor_tensor(out[:, c0:c1], raw[:, j, c0 + 1 + skip:c1 + 1 + skip], mu[:, 0, bass.ds(q + 8 * j, 1)],
                                                     sh[:, c0 + skip:c1 + skip], ALU.mult, ALU.add)
                    ins.then_inc(S("shifted"), 1)
                    dve.wait_ge(S("shifted"), 3 * q + j + 1)
                if step == 1:
                    V.tensor_scalar(kk[:], k[:], col(K_K), None, ALU.mult).then_inc(S("kk_raw"), 1)
                if step == 3:
                    link = Link(dve, S("key_dve"), 2 * q)
                    dve.wait_ge(S("sig_out"), 3 * q + 1)
                    link(V.tensor_scalar(ka[:], a[:], col(K_A), omk[:, bass.ds(q, 1)], ALU.mult, ALU.add))
                    link(V.tensor_tensor(k[:], k[:], ka[:], ALU.mult))
                if step == 4:
                    link = Link(dve, S("unit_dve"), 3 * q)
                    dve.wait_ge(S("kk_root"), q + 1)
                    link(V.tensor_scalar(t0[:], t0[:], 1e-12, None, ALU.max))
                    link(V.reciprocal(t0[:], t0[:]))
                    link(V.tensor_tensor(kk[:], kk[:], t0[:], ALU.mult))
                if step == 5:
                    V.scalar_tensor_tensor(rk[:], r[:], col(R_K), k[:], ALU.mult, ALU.mult).then_inc(S("rk"), 1)
                    V.tensor_tensor(ka[:], kk[:], a[:], ALU.mult).then_inc(S("ka"), 1)
                if step == 6:
                    dve.wait_ge(S("sig_out"), 3 * q + 2)
                    cumulate(q, 0)

            def cumulate(q, d):
                back = slice(None, None, -1) if d else slice(None)
                V.tensor_tensor_scan(ex[:, 1][:, back], reset[:], sg[:, d][:, back], 0.0, ALU.mult, ALU.add).then_inc(S("scanned"), 1)
                dve.wait_ge(S("scanned"), 2 * q + d + 1)
                V.tensor_tensor(ex[:, 2], ex[:, 1], sg[:, d], ALU.subtract).then_inc(S("cum_done"), 1)

            def hats(p, d):
                dve.wait_ge(S("ex_ready"), 2 * p + d + 1)
                if d == 0:
                    dve.wait_ge(S("ka"), p + 1)
                end = 0 if d else Q - 1
                V.tensor_copy(wl[:, d * NCH:(d + 1) * NCH].unsqueeze(2), c6(ex[:, 0])[:, :, end:end + 1]).then_inc(S("wl_ready"), 1)
                for out, x, y in ((M2[d][:, :, 2], kk, 2), (M1[d][:, :, 1], k, 1), (M1[d][:, :, 2], ka, 1), (M2[d][:, :, 0], r, 0)):
                    V.tensor_tensor(out, c6(x[:]), c6(ex[:, y]), ALU.mult).then_inc(S(f"hats{d}"), 1)
                dve.wait_ge(S(f"hats{d}"), 4 * p + 4)

            def y_read(q):
                dve.wait_ge(S("y_in_r"), q + 1)
                V.tensor_copy(yc[:], ps[2][:, 0:T]).then_inc(S("y_read"), 1)

            def centre(q):
                dve.wait_ge(S("y_read"), q + 1)
                dve.wait_ge(S("mean_in"), q + 1)
                V.scalar_tensor_tensor(yc[:], ps[4][:, 0:T], -1.0 / HD, yc[:], ALU.mult, ALU.add).then_inc(S("yc"), 1)

            def var_read(q):
                dve.wait_ge(S("var_in"), q + 1)
                V.tensor_scalar(rstd[:], ps[5][:, 0:T], 1.0 / HD, GN_EPS, ALU.mult, ALU.add).then_inc(S("var_read"), 1)

            def end(q):
                link = Link(dve, S("end_dve"), 4 * q)
                dve.wait_ge(S("var_root"), q + 1)
                link(V.reciprocal(rstd[:], rstd[:]))
                link(V.tensor_tensor(yc[:], yc[:], rstd[:], ALU.mult))
                link(V.tensor_scalar(yc[:], yc[:], par[:, bass.ds(q + LN_G, 1)], par[:, bass.ds(q + LN_B, 1)], ALU.mult, ALU.add))
                link(V.tensor_tensor(yc[:], yc[:], bonus[:], ALU.add))
                V.tensor_tensor(mixed[:, bass.ds(q + PAIRS, 1)].rearrange("p a t -> p (a t)"), yc[:], g[:], ALU.mult).then_inc(S("pair_done"), 1)

            FRONT = {(1, 0): (0,), (2, 0): (1,), (2, 1): (2,), (3, 1): (3,), (4, 0): (6,), (4, 1): (4,), (5, 0): (5,)}

            def add_part(p, i):
                n = out_chunk(p, i)
                if n is None:
                    return
                dve.wait_ge(S("w_used"), 6 * p + 13 + i)
                for ctx, c0, c1 in ((1, 0, LC), (0, LC, T)):
                    ins = V.scalar_tensor_tensor(xT[:, n, c0:c1], ps[6][:, c0:c1], modT[:, 2 * KC + n, ctx:ctx + 1], xT[:, n, c0:c1], ALU.mult, ALU.add)
                ins.then_inc(S("out_part"), 1)

            def body(p, prev, more):
                if prev:
                    y_read(p - 1)
                hats(p, 0)
                dve.wait_ge(S("sig_out"), 3 * p + 3)
                cumulate(p, 1)
                if prev:
                    centre(p - 1)
                hats(p, 1)
                if prev:
                    var_read(p - 1)
                link = Link(dve, S("X_dve"), 4 * p)
                i2 = C("i2").unsqueeze(1).to_broadcast([P, NCH, Q])

                def masked(n, d, dst, mask):
                    dve.wait_ge(S(f"E{n}_in{d}"), p + 1)
                    for b in range(3):
                        V.tensor_tensor(dst[:, 2 * b:2 * b + 2].rearrange("p c j q -> p c (j q)"), ps[3 * d + b][:, 0:384].rearrange("p (c q) -> p c q", c=2),
                                        C(mask).unsqueeze(1).to_broadcast([P, 2, 3 * Q]), ALU.mult).then_inc(S(f"W{n}_ready{d}"), 1)

                def identity_minus(out, Ab, mask):
                    link(V.tensor_tensor(out, Ab, C(mask).unsqueeze(1).to_broadcast([P, NCH, Q]), ALU.mult))
                    return V.tensor_tensor(out, i2, out, ALU.subtract)

                for d in range(2):
                    masked(1, d, W1[d], f"e1_{d}")
                for d in range(2):
                    dve.wait_ge(S(f"W1_ready{d}"), 3 * p + 3)
                    identity_minus(X[d], W1[d][:, :, 2], ("low0", "high0")[d])
                for d in range(2):
                    masked(2, d, W2[d], f"e2_{d}")
                    dve.wait_ge(S(f"W2_ready{d}"), 3 * p + 3)
                    identity_minus(XT[d], W2[d][:, :, 2], ("high0", "low0")[d]).then_inc(S(f"X_ready{d}"), 1)
                    if d == 0:
                        add_part(p, 0)
                for n in range(1, 6):
                    for d in range(2):
                        dve.wait_ge(S(f"D_in{d}"), 5 * p + n)
                        dve.wait_ge(S(f"X_ready{d}"), 5 * p + n)
                        ins = V.tensor_tensor(X[d], X[d], c6(ps[3 * d + 1][:, 0:T]), ALU.subtract)
                        if n < 5:
                            V.tensor_tensor(XT[d], XT[d], c6(ps[3 * d + 2][:, 0:T]), ALU.subtract).then_inc(S(f"X_ready{d}"), 1)
                        else:
                            ins.then_inc(S(f"X_final{d}"), 1)
                        if d == 1 and n != 3:
                            add_part(p, (1, 2, None, 3, 4)[n - 1])
                        if (n, d) == (1, 1):
                            if prev:
                                end(p - 1)
                                dve.wait_ge(S("pair_done"), p)
                            dve.wait_ge(S("bonus_sum"), p + 1)
                            V.tensor_tensor(bonus[:], ps[7][:, 0:T], v[:, Q:Q + T], ALU.mult).then_inc(S("bonus_ready"), 1)
                            dve.wait_ge(S("bonus_ready"), p + 1)
                        if more:
                            for step in FRONT.get((n, d), ()):
                                front(p + 1, step)
                for u in range(8):
                    for d in range(2):
                        h, c0, c1 = u // 4, (0, 4)[u // 2 % 2], (4, NCH)[u // 2 % 2]
                        dve.wait_ge(S(f"XX_in{d}"), 8 * p + u + 1)
                        src = ps[3 * d + (2 + u) % 3][:, 0:(c1 - c0) * P].rearrange("p (c q) -> p c q", q=P)
                        dst = XX[d][:, h, c0:c1]
                        if u % 2 == 0:
                            V.tensor_tensor(dst, src, C(f"x_{d}").unsqueeze(1).to_broadcast([P, c1 - c0, P]), ALU.mult).then_inc(S(f"XX_ready{d}"), 1)
                        else:
                            dve.wait_ge(S(f"XX_ready{d}"), 8 * p + u + 1)
                            V.tensor_tensor(dst, dst, src, ALU.add).then_inc(S(f"XX_ready{d}"), 1)
                dve.wait_ge(S("g_out"), p + 1)
                for n, (rnd, item, d, c, nxt) in enumerate(rounds()):
                    dve.wait_ge(S("state_in"), 10 * p + (4, 8, 10)[rnd])
                    src = ps[rnd % 2][0:Q, item * P:(item + 1) * P].rearrange("p (h v) -> p h v", h=2)
                    dst = (fin[:, d] if nxt is None else VS[d][0:Q, nxt].rearrange("p h v -> p (h v)")).rearrange("p (h v) -> p h v", h=2)
                    V.tensor_tensor(dst, src, wls[:, :, d * NCH + c:d * NCH + c + 1].to_broadcast([Q, 2, HD]), ALU.mult).then_inc(S("state_out"), 1)
                add_part(p, 5)

            norm_vector(dve)
            link = Link(dve, S("rwkv_dve"))
            link(V.tensor_scalar(mu[:, 0], par[:, MU:MU + 24], -1.0, 1.0, ALU.mult, ALU.add))
            link(V.tensor_scalar(mu[:, 1], par[:, MU:MU + 24], 0.5, None, ALU.mult))
            link(V.tensor_scalar(omk[:], par[:, K_A:K_A + PAIRS], -1.0, 1.0, ALU.mult, ALU.add))
            for step in (0, 1, 2, 3, 6, 4, 5):
                front(0, step)
            turns(dve, body)
            y_read(PAIRS - 1)
            centre(PAIRS - 1)
            var_read(PAIRS - 1)
            end(PAIRS - 1)


def project_out(nc, I, O, table, S, sb, ps, cst, par, modT, gain, xT, C, mixed):
    RING = 4
    LAST = KC // RING - 1
    w_out = I["w_out"].rearrange("l (k p) n -> p (l k) n", p=P)
    with ExitStack() as st:
        w = sb(st, "w_out_ring", [P, RING, KC, P])
        loaded = [S(f"out_loaded{n}") for n in range(RING)]
        block = st.enter_context(nc.Block())

        @block.gpsimd
        def _(pool):
            ahead(pool, S, "out_added")

        @block.sync
        def _(sp):
            def load(i, n, k0):
                sp.dma_start(w[:, n, k0:KC], w_out[:, k0:KC, bass.ds(i * (RING * P) + n * P, P)]).then_inc(loaded[n], 16)

            for n in range(RING):
                load(0, n, KC // 2)
            with sp.Fori(1, LAST) as i:
                for n in range(RING):
                    sp.wait_ge(S("out_in"), i * RING + (n - RING + 1))
                    load(i, n, KC // 2)
            for n in range(RING):
                sp.wait_ge(S("out_in"), LAST * RING + (n - RING + 1))
                load(LAST, n, 0)

        @block.tensor
        def _(pe):
            def body(i, k0):
                for n in range(RING):
                    pe.wait_ge(loaded[n], (i + 1) * 16)
                    pe.wait_ge(S("out_added"), i * RING + 1)
                    for k in range(k0, KC):
                        mm = pe.matmul(ps[n][:, 0:T], w[:, n, k], mixed[:, k], start=(k == k0), stop=(k == KC - 1))
                    mm.then_inc(S("out_in"), 1)

            with pe.Fori(0, LAST) as i:
                body(i, KC // 2)
            body(LAST, 0)

        @block.vector
        def _(dve):
            with dve.Fori(0, KC // RING) as i:
                for n in range(RING):
                    dve.wait_ge(S("out_in"), i * RING + (n + 1))
                    for a, c0, c1 in ((1, 0, LC), (0, LC, T)):
                        x = xT[:, bass.ds(i * RING + n, 1), c0:c1].rearrange("p a t -> p (a t)")
                        gate = modT[:, bass.ds(i * RING + (2 * KC + n), 1), a]
                        ins = nc.vector.scalar_tensor_tensor(x, ps[n][:, c0:c1], gate, x, ALU.mult, ALU.add)
                    ins.then_inc(S("out_added"), 1)


HALVES = ((0, CAPC, 1, 0), (CAPC, SLOTS, 0, 1), (SLOTS, SLOTS + CAPC, 1, 0), (SLOTS + CAPC, 2 * SLOTS, 0, 1))


def route(nc, I, O, table, S, sb, ps, cst, par, modT, gain, xT, C, picked, rank, aff, gates):
    with ExitStack() as st:
        h2 = sb(st, "h2", [P, KC, T])
        norm_scalar, norm_tensor, norm_vector = norm(nc, st, S, sb, ps, modT, gain, xT, C, 1, h2)
        rw = sb(st, "rw", [P, KC, N_EXP])
        hhi = sb(st, "hhi", [P, TILES, D], F32R)
        hlo = sb(st, "hlo", [P, TILES, D], F32R)
        ohc = sb(st, "ohc", [P, N_EXP, CAPC], F32R)
        ohs = sb(st, "ohs", [P, 2, N_EXP, CAPS], F32R)
        lg = sb(st, "lg", [N_EXP, T])
        work = sb(st, "work", [N_EXP, 3, T])
        top8 = sb(st, "top8", [N_EXP, 8])
        mx = sb(st, "mx", [P, TILES])
        gcol = sb(st, "gcol", [P, KC, 2 * SLOTS])
        block = st.enter_context(nc.Block())

        @block.sync
        def _(sp):
            sp.dma_start(rw[:], I["router_w"].rearrange("l (k p) n -> p (l k) n", p=P)).then_inc(S("rw_loaded"), 16)

        @block.tensor
        def _(pe):
            norm_tensor(pe)
            pe.wait_ge(S("rw_loaded"), 16)
            for k in range(KC):
                pe.wait_ge(S("norm1_out"), k + 1)
                mm = pe.matmul(ps[0][0:N_EXP, 0:T], rw[:, k], h2[:, k], start=(k == 0), stop=(k == KC - 1))
            mm.then_inc(S("logits_in"), 1)
            pe.wait_ge(S("logits"), 1)
            for t in range(TILES):
                mm = pe.transpose(ps[1][:, t * N_EXP:(t + 1) * N_EXP], lg[:, t * P:(t + 1) * P], C("ident", 0, N_EXP)[:, 0:N_EXP])
            mm.then_inc(S("logits_T"), 1)
            for g in range(12):
                t, q = g // 4, g % 4
                if g >= 2:
                    pe.wait_ge(S("h_lo"), g - 1)
                for k in range(4):
                    mm = pe.transpose(ps[4 + g % 2][:, k * P:(k + 1) * P], h2[:, 4 * q + k, t * P:(t + 1) * P], C("ident"))
                mm.then_inc(S("h_T"), 1)
            pe.wait_ge(S("aff"), 1)
            for t in range(TILES):
                mm = pe.transpose(ps[2][0:N_EXP, t * P:(t + 1) * P], aff[:, t], C("ident"))
            mm.then_inc(S("aff_T"), 1)
            pe.wait_ge(S("gcol"), 1)
            pe.wait_ge(S("h_lo"), 12)
            for q in range(4):
                if q >= 2:
                    pe.wait_ge(S("gates"), q - 1)
                for k in range(4):
                    mm = pe.matmul(ps[4 + q % 2][0:2 * SLOTS, k * P:(k + 1) * P], gcol[:, 4 * q + k], C("ident"), start=True, stop=True)
                mm.then_inc(S("gates_in"), 1)
            pe.wait_ge(S("rank_row"), 1)
            for t in range(TILES):
                mm = pe.transpose(ps[3][:, t * N_EXP:(t + 1) * N_EXP], work[:, 2, t * P:(t + 1) * P], C("ident", 0, N_EXP)[:, 0:N_EXP])
            mm.then_inc(S("rank_T"), 1)
            pe.wait_ge(S("onehot"), 1)
            for k in range(KC):
                if k >= 1:
                    pe.wait_ge(S("picked_c"), k)
                for half in (hhi, hlo):
                    mm = pe.matmul(ps[6][:, 0:N_EXP * CAPC], half[:, 0, k * P:(k + 1) * P], ohc[:].rearrange("p e c -> p (e c)"), start=(half is hhi), stop=(half is hlo))
                mm.then_inc(S("pick_c"), 1)
                if k >= 1:
                    pe.wait_ge(S("picked_s"), k)
                for t in range(2):
                    for half in (hhi, hlo):
                        mm = pe.matmul(ps[7][:], half[:, 1 + t, k * P:(k + 1) * P], ohs[:, t].rearrange("p e c -> p (e c)"),
                                       start=(t == 0 and half is hhi), stop=(t == 1 and half is hlo))
                mm.then_inc(S("pick_s"), 1)

        @block.scalar
        def _(act):
            norm_scalar(act)
            act.wait_ge(S("logits_in"), 1)
            nc.scalar.copy(lg[:], ps[0][0:N_EXP, 0:T]).then_inc(S("logits"), 1)
            act.wait_ge(S("shift_max"), 1)
            nc.scalar.activation(aff[:], aff[:], ACT.Exp).then_inc(S("aff_exp"), 1)
            for g in range(12):
                t, q = g // 4, g % 4
                act.wait_ge(S("h_T"), g + 1)
                nc.scalar.copy(hhi[:, t, q * 512:(q + 1) * 512], ps[4 + g % 2][:]).then_inc(S("h_hi"), 1)
            for q in range(4):
                act.wait_ge(S("gates_in"), q + 1)
                nc.scalar.copy(gates[:, q * 512:(q + 1) * 512], ps[4 + q % 2][0:2 * SLOTS, :]).then_inc(S("gates"), 1)
            for k in range(KC):
                act.wait_ge(S("pick_c"), k + 1)
                nc.scalar.copy(picked[:, k].rearrange("p (e s) -> p e s", s=SLOTS)[:, :, 0:CAPC],
                               ps[6][:, 0:N_EXP * CAPC].rearrange("p (e c) -> p e c", e=N_EXP)).then_inc(S("picked_c"), 1)

        @block.vector
        def _(dve):
            V = nc.vector
            norm_vector(dve)
            link = Link(dve, S("route_dve"))
            dve.wait_ge(S("logits_T"), 1)
            lt = ps[1][:, 0:TILES * N_EXP].rearrange("p (t e) -> p t e", t=TILES)
            link(V.tensor_reduce(mx[:], lt, AX.X, ALU.max))
            V.tensor_tensor(aff[:], lt, mx[:].unsqueeze(2).to_broadcast([P, TILES, N_EXP]), ALU.subtract).then_inc(S("shift_max"), 1)
            dve.wait_ge(S("aff_exp"), 1)
            link(V.tensor_reduce(mx[:], aff[:], AX.X, ALU.add))
            link(V.reciprocal(mx[:], mx[:]))
            V.tensor_tensor(aff[:], aff[:], mx[:].unsqueeze(2).to_broadcast([P, TILES, N_EXP]), ALU.mult).then_inc(S("aff"), 1)
            for c0, c1, a, _ in HALVES:
                ins = V.tensor_copy(gcol[:, :, c0:c1], modT[:, 5 * KC:6 * KC, a:a + 1].to_broadcast([P, KC, c1 - c0]))
            ins.then_inc(S("gcol"), 1)
            for g in range(12):
                t, q = g // 4, g % 4
                dve.wait_ge(S("h_hi"), g + 1)
                V.tensor_tensor(hlo[:, t, q * 512:(q + 1) * 512], ps[4 + g % 2][:], hhi[:, t, q * 512:(q + 1) * 512].bitcast(F32), ALU.subtract).then_inc(S("h_lo"), 1)
            dve.wait_ge(S("aff_T"), 1)
            link(V.tensor_copy(work[:, 0], ps[2][0:N_EXP, 0:T]))
            for c0, c1, cap in ((0, LC, CAPC), (LC, T, CAPS)):
                for _ in range(cap // 8):
                    link(V.max(top8[:], work[:, 0, c0:c1]))
                    link(V.match_replace(work[:, 0, c0:c1], top8[:], work[:, 0, c0:c1], -1.0))
            link(V.tensor_scalar(work[:, 1], work[:, 0], 0.0, None, ALU.is_lt))
            link(V.memset(work[:, 0], 1.0))
            for c0, c1 in ((0, LC), (LC, T)):
                link(V.tensor_tensor_scan(work[:, 2, c0:c1], work[:, 0, c0:c1], work[:, 1, c0:c1], 0.0, ALU.mult, ALU.add))
            link(V.tensor_tensor(work[:, 2], work[:, 2], work[:, 1], ALU.mult))
            V.tensor_scalar(work[:, 2], work[:, 2], -1.0, None, ALU.add).then_inc(S("rank_row"), 1)
            dve.wait_ge(S("rank_T"), 1)
            link(V.tensor_copy(rank[:].rearrange("p t e -> p (t e)"), ps[3][:, 0:TILES * N_EXP]))
            V.tensor_tensor(ohc[:], rank[:, 0].unsqueeze(2).to_broadcast([P, N_EXP, CAPC]), C("iota")[:, 0:CAPC].unsqueeze(1).to_broadcast([P, N_EXP, CAPC]), ALU.is_equal)
            for t in range(2):
                ins = V.tensor_tensor(ohs[:, t], rank[:, 1 + t].unsqueeze(2).to_broadcast([P, N_EXP, CAPS]), C("iota").unsqueeze(1).to_broadcast([P, N_EXP, CAPS]), ALU.is_equal)
            ins.then_inc(S("onehot"), 1)
            for k in range(KC):
                dve.wait_ge(S("pick_s"), k + 1)
                V.tensor_copy(picked[:, k].rearrange("p (e s) -> p e s", s=SLOTS)[:, :, CAPC:SLOTS],
                              ps[7][:].rearrange("p (e c) -> p e c", e=N_EXP)).then_inc(S("picked_s"), 1)


def experts(nc, I, O, table, S, sb, ps, cst, par, modT, gain, xT, C, picked, rank, aff, gates):
    RING, HL, NS, R2 = 4, 3, 24, 2 * SLOTS
    DOWN = 16
    w_src = [I[n].rearrange("l e (q c p) n -> p (l e q) c n", p=P, c=4) for n in ("exp_w_gate", "exp_w_up", "exp_w_down")]
    with ExitStack() as st:
        raw = sb(st, "w_raw", [P, RING, 4, 512])
        hi = sb(st, "w_hi", [P, HL, 4, 512], F32R)
        lo = sb(st, "w_lo", [P, HL, 4, 512], F32R)
        xs = sb(st, "xs", [P, KC, R2], F32R)
        gu = sb(st, "gu", [R2, 4, 512])
        gs = sb(st, "gs", [P, 4, 4, SLOTS])
        sg = sb(st, "sg_e", [P, 2, 4, SLOTS])
        hid = sb(st, "hid", [P, FF // P, R2], F32R)
        outs = sb(st, "outs", [R2, D])
        pg = sb(st, "pg", [P, TILES, R2])
        G = sb(st, "G", [R2, T])
        loaded = [S(f"exp_loaded{n}") for n in range(RING)]
        block = st.enter_context(nc.Block())

        def turns(eng, body):
            body(0)
            body(1)
            with eng.Fori(2, N_EXP - 1) as i:
                body(i)
            body(N_EXP - 1)
            body(N_EXP)

        def parts(i):
            if not isinstance(i, int):
                return True, True, True, range(NS)
            up, down = i < N_EXP, i >= 1
            return up, down, i >= 2, range(0 if up else DOWN, NS if down else DOWN)

        def before(i, n):
            if isinstance(i, int) and i == 0:
                return 0, n
            if isinstance(i, int) and i == N_EXP:
                return i - 1, n
            return i - 1, DOWN + n

        def count(i, n):
            t, r = before(i, n)
            return t * NS + r

        @block.sync
        def _(sp):
            def body(i):
                for n in parts(i)[3]:
                    t, r = before(i, n)
                    j, e, per, q, c0 = (n // 8, i, 4, n % 4, n % 8 // 4 * 512) if n < DOWN else (2, i - 1, 2, n % 2, (n - DOWN) // 2 * 512)
                    if not (isinstance(i, int) and i == 0 and n < RING):
                        sp.wait_ge(S("exp_lo"), t * NS + (r - RING + 1))
                        sp.sem_inc(S("sp_held"), 1)
                    src = w_src[j][:, bass.ds(e * per + q, 1), :, c0:c0 + 512].rearrange("p a c n -> p (a c) n")
                    sp.dma_start(raw[:, r % RING], src).then_inc(loaded[r % RING], 16)

            turns(sp, body)

        @block.tensor
        def _(pe):
            def slot(i, n):
                t, r = before(i, n)
                pe.wait_ge(S("exp_lo"), t * NS + (r + 1))
                bank, first, last = (n // 4, n % 4 == 0, n % 4 == 3) if n < DOWN else (4 + (n - DOWN) // 2 % 2, n % 2 == 0, n % 2 == 1)
                for c in range(4):
                    lhs = xs[:, 4 * (n % 4) + c] if n < DOWN else hid[:, 4 * (n % 2) + c]
                    for half in (hi, lo):
                        mm = pe.matmul(ps[bank][0:R2, :], lhs, half[:, r % HL, c], start=(first and c == 0 and half is hi), stop=(last and c == 3 and half is lo))
                mm.then_inc(S("exp_used"), 1)

            def turn_back(i, j):
                pe.wait_ge(S("gu_out"), i * 4 + (j + 1))
                for f in range(4):
                    mm = pe.transpose(ps[j][:, f * R2:(f + 1) * R2], gu[:, j, f * P:(f + 1) * P], C("ident", 0, R2)[:, 0:R2])
                mm.then_inc(S("gu_T"), 1)

            def add_out(i, k):
                pe.wait_ge(S("outs"), i * 4 + (k // 4 - 7))
                if k == 0:
                    pe.wait_ge(S("G"), i - 1)
                if k >= 2:
                    pe.wait_ge(S("added"), i * KC + (k - 1 - 2 * KC))
                pe.matmul(ps[6 + k % 2][:, 0:T], outs[:, k * P:(k + 1) * P], G[:], start=True, stop=True).then_inc(S("add_in"), 1)

            def body(i):
                up, down, add, _ = parts(i)
                if up:
                    pe.wait_ge(S("xs_lo"), i + 1)
                for n in range(DOWN):
                    if up:
                        if n % 4 == 0 and not (isinstance(i, int) and i == 0):
                            pe.wait_ge(S("gs"), i * 4 + (n // 4 - 3))
                        slot(i, n)
                        if n in (6, 10, 14):
                            turn_back(i, (n - 6) // 4)
                        if n == DOWN - 1 and not down:
                            turn_back(i, 3)
                    if add:
                        add_out(i, n)
                for n in range(DOWN, NS):
                    if down:
                        if n == DOWN:
                            pe.wait_ge(S("hid"), i)
                        if n % 2 == 0 and not (isinstance(i, int) and i == 1 and n < DOWN + 4):
                            pe.wait_ge(S("outs"), i * 4 + ((n - DOWN) // 2 - 5))
                        slot(i, n)
                    if n == 18 and up and down:
                        turn_back(i, 3)
                    if n == 20 and down:
                        pe.wait_ge(S("pg"), i)
                        if add:
                            pe.wait_ge(S("added"), i * KC - KC)
                        for t in range(TILES):
                            mm = pe.transpose(ps[6][0:R2, t * P:(t + 1) * P], pg[:, t], C("ident"))
                        mm.then_inc(S("pg_T"), 1)

            turns(pe, body)
            for k in range(KC):
                add_out(N_EXP + 1, k)

        @block.scalar
        def _(act):
            def xs_hi(e):
                nc.scalar.copy(xs[:, :, 0:SLOTS], picked[:, :, bass.ds(e * SLOTS, SLOTS)]).then_inc(S("xs_hi"), 1)

            def gu_out(i, j):
                act.wait_ge(S("exp_used"), count(i, 4 * j + 3) + 1)
                nc.scalar.copy(gu[:, j], ps[j][0:R2, :]).then_inc(S("gu_out"), 1)

            def gate(i):
                act.wait_ge(S("gs"), i * 4)
                nc.scalar.activation(sg[:], gs[:, 0:2], ACT.Sigmoid).then_inc(S("hid_sig"), 1)

            def body(i):
                up, down, add, slots = parts(i)
                more = up and not (isinstance(i, int) and i == N_EXP - 1)
                if not up:
                    gate(i)
                for n in slots:
                    t, r = before(i, n)
                    act.wait_ge(loaded[r % RING], (t * (NS // RING) + (r // RING + 1)) * 16)
                    if not (isinstance(i, int) and i == 0 and n < HL):
                        act.wait_ge(S("exp_used"), t * NS + (r - HL + 1))
                    nc.scalar.copy(hi[:, r % HL], raw[:, r % RING]).then_inc(S("exp_hi"), 1)
                    if n == 2 and down:
                        gate(i)
                    if n in (5, 9, 13) or (up and n == 17):
                        gu_out(i, (n - 5) // 4)
                    if n == 18 and more:
                        act.wait_ge(S("exp_used"), count(i, DOWN - 1) + 1)
                        xs_hi(i + 1)
                    if n == 22:
                        act.wait_ge(S("pg_T"), i)
                        nc.scalar.copy(G[:], ps[6][0:R2, 0:T]).then_inc(S("G"), 1)
                if not down:
                    gu_out(i, 3)
                    xs_hi(i + 1)

            xs_hi(0)
            turns(act, body)

        @block.vector
        def _(dve):
            V = nc.vector

            def added(i, k):
                dve.wait_ge(S("add_in"), i * KC + (k + 1 - 2 * KC))
                V.tensor_tensor(xT[:, k], xT[:, k], ps[6 + k % 2][:, 0:T], ALU.add).then_inc(S("added"), 1)

            def out(i, j):
                dve.wait_ge(S("exp_used"), count(i, DOWN + 2 * j + 1) + 1)
                V.tensor_tensor(outs[:, j * 512:(j + 1) * 512], ps[4 + j % 2][0:R2, :], gates[:, j * 512:(j + 1) * 512], ALU.mult).then_inc(S("outs"), 1)

            def halves(i, j):
                dve.wait_ge(S("gu_T"), i * 4 + (j + 1))
                src = ps[j][:, 0:4 * R2].rearrange("p (f r) -> p f r", f=4)
                V.tensor_copy(gs[:, j], src[:, :, 0:SLOTS]).then_inc(S("gs_half"), 1)
                dve.wait_ge(S("gs_half"), i * 4 + (j + 1))
                V.tensor_tensor(gs[:, j], gs[:, j], src[:, :, SLOTS:R2], ALU.add).then_inc(S("gs"), 1)

            def xs_lo(e):
                dve.wait_ge(S("xs_hi"), e + 1)
                V.tensor_tensor(xs[:, :, SLOTS:R2], picked[:, :, bass.ds(e * SLOTS, SLOTS)], xs[:, :, 0:SLOTS].bitcast(F32), ALU.subtract).then_inc(S("xs_lo"), 1)

            def hidden(i):
                link = Link(dve, S("exp_dve"), (i - 1) * 3)
                dve.wait_ge(S("hid_sig"), i)
                if not (isinstance(i, int) and i == 1):
                    dve.wait_ge(S("exp_used"), count(i - 1, NS - 1) + 1)
                link(V.tensor_tensor(sg[:], sg[:], gs[:, 0:2], ALU.mult))
                link(V.tensor_tensor(sg[:], sg[:], gs[:, 2:4], ALU.mult))
                s8 = sg[:].rearrange("p j f s -> p (j f) s")
                link(V.tensor_copy(hid[:, :, 0:SLOTS], s8))
                V.tensor_tensor(hid[:, :, SLOTS:R2], s8, hid[:, :, 0:SLOTS].bitcast(F32), ALU.subtract).then_inc(S("hid"), 1)

            def weights(i):
                if not (isinstance(i, int) and i == 1):
                    dve.wait_ge(S("pg_T"), i - 1)
                for c0, c1, a, late in HALVES:
                    for t in ((1, 2) if late else (0,)):
                        ins = V.tensor_scalar(pg[:, t, c0:c1], C("iota")[:, 0:c1 - c0], rank[:, t, bass.ds(i - 1, 1)], aff[:, t, bass.ds(i - 1, 1)], ALU.is_equal, ALU.mult)
                ins.then_inc(S("pg"), 1)

            def body(i):
                up, down, add, slots = parts(i)
                for n in range(NS):
                    if n in slots:
                        t, r = before(i, n)
                        dve.wait_ge(S("exp_hi"), t * NS + (r + 1))
                        V.tensor_tensor(lo[:, r % HL], raw[:, r % RING], hi[:, r % HL].bitcast(F32), ALU.subtract).then_inc(S("exp_lo"), 1)
                    if n == 1 and add:
                        out(i - 1, 3)
                    if n == 3 and down:
                        hidden(i)
                    if 2 <= n < KC + 2 and add:
                        added(i, n - 2)
                    if n == 5 and down:
                        weights(i)
                    if up and (n in (8, 12) or (down and n in (16, 20))):
                        halves(i, (n - 8) // 4)
                    if n == 19 and up and down and not (isinstance(i, int) and i == N_EXP - 1):
                        xs_lo(i + 1)
                    if down and n in (19, 21, 23):
                        out(i, (n - 19) // 2)
                if not down:
                    halves(i, 2)
                    halves(i, 3)
                    xs_lo(i + 1)

            V.memset(pg[:], 0.0).then_inc(S("pg_zero"), 1)
            dve.wait_ge(S("pg_zero"), 1)
            xs_lo(0)
            turns(dve, body)
            out(N_EXP, 3)
            for k in range(KC):
                added(N_EXP + 1, k)


def finish(nc, I, O, table, S, sb, ps, cst, par, modT, gain, xT, C):
    with ExitStack() as st:
        sq = sb(st, "f_sq", [P, 2, T])
        rstd = sb(st, "f_rstd", [P, T])
        ytok = sb(st, "ytok", [P, TILES, D])
        block = st.enter_context(nc.Block())

        @block.scalar
        def _(act):
            for k in range(KC):
                if k >= 2:
                    act.wait_ge(S("f_sum"), k - 1)
                nc.scalar.activation(sq[:, k % 2], xT[:, k], ACT.Square).then_inc(S("f_sq"), 1)
            act.wait_ge(S("f_mean"), 1)
            nc.scalar.sqrt(rstd[:], rstd[:]).then_inc(S("f_root"), 1)
            for g in range(1, 12, 2):
                act.wait_ge(S("f_T"), g + 1)
                nc.scalar.copy(ytok[:, g % 3, (g // 3) * 512:(g // 3 + 1) * 512], ps[1 + g % 4][:]).then_inc(S("f_out1"), 1)

        @block.tensor
        def _(pe):
            for k in range(KC):
                pe.wait_ge(S("f_sq"), k + 1)
                pe.matmul(ps[0][:, 0:T], C("ones"), sq[:, k % 2], start=(k == 0), stop=(k == KC - 1)).then_inc(S("f_sum"), 1)
            for g in range(12):
                t, q = g % 3, g // 3
                pe.wait_ge(S("f_y"), 4 * q + 4)
                if g >= 4:
                    pe.wait_ge(S(f"f_out{g % 2}"), (g - 4) // 2 + 1)
                for k in range(4):
                    mm = pe.transpose(ps[1 + g % 4][:, k * P:(k + 1) * P], xT[:, 4 * q + k, t * P:(t + 1) * P], C("ident"))
                mm.then_inc(S("f_T"), 1)

        @block.vector
        def _(dve):
            dve.wait_ge(S("f_sum"), KC)
            nc.vector.tensor_scalar(rstd[:], ps[0][:, 0:T], 1.0 / D, EPS, ALU.mult, ALU.add).then_inc(S("f_mean"), 1)
            dve.wait_ge(S("f_root"), 1)
            nc.vector.reciprocal(rstd[:], rstd[:]).then_inc(S("f_rstd"), 1)
            dve.wait_ge(S("f_rstd"), 1)
            for k in range(KC):
                nc.vector.scalar_tensor_tensor(xT[:, k], xT[:, k], par[:, G_FIN + k:G_FIN + k + 1], rstd[:], ALU.mult, ALU.mult).then_inc(S("f_y"), 1)
            for g in range(0, 12, 2):
                dve.wait_ge(S("f_T"), g + 1)
                nc.vector.tensor_copy(ytok[:, g % 3, (g // 3) * 512:(g // 3 + 1) * 512], ps[1 + g % 4][:]).then_inc(S("f_out0"), 1)

        @block.sync
        def _(sp):
            for q in range(4):
                n = 3 * q + 3
                sp.wait_ge(S("f_out0"), (n + 1) // 2)
                sp.wait_ge(S("f_out1"), n // 2)
                for t in range(TILES):
                    dst = O["y_prompt"][0] if t == 0 else O["y_sample"][0, (t - 1) * P:t * P, :]
                    sp.dma_start(dst[:, q * 512:(q + 1) * 512], ytok[:, t, q * 512:(q + 1) * 512]).then_inc(S("y_stored"), 16)
            sp.wait_ge(S("y_stored"), 16 * 12)


INS = ["x_prompt", "x_sample", "state_ssd_fwd", "state_ssd_bwd", "state_rwkv_fwd", "state_rwkv_bwd", "c", "c_ctx",
       "w_ada", "b_ada", "norm_mix_g", "norm_ffn_g", "w_in", "w_out", "ssd_conv_w", "ssd_conv_b", "ssd_A_log",
       "ssd_dt_bias", "ssd_D", "ssd_norm_g", "rwkv_mu", "rwkv_w0", "rwkv_w_up", "rwkv_a0", "rwkv_a_up", "rwkv_g_up",
       "rwkv_k_k", "rwkv_k_a", "rwkv_r_k", "rwkv_ln_g", "rwkv_ln_b", "router_w", "exp_w_gate", "exp_w_up",
       "exp_w_down", "final_norm_g"]
OUTS = [("y_prompt", (1, LC, D)), ("y_sample", (1, LS, D)),
        ("ssd_fwd", (1, 1, HEADS, HD, P)), ("ssd_bwd", (1, 1, HEADS, HD, P)),
        ("rwkv_fwd", (1, 1, HEADS, HD, HD)), ("rwkv_bwd", (1, 1, HEADS, HD, HD))]


def kernel(**inputs):
    import concourse.bacc as bacc
    from concourse.bass_utils import run_bass_kernel_spmd

    nc = bacc.Bacc("TRN2", target_bir_lowering=False, num_devices=1)
    table = constants()
    arrays = {"table": table}
    I, O = {}, {}
    for name in INS:
        arrays[name] = np.ascontiguousarray(inputs[name])
        I[name] = nc.dram_tensor(name, arrays[name].shape, F32, kind="ExternalInput").ap()
    for name, shape in OUTS:
        O[name] = nc.dram_tensor("out_" + name, shape, F32, kind="ExternalOutput").ap()
    table_ap = nc.dram_tensor("table", table.shape, F32, kind="ExternalInput").ap()
    program(nc, I, O, table_ap)
    got = run_bass_kernel_spmd(nc, [arrays], core_ids=[0]).results[0]
    return tuple(got["out_" + name] for name, _ in OUTS)
```
